# Optimizing a Trainium2 kernel written in Bass

```python
import jax, jax.numpy as jnp
from jax import lax
import numpy as np

D_MODEL = 1024
BATCH = 1
SEQ = 256
DEPTH = 1

CHUNK = 64
NORM_EPS = 1e-6
SSM_D_INNER = 2 * D_MODEL
SSM_HEAD_DIM = 64
SSM_HEADS = SSM_D_INNER // SSM_HEAD_DIM
SSM_GROUPS = 4
SSM_STATE = 128
SSM_CONV = 4
SSM_XBC = SSM_D_INNER + 2 * SSM_GROUPS * SSM_STATE
ATT_HEADS = 16
ATT_HEAD_DIM = 64
ATT_WIDTH = ATT_HEADS * ATT_HEAD_DIM
KV_LATENT = 256
IDX_HEADS = 8
IDX_HEAD_DIM = 64
TOPK_MAX = 256
Q_BLOCK = 128
MOE_GROUPS = 4
MOE_EXPERTS = 8
MOE_TOPK = 2
MOE_FF = 256
N_BRANCHES = 2
IN_SIZES = (SSM_D_INNER, SSM_XBC, SSM_HEADS, ATT_WIDTH, KV_LATENT,
            IDX_HEADS * IDX_HEAD_DIM, IDX_HEAD_DIM, IDX_HEADS, N_BRANCHES * D_MODEL)
IN_TOTAL = 9064

kernel_name = "hybrid_ssd_dsa_hmoe_block"

def rms_norm(x, g):
    xf = x.astype(jnp.float32)
    y = xf * lax.rsqrt(jnp.mean(xf * xf, axis=-1, keepdims=True) + NORM_EPS)
    return (y * g.astype(jnp.float32)).astype(x.dtype)

def split_cols(u, sizes):
    cuts = [int(c) for c in np.cumsum(sizes)[:-1]]
    return jnp.split(u, cuts, axis=-1)

def causal_depthwise_conv(u, w, b):
    out = lax.conv_general_dilated(
        u, w[:, None, :].astype(u.dtype), window_strides=(1,),
        padding=[(SSM_CONV - 1, 0)], dimension_numbers=('NWC', 'WIO', 'NWC'),
        feature_group_count=u.shape[-1])
    return out + b.astype(u.dtype)

def ssd_chunked(xh, dt, a, bm, cm):
    b, s, h, p = xh.shape
    g, n = bm.shape[2], bm.shape[3]
    nc, hg = s // CHUNK, h // g
    x_c = xh.reshape(b, nc, CHUNK, g, hg, p)
    dt_c = dt.reshape(b, nc, CHUNK, g, hg)
    b_c = bm.reshape(b, nc, CHUNK, g, n)
    c_c = cm.reshape(b, nc, CHUNK, g, n)
    a_cs = jnp.cumsum(dt_c * a.reshape(g, hg), axis=2)
    seg = a_cs[:, :, :, None] - a_cs[:, :, None, :]
    causal = jnp.tril(jnp.ones((CHUNK, CHUNK), dtype=bool))[:, :, None, None]
    decay = jnp.exp(jnp.where(causal, seg, -jnp.inf))
    cb = jnp.einsum('bclgn,bcsgn->bclsg', c_c, b_c)
    wts = cb[..., None] * decay * dt_c[:, :, None]
    y_diag = jnp.einsum('bclsgh,bcsghp->bclghp', wts, x_c)
    decay_st = jnp.exp(a_cs[:, :, -1:] - a_cs) * dt_c
    states = jnp.einsum('bclgn,bclghp->bcghpn', b_c, decay_st[..., None] * x_c)
    chunk_decay = jnp.exp(a_cs[:, :, -1])

    def step(carry, inp):
        st, dec = inp
        return carry * dec[..., None, None] + st, carry

    init = jnp.zeros((b, g, hg, p, n), jnp.float32)
    _, prev = lax.scan(step, init, (jnp.moveaxis(states, 1, 0), jnp.moveaxis(chunk_decay, 1, 0)))
    prev = jnp.moveaxis(prev, 0, 1)
    y_off = jnp.einsum('bclgn,bcghpn->bclghp', c_c, prev) * jnp.exp(a_cs)[..., None]
    return (y_diag + y_off).reshape(b, s, h, p)

def mamba2_branch(z, xbc, dt_raw, conv_w, conv_b, dt_bias, a_log, d_skip, norm_g):
    b, s, _ = z.shape
    xbc = jax.nn.silu(causal_depthwise_conv(xbc, conv_w, conv_b))
    xs, bm, cm = split_cols(xbc, (SSM_D_INNER, SSM_GROUPS * SSM_STATE, SSM_GROUPS * SSM_STATE))
    xh = xs.reshape(b, s, SSM_HEADS, SSM_HEAD_DIM).astype(jnp.float32)
    bm = bm.reshape(b, s, SSM_GROUPS, SSM_STATE).astype(jnp.float32)
    cm = cm.reshape(b, s, SSM_GROUPS, SSM_STATE).astype(jnp.float32)
    dt = jax.nn.softplus(dt_raw.astype(jnp.float32) + dt_bias.astype(jnp.float32))
    a = -jnp.exp(a_log.astype(jnp.float32))
    y = ssd_chunked(xh, dt, a, bm, cm) + d_skip.astype(jnp.float32)[:, None] * xh
    y = y.reshape(b, s, SSM_D_INNER) * jax.nn.silu(z.astype(jnp.float32))
    yg = y.reshape(b, s, SSM_GROUPS, SSM_D_INNER // SSM_GROUPS)
    yg = yg * lax.rsqrt(jnp.mean(yg * yg, axis=-1, keepdims=True) + NORM_EPS)
    y = yg.reshape(b, s, SSM_D_INNER) * norm_g.astype(jnp.float32)
    return y.astype(z.dtype)

def dsa_branch(q, c_kv, q_idx, k_idx, w_idx, w_uk, w_uv):
    b, s = q.shape[0], q.shape[1]
    topk = min(TOPK_MAX, s // 4)
    q_abs = jnp.einsum('bshd,hrd->bshr', q, w_uk)
    slopes = 2.0 ** (-8.0 * jnp.arange(1, ATT_HEADS + 1, dtype=jnp.float32) / ATT_HEADS)
    key_pos = jnp.arange(s)

    def block(i):
        t0 = i * Q_BLOCK
        qa = lax.dynamic_slice_in_dim(q_abs, t0, Q_BLOCK, axis=1)
        qi = lax.dynamic_slice_in_dim(q_idx, t0, Q_BLOCK, axis=1)
        wi = lax.dynamic_slice_in_dim(w_idx, t0, Q_BLOCK, axis=1)
        t_pos = t0 + jnp.arange(Q_BLOCK)
        logit = jnp.einsum('bthd,bsd->bths', qi, k_idx).astype(jnp.float32) * (IDX_HEAD_DIM ** -0.5)
        score = jnp.einsum('bths,bth->bts', jax.nn.relu(logit), wi.astype(jnp.float32))
        visible = key_pos[None, :] < (t_pos[:, None] // CHUNK + 1) * CHUNK
        score = jnp.where(visible[None], score, -jnp.inf)
        top_val, top_idx = lax.top_k(score, topk)
        valid = top_val > -jnp.inf
        c_sel = jax.vmap(lambda c, ix: c[ix])(c_kv, top_idx)
        att = jnp.einsum('bthr,btkr->bthk', qa, c_sel).astype(jnp.float32) * (ATT_HEAD_DIM ** -0.5)
        dist = jnp.abs(t_pos[None, :, None] - top_idx).astype(jnp.float32)
        att = att - slopes[None, None, :, None] * dist[:, :, None, :]
        att = jnp.where(valid[:, :, None, :], att, -jnp.inf)
        p = jax.nn.softmax(att, axis=-1).astype(c_sel.dtype)
        o_lat = jnp.einsum('bthk,btkr->bthr', p, c_sel)
        return jnp.einsum('bthr,hrd->bthd', o_lat, w_uv)

    out = lax.map(block, jnp.arange(s // Q_BLOCK))
    return jnp.moveaxis(out, 0, 1).reshape(b, s, ATT_WIDTH)

def hier_moe(h, w_group, b_group, w_router, b_router, w_e1, w_e3, w_e2):
    b, s, d = h.shape
    t = h.reshape(b * s, d)
    g_logits = (t @ w_group + b_group).astype(jnp.float32)
    g_prob = jax.nn.softmax(g_logits, axis=-1)
    g_val, g_sel = lax.top_k(g_prob, 1)
    e_logits = (jnp.einsum('td,gde->tge', t, w_router) + b_router).astype(jnp.float32)
    e_logits = jnp.take_along_axis(e_logits, g_sel[:, :, None], axis=1)[:, 0]
    e_prob = jax.nn.softmax(e_logits, axis=-1)
    e_val, e_sel = lax.top_k(e_prob, MOE_TOPK)
    e_val = e_val / jnp.sum(e_val, axis=-1, keepdims=True)
    comb = jnp.sum(jax.nn.one_hot(e_sel, MOE_EXPERTS, dtype=jnp.float32) * e_val[..., None], axis=1)
    gate = jax.nn.one_hot(g_sel[:, 0], MOE_GROUPS, dtype=jnp.float32)[:, :, None] * (g_val * comb)[:, None, :]
    gate = gate.astype(h.dtype)
    y = jnp.zeros_like(t)
    for gi in range(MOE_GROUPS):
        hid = jax.nn.silu(jnp.einsum('td,edf->tef', t, w_e1[gi])) * jnp.einsum('td,edf->tef', t, w_e3[gi])
        y = y + jnp.einsum('tef,efd->td', hid * gate[:, gi, :, None], w_e2[gi])
    return y.reshape(b, s, d)

def setup_inputs(seed: int = 0) -> dict:
    key = jax.random.key(seed)
    ks = jax.random.split(key, 32)
    f32 = jnp.float32
    nrm = lambda k, shape, scale: jax.random.normal(k, shape, f32) * scale
    gain = lambda k, shape: 1.0 + 0.02 * jax.random.normal(k, shape, f32)
    dt0 = jnp.exp(jax.random.uniform(ks[5], (DEPTH, SSM_HEADS), f32, np.log(1e-3), np.log(1e-1)))
    return {
        "x": jax.random.normal(ks[0], (BATCH, SEQ, D_MODEL), f32),
        "norm_mix_g": gain(ks[1], (DEPTH, D_MODEL)),
        "w_in": nrm(ks[2], (DEPTH, D_MODEL, IN_TOTAL), D_MODEL ** -0.5),
        "conv_w": nrm(ks[3], (DEPTH, SSM_CONV, SSM_XBC), SSM_CONV ** -0.5),
        "conv_b": nrm(ks[4], (DEPTH, SSM_XBC), 0.01),
        "dt_bias": dt0 + jnp.log(-jnp.expm1(-dt0)),
        "a_log": jnp.log(jax.random.uniform(ks[6], (DEPTH, SSM_HEADS), f32, 1.0, 16.0)),
        "d_skip": 1.0 + 0.1 * jax.random.normal(ks[7], (DEPTH, SSM_HEADS), f32),
        "ssm_norm_g": gain(ks[8], (DEPTH, SSM_D_INNER)),
        "kv_norm_g": gain(ks[9], (DEPTH, KV_LATENT)),
        "w_uk": nrm(ks[10], (DEPTH, ATT_HEADS, KV_LATENT, ATT_HEAD_DIM), KV_LATENT ** -0.5),
        "w_uv": nrm(ks[11], (DEPTH, ATT_HEADS, KV_LATENT, ATT_HEAD_DIM), KV_LATENT ** -0.5),
        "gate_b": nrm(ks[12], (DEPTH, N_BRANCHES, D_MODEL), 0.01),
        "w_branch_ssm": nrm(ks[13], (DEPTH, SSM_D_INNER, D_MODEL), SSM_D_INNER ** -0.5),
        "w_branch_att": nrm(ks[14], (DEPTH, ATT_WIDTH, D_MODEL), ATT_WIDTH ** -0.5),
        "w_out": nrm(ks[15], (DEPTH, D_MODEL, D_MODEL), D_MODEL ** -0.5),
        "norm_ffn_g": gain(ks[16], (DEPTH, D_MODEL)),
        "w_group": nrm(ks[17], (DEPTH, D_MODEL, MOE_GROUPS), D_MODEL ** -0.5),
        "b_group": nrm(ks[18], (DEPTH, MOE_GROUPS), 0.01),
        "w_router": nrm(ks[19], (DEPTH, MOE_GROUPS, D_MODEL, MOE_EXPERTS), D_MODEL ** -0.5),
        "b_router": nrm(ks[20], (DEPTH, MOE_GROUPS, MOE_EXPERTS), 0.01),
        "w_e1": nrm(ks[21], (DEPTH, MOE_GROUPS, MOE_EXPERTS, D_MODEL, MOE_FF), D_MODEL ** -0.5),
        "w_e3": nrm(ks[22], (DEPTH, MOE_GROUPS, MOE_EXPERTS, D_MODEL, MOE_FF), D_MODEL ** -0.5),
        "w_e2": nrm(ks[23], (DEPTH, MOE_GROUPS, MOE_EXPERTS, MOE_FF, D_MODEL), MOE_FF ** -0.5),
        "norm_final_g": gain(ks[24], (D_MODEL,)),
    }

def reference(x, norm_mix_g, w_in, conv_w, conv_b, dt_bias, a_log, d_skip, ssm_norm_g,
              kv_norm_g, w_uk, w_uv, gate_b, w_branch_ssm, w_branch_att, w_out,
              norm_ffn_g, w_group, b_group, w_router, b_router, w_e1, w_e3, w_e2,
              norm_final_g):
    b, s, d = x.shape
    for layer in range(DEPTH):
        h = rms_norm(x, norm_mix_g[layer])
        u = h @ w_in[layer]
        z, xbc, dt_raw, q, c_kv, q_idx, k_idx, w_idx, gates = split_cols(u, IN_SIZES)
        y_ssm = mamba2_branch(z, xbc, dt_raw, conv_w[layer], conv_b[layer], dt_bias[layer],
                              a_log[layer], d_skip[layer], ssm_norm_g[layer])
        c_kv = rms_norm(c_kv, kv_norm_g[layer])
        w_idx = w_idx * (IDX_HEADS ** -0.5)
        y_att = dsa_branch(q.reshape(b, s, ATT_HEADS, ATT_HEAD_DIM), c_kv,
                           q_idx.reshape(b, s, IDX_HEADS, IDX_HEAD_DIM), k_idx, w_idx,
                           w_uk[layer], w_uv[layer])
        g = jax.nn.sigmoid(gates.reshape(b, s, N_BRANCHES, d) + gate_b[layer])
        mixed = g[:, :, 0] * (y_ssm @ w_branch_ssm[layer]) + g[:, :, 1] * (y_att @ w_branch_att[layer])
        x = x + mixed @ w_out[layer]
        h = rms_norm(x, norm_ffn_g[layer])
        x = x + hier_moe(h, w_group[layer], b_group[layer], w_router[layer], b_router[layer],
                         w_e1[layer], w_e3[layer], w_e2[layer])
    return rms_norm(x, norm_final_g)


_drawn_inputs = setup_inputs


def setup_inputs(seed=0):
    import zlib

    import numpy as np

    out = dict(_drawn_inputs(seed))
    spreads = {}
    factors = {'conv_b': 3.615,
     'ssm_norm_g': 19.058,
     'kv_norm_g': 6.578,
     'gate_b': 8.0,
     'b_group': 28.973,
     'b_router': 27.152,
     'norm_final_g': 8.121,
     'norm_ffn_g': 5.072}
    for name, (base, spread) in spreads.items():
        noise = np.random.default_rng([zlib.crc32(name.encode()), seed]).standard_normal(out[name].shape)
        drawn = base * np.exp(spread * noise) if base else spread * noise
        out[name] = __import__('jax').numpy.asarray(drawn.astype(out[name].dtype))
    for name, factor in factors.items():
        out[name] = (out[name] * factor).astype(out[name].dtype)
    return out
```

```python
from contextlib import ExitStack

import concourse.bass as bass
from concourse import mybir

F32 = mybir.dt.float32
I32 = mybir.dt.int32
ALU = mybir.AluOpType
ACT = mybir.ActivationFunctionType
AX = mybir.AxisListType

P = 128
D = 1024
S = 256
TT = S // P
KD = D // P
EPS = 1e-6
D_INNER = 2 * D
HEADS = 32
HD = 64
GROUPS = 4
HPG = HEADS // GROUPS
XBC = D_INNER + 2 * GROUPS * P
TAPS = 4
ATT_HEADS = 16
LATENT = 256
IDX_HEADS = 8
TOPK = 64
MG = 4
ME = 8
FF = 256
LEAST = -1e30
TAKEN = -3e38

C_Z = 0
C_XBC = C_Z + D_INNER
C_DT = C_XBC + XBC
C_Q = C_DT + HEADS
C_CKV = C_Q + ATT_HEADS * HD
C_QI = C_CKV + LATENT
C_KI = C_QI + IDX_HEADS * HD
C_WI = C_KI + HD
C_GATE = C_WI + IDX_HEADS

N_SMALL = IDX_HEADS + LATENT + HEADS
SLOT = 4096
NSLOTS = 5
ESLOT = 6144
CONV_ORDER = list(range(16, 24)) + list(range(16))


def hybrid_block(nc, x, norm_mix_g, w_in, conv_w, conv_b, dt_bias, a_log, d_skip, ssm_norm_g,
                 kv_norm_g, w_uk, w_uv, gate_b, w_branch_ssm, w_branch_att, w_out, norm_ffn_g,
                 w_group, b_group, w_router, b_router, w_e1, w_e3, w_e2, norm_final_g, out):
    ctx = ExitStack()
    with ctx:
        def sb(name, shape, dt=F32):
            return ctx.enter_context(nc.sbuf_tensor(name, shape, dt))

        def sem(name):
            return ctx.enter_context(nc.semaphore(name))

        ring = sb("ring", [P, NSLOTS * SLOT])
        hT = sb("hT", [P, KD, S])
        xcT = sb("xcT", [P, 24, S])
        xs = sb("xs", [P, TT * D_INNER])
        xdt = sb("xdt", [P, TT * D_INNER])
        kv = sb("kv", [P, 16, S])
        qT = sb("qT", [P, 8, S])
        work = sb("work", [P, 5120])
        ident = sb("ident", [P, P])
        tri = sb("tri", [P, P])
        below = sb("below", [P, P])
        above = sb("above", [P, P])
        ones = sb("ones", [P, P])
        iota_i = sb("iota_i", [P, S], I32)
        iota = sb("iota", [P, P])
        crow = sb("crow", [P, 2, P])
        ccol = sb("ccol", [P, 2, P])
        g_ffn = sb("g_ffn", [P, KD])
        hvec = sb("hvec", [P, 3, HEADS])
        b_route = sb("b_route", [P, MG + MG * ME])
        w_grp = sb("w_grp", [P, KD, MG])
        w_rt = sb("w_rt", [P, MG, KD, ME])
        st = sb("st", [P, 64])
        sp_t = sb("sp_t", [P, 4, TT, HEADS])
        dt = sb("dt", [P, TT, HEADS])
        dA = sb("dA", [P, TT, HEADS])
        eacs = sb("eacs", [P, TT, HEADS])
        dec = sb("dec", [P, HEADS])
        rt = sb("rt", [P, 1024])
        wi = sb("wi", [P, TT, IDX_HEADS])
        top8 = sb("top8", [P, TT, 8])
        n_over_i = sb("n_over_i", [P, 2], I32)

        xn = xdt[:, 0:TT * D].rearrange("p (t d) -> p t d", t=TT)
        x_in = xs[:, 0:TT * D].rearrange("p (t d) -> p t d", t=TT)
        y = xs[:, :].rearrange("p (t d) -> p t d", t=TT)
        xdt3 = xdt[:, :].rearrange("p (t d) -> p t d", t=TT)
        yT = xcT[:, 0:16, :]
        mixT = hT
        kT = kv[:, 0:8, :]
        v_tok = kv[:, 8:16, :].rearrange("p (t a) b -> p t (a b)", t=TT)
        gT = kv
        attT = qT
        qiT = work[:, 0:1024].rearrange("p (m s) -> p m s", m=4)
        kiT = work[:, 1024:1280]
        c_tok = work[:, 1280:1792].rearrange("p (t r) -> p t r", t=TT)
        cT = work[:, 1792:2304].rearrange("p (r s) -> p r s", r=2)
        prob = work[:, 2304:3072].rearrange("p (b s) -> p b s", b=2)
        probT = work[:, 3072:3840].rearrange("p (b s) -> p b s", b=2)
        bias = work[:, 3840:4224]
        dist = work[:, 4224:4608]
        unsel = work[:, 4608:4992]
        stateT = work[:, 0:2048].rearrange("p (g d) -> p g d", g=GROUPS)
        seg_in = work[:, 2048:3072]
        decay = work[:, 3072:4096]
        xdec = work[:, 4096:4608]
        y_off = work[:, 4608:5120]
        th = sb("th", [P, 2, 512])
        cbm = sb("cbm", [P, 2, P])
        sel_work = rt[:, 0:384]
        relu = xs[:, 0:768].rearrange("p (b s) -> p b s", b=2)
        x_again = xdt[:, 0:2048].rearrange("p (t d) -> p t d", t=TT)
        h2T = xdt[:, 2048:4096].rearrange("p (k s) -> p k s", k=KD)
        x2 = xs[:, 0:2048].rearrange("p (t d) -> p t d", t=TT)
        h2 = xs[:, 2048:4096].rearrange("p (t d) -> p t d", t=TT)
        kvf = kv[:, :, :].rearrange("p a b -> p (a b)")
        xgT = kvf[:, 0:1024].rearrange("p (k s) -> p k s", k=KD)
        hid = kvf[:, 1024:1536].rearrange("p (b s) -> p b s", b=2)
        sil = kvf[:, 1536:2048].rearrange("p (b s) -> p b s", b=2)
        hidT = kvf[:, 2048:2560].rearrange("p (b f s) -> p b f s", b=2, f=2)
        y_grp = kvf[:, 2560:3584]
        permT = kvf[:, 3584:3840].rearrange("p (t s) -> p t s", t=TT)
        gate_g = kvf[:, 3840:3848]
        hf = hT[:, :, :].rearrange("p a b -> p (a b)")
        perm = hf[:, 0:1024].rearrange("p (t g s) -> p t g s", t=TT, g=MG)
        perm_cur = hf[:, 1024:1280].rearrange("p (t s) -> p t s", t=TT)
        gate_cur = hf[:, 1280:1296].rearrange("p (t s) -> p t s", t=TT)
        g_fin = xdt[:, 0:D]
        xcf = xcT[:, :, :].rearrange("p a b -> p (a b)")
        eslots = [ring[:, 2 * ESLOT:3 * ESLOT], xcf, ring[:, 0:ESLOT], ring[:, ESLOT:2 * ESLOT]]
        e13 = [e[:, 0:4096].rearrange("p (w k f) -> p w k f", w=2, k=KD) for e in eslots]
        e2 = [e[:, 4096:6144].rearrange("p (k d) -> p k d", k=2) for e in eslots]

        def tap(j, m):
            return ccol[:, 0, j * 24 + m:j * 24 + m + 1]

        def conv_bias(m):
            return ccol[:, 0, 96 + m:97 + m]

        def g_mix(k):
            return ccol[:, 1, k:k + 1]

        def g_ssm(m):
            return ccol[:, 1, 8 + m:9 + m]

        def b_gate(m):
            return ccol[:, 1, 24 + m:25 + m]

        def g_kv(r):
            return ccol[:, 1, 40 + r:41 + r]

        bank = [ctx.enter_context(nc.psum_tensor(f"bank{i}", [P, 512], F32)) for i in range(8)]

        jobs = [("qi",), ("small",), ("q", 0), ("q", 1), ("ukv",)]
        jobs += [("xbc", b) for b in (4, 5, 0, 1, 2, 3)]
        jobs += [("gate", b) for b in range(4)] + [("z", b) for b in range(4)]
        jobs += [("att", b) for b in range(2)] + [("ssm", b) for b in range(4)]
        jobs += [("out", b) for b in range(2)]
        job_no = {j: n for n, j in enumerate(jobs)}
        N_JOBS = len(jobs)

        def slot(job):
            n = job_no[job] % NSLOTS
            return ring[:, n * SLOT:(n + 1) * SLOT]

        def block512(job):
            return slot(job).rearrange("p (k n) -> p k n", k=KD)

        small = slot(("small",))[:, 0:KD * 424].rearrange("p (k n) -> p k n", k=KD)
        w_k = slot(("ukv",))[:, 0:2048].rearrange("p (r n) -> p r n", r=2)
        w_v = slot(("ukv",))[:, 2048:4096].rearrange("p (r n) -> p r n", r=2)
        win = w_in[0].rearrange("(k p) n -> p k n", p=P)

        def loads(job):
            kind = job[0]
            b = block512(job) if kind not in ("small", "ukv", "ssm") else None
            if kind == "small":
                return [(small[:, :, 0:64], win[:, :, C_KI:C_KI + 64]),
                        (small[:, :, 64:136], win[:, :, C_KI:C_KI + 72]),
                        (small[:, :, 136:392], win[:, :, C_CKV:C_CKV + LATENT]),
                        (small[:, :, 392:424], win[:, :, C_DT:C_DT + HEADS])]
            if kind == "ukv":
                res = []
                for dst, src in ((w_k, w_uk), (w_v, w_uv)):
                    for r in range(2):
                        res.append((dst[:, r, :].rearrange("p (h d) -> p h d", d=HD),
                                    src[0, :, r * P:(r + 1) * P, :].rearrange("h p d -> p h d")))
                return res
            if kind == "ssm":
                n = job[1]
                return [(slot(job).rearrange("p (k n) -> p k n", k=16),
                         w_branch_ssm[0].rearrange("(k p) n -> p k n", p=P)[:, :, n * 256:(n + 1) * 256])]
            if kind in ("att", "out"):
                w = (w_branch_att if kind == "att" else w_out)[0].rearrange("(k p) n -> p k n", p=P)
                return [(b, w[:, :, job[1] * 512:(job[1] + 1) * 512])]
            c = {"qi": C_QI, "q": C_Q, "xbc": C_XBC, "gate": C_GATE, "z": C_Z}[kind]
            c += 512 * (job[1] if len(job) > 1 else 0)
            return [(b, win[:, :, c:c + 512])]

        landed_at, per_slot = {}, [0] * NSLOTS
        for n, j in enumerate(jobs):
            per_slot[n % NSLOTS] += 16 * len(loads(j))
            landed_at[j] = per_slot[n % NSLOTS]

        units = [("qi", m) for m in range(4)] + [("ki", 0)] + [("small", t) for t in range(2)]
        units += [("q", m) for m in range(8)] + [("k", m) for m in range(8)]
        units += [("v", n) for n in range(4)] + [("xbc", i) for i in range(24)]
        units += [("gate", m) for m in range(16)] + [("z", n) for n in range(8)]
        units += [("att", m) for m in range(8)] + [("ssm", m) for m in range(8)]
        units += [("out", n) for n in range(4)]
        unit_no = {u: n for n, u in enumerate(units)}
        units_per_bank = [0, 0]
        for n in range(len(units)):
            units_per_bank[n % 2] += 1

        last_unit = {("qi",): ("qi", 3), ("small",): ("small", 1), ("ukv",): ("v", 3)}
        for n in range(4):
            last_unit[("gate", n)] = ("gate", 4 * n + 3)
            last_unit[("z", n)] = ("z", 2 * n + 1)
            last_unit[("ssm", n)] = ("ssm", 2 * n + 1)
        for n in range(2):
            last_unit[("q", n)] = ("q", 4 * n + 3)
            last_unit[("att", n)] = ("att", 4 * n + 3)
            last_unit[("out", n)] = ("out", 2 * n + 1)
        for i in range(3, 24, 4):
            last_unit[("xbc", CONV_ORDER[i] // 4)] = ("xbc", i)
        units_until = [unit_no[last_unit[j]] + 1 for j in jobs]

        def acc(u):
            return bank[unit_no[u] % 2]

        block_landed = [sem(f"block_landed{i}") for i in range(NSLOTS)]
        x_landed = sem("x_landed")
        rows_landed = sem("rows_landed")
        vecs_landed = sem("vecs_landed")
        g_fin_landed = sem("g_fin_landed")
        x_again_landed = sem("x_again_landed")
        masks_ready = sem("masks_ready")
        iota_made = sem("iota_made")
        consts_turned = sem("consts_turned")
        consts_ready = sem("consts_ready")
        ss_ready = sem("ss_ready")
        rms_ready = sem("rms_ready")
        xn_ready = sem("xn_ready")
        xn_turned = sem("xn_turned")
        hT_ready = sem("hT_ready")
        unit_done = sem("unit_done")
        unit_taken = [sem("unit_taken0"), sem("unit_taken1")]
        negA_ready = sem("negA_ready")
        ckv_ss_ready = sem("ckv_ss_ready")
        ckv_rms_ready = sem("ckv_rms_ready")
        c_ready = sem("c_ready")
        c_turned = sem("c_turned")
        cT_ready = sem("cT_ready")
        dt_abs_ready = sem("dt_abs_ready")
        dt_exp_ready = sem("dt_exp_ready")
        dt_u_ready = sem("dt_u_ready")
        dt_ln_ready = sem("dt_ln_ready")
        dA_ready = sem("dA_ready")
        acs_done = sem("acs_done")
        eacs_ready = sem("eacs_ready")
        index_done = sem("index_done")
        relu_ready = sem("relu_ready")
        relu_used = sem("relu_used")
        sel_ready = sem("sel_ready")
        logits_done = sem("logits_done")
        att_biased = sem("att_biased")
        exp_ready = sem("exp_ready")
        prob_ready = sem("prob_ready")
        prob_turned = sem("prob_turned")
        probT_ready = sem("probT_ready")
        pv_done = sem("pv_done")
        attT_ready = sem("attT_ready")
        first_tap_ready = sem("first_tap_ready")
        conv_ready = sem("conv_ready")
        tanh_ready = sem("tanh_ready")
        xc_ready = sem("xc_ready")
        gate_ready = sem("gate_ready")
        seg_in_ready = sem("seg_in_ready")
        seg_done = sem("seg_done")
        xs_turned = sem("xs_turned")
        xdt_ready = sem("xdt_ready")
        cb_done = sem("cb_done")
        cb_ready = sem("cb_ready")
        b_tok_ready = sem("b_tok_ready")
        decay_ready = sem("decay_ready")
        wts_ready = sem("wts_ready")
        y_diag_done = sem("y_diag_done")
        state_done = sem("state_done")
        state_ready = sem("state_ready")
        y_off_done = sem("y_off_done")
        y_ready = sem("y_ready")
        z_tanh_ready = sem("z_tanh_ready")
        y_gated = sem("y_gated")
        y_ss_ready = sem("y_ss_ready")
        y_rms_ready = sem("y_rms_ready")
        y_normed = sem("y_normed")
        y_turned = sem("y_turned")
        yT_ready = sem("yT_ready")
        mix_ready = sem("mix_ready")
        x2_ready = sem("x2_ready")
        x2_ss_ready = sem("x2_ss_ready")
        x2_rms_ready = sem("x2_rms_ready")
        h2_ready = sem("h2_ready")
        h2_turned = sem("h2_turned")
        h2T_ready = sem("h2T_ready")
        route_done = sem("route_done")
        route_in = sem("route_in")
        route_exp = sem("route_exp")
        onehot_ready = sem("onehot_ready")
        rank_done = sem("rank_done")
        route_ready = sem("route_ready")
        e13_landed = [sem(f"e13_landed{i}") for i in range(4)]
        e2_landed = [sem(f"e2_landed{i}") for i in range(4)]
        perm_ready = sem("perm_ready")
        perm_copied = sem("perm_copied")
        gathered = sem("gathered")
        places_done = sem("places_done")
        places_ready = sem("places_ready")
        xgT_ready_a = sem("xgT_ready_a")
        xgT_ready_v = sem("xgT_ready_v")
        up_done = sem("up_done")
        silu_ready = sem("silu_ready")
        hid_ready = sem("hid_ready")
        hid_turned = sem("hid_turned")
        hidT_ready = sem("hidT_ready")
        down_done = sem("down_done")
        y_grp_ready = sem("y_grp_ready")
        scattered = sem("scattered")
        added = sem("added")
        fin_ss_ready = sem("fin_ss_ready")
        fin_rms_ready = sem("fin_rms_ready")
        out_ready = sem("out_ready")
        out_stored = sem("out_stored")
        v_step = sem("v_step")
        a_step = sem("a_step")
        p_step = sem("p_step")

        class Steps:

            def __init__(self, eng, own):
                self.eng, self.own, self.n = eng, own, 0

            def __call__(self, ins):
                self.n += 1
                ins.then_inc(self.own, 1)
                self.eng.wait_ge(self.own, self.n)

        def wait_unit(eng, u):
            eng.wait_ge(unit_done, unit_no[u] + 1)

        def took(ins, u):
            ins.then_inc(unit_taken[unit_no[u] % 2], 1)

        KEYS = [(0, 128), (128, 384)]
        e1_v = w_e1[0].rearrange("g e (p k) f -> (g e) p k f", k=KD)
        e3_v = w_e3[0].rearrange("g e (p k) f -> (g e) p k f", k=KD)
        e2_v = w_e2[0].rearrange("g e (k p) d -> (g e) p k d", p=P)

        block = ctx.enter_context(nc.Block())

        @block.sync
        def _(sp):
            for t in range(TT):
                sp.dma_start(x_in[:, t, :], x[0, t * P:(t + 1) * P, :]).then_inc(x_landed, 16)
            for n, job in enumerate(jobs):
                if n >= NSLOTS:
                    sp.wait_ge(unit_done, units_until[n - NSLOTS])
                for dst, src in loads(job):
                    sp.dma_start(dst, src).then_inc(block_landed[n % NSLOTS], 16)

            def load_expert(e, idx):
                s = e % 4
                sp.dma_start(e13[s][:, 0, :, :], e1_v[bass.ds(idx, 1)].rearrange("o p k f -> p (o k) f"))\
                    .then_inc(e13_landed[s], 16)
                sp.dma_start(e13[s][:, 1, :, :], e3_v[bass.ds(idx, 1)].rearrange("o p k f -> p (o k) f"))\
                    .then_inc(e13_landed[s], 16)

            def load_expert2(e, idx):
                s = e % 4
                sp.dma_start(e2[s], e2_v[bass.ds(idx, 1)].rearrange("o p k d -> p (o k) d"))\
                    .then_inc(e2_landed[s], 16)

            for e in range(4):
                sp.wait_ge(unit_done, units_until[N_JOBS - 3 if e < 2 else N_JOBS - 1])
                load_expert(e, e)
                load_expert2(e, e)
            with sp.Fori(0, MG - 1) as it:
                for e in range(ME):
                    sp.wait_ge(up_done, it * ME + (e + 1))
                    load_expert(e, it * ME + (e + 4))
                    sp.wait_ge(down_done, it * ME + (e + 1))
                    load_expert2(e, it * ME + (e + 4))
            for e in range(4):
                n = (MG - 1) * ME + e
                sp.wait_ge(up_done, n + 1)
                load_expert(e, n + 4)
                sp.wait_ge(down_done, n + 1)
                load_expert2(e, n + 4)
            sp.wait_ge(route_ready, 1)
            over = sp.value_load(n_over_i[0:1, 0:1], min_val=0, max_val=1)
            with sp.If(over):
                gx = sp.value_load(n_over_i[0:1, 1:2], min_val=0, max_val=MG - 1)
                for e in range(ME):
                    n = MG * ME + e
                    sp.wait_ge(up_done, n - 3)
                    load_expert(e, gx * ME + e)
                    sp.wait_ge(down_done, n - 3)
                    load_expert2(e, gx * ME + e)
            for t in range(TT):
                sp.wait_ge(out_ready, t + 1)
                sp.dma_start(out[0, t * P:(t + 1) * P, :], x2[:, t, :]).then_inc(out_stored, 16)
            sp.wait_ge(out_stored, 16 * TT)

        @block.gpsimd
        def _(pool):
            pool.memset(ones[:, :], 1.0).then_inc(masks_ready, 1)
            for m in (ident, tri, below, above):
                pool.memset(m[:, :], 0.0 if m is ident else 1.0).then_inc(p_step, 1)
            pool.wait_ge(p_step, 4)
            for m, cmp, fill, mult, step in ((ident, ALU.not_equal, 1.0, 1, -1), (tri, ALU.is_ge, 0.0, -1, 1),
                                             (below, ALU.is_gt, 0.0, 1, -1), (above, ALU.is_gt, 0.0, -1, 1)):
                pool.affine_select(out=m[:, :], in_=m[:, :], compare_op=cmp, fill=fill, base=0,
                                   pattern=[[step, P]], channel_multiplier=mult).then_inc(masks_ready, 1)
            for dst, base, mult, n in ((dist[:, 0:128], 0, 1, P), (dist[:, 128:384], P, 1, S)):
                pool.iota(iota_i[:, 0:n], pattern=[[-1, n]], base=base, channel_multiplier=mult).then_inc(p_step, 1)
                pool.wait_ge(p_step, 5 if n == P else 7)
                pool.tensor_copy(dst, iota_i[:, 0:n]).then_inc(p_step, 1)
                pool.wait_ge(p_step, 6 if n == P else 8)
            pool.iota(iota_i[:, 0:P], pattern=[[1, P]], base=0, channel_multiplier=0).then_inc(p_step, 1)
            pool.wait_ge(p_step, 9)
            pool.tensor_copy(iota[:, :], iota_i[:, 0:P]).then_inc(iota_made, 1)
            row = lambda a, n: a.rearrange("(o n) -> o n", o=1).to_broadcast([P, n])
            for m in range(16):
                i = unit_no[("gate", m)]
                pool.wait_ge(unit_taken[i % 2], i // 2 + 1)
                pool.tensor_scalar(gT[:, m, :], gT[:, m, :], 1.0, 0.5, ALU.add, ALU.mult).then_inc(gate_ready, 1)
            pool.wait_ge(y_ready, 8)
            for t in range(TT):
                pool.dma_start(x_again[:, t, :], x[0, t * P:(t + 1) * P, :]).then_inc(x_again_landed, 16)
            pool.wait_ge(x_again_landed, 32)
            pool.wait_ge(x2_ready, 4)
            pool.dma_start(g_fin, row(norm_final_g, D)).then_inc(g_fin_landed, 16)
        VECS = 16 * 8

        @block.tensor
        def _(pe):
            def unit(u, pairs, n, m=P):
                i = unit_no[u]
                if i >= 2:
                    pe.wait_ge(unit_taken[i % 2], i // 2)
                for k, (lhsT, rhs) in enumerate(pairs):
                    mm = pe.matmul(bank[i % 2][0:m, 0:n], lhsT, rhs, start=(k == 0), stop=(k == len(pairs) - 1))
                mm.then_inc(unit_done, 1)
                return mm

            def landed(job):
                pe.wait_ge(block_landed[job_no[job] % NSLOTS], landed_at[job])

            pe.wait_ge(masks_ready, 5)
            pe.wait_ge(rows_landed, 16 * 6)
            pe.transpose(bank[7][:, 0:120], crow[0:120, 0, :], ident[0:120, 0:120])
            pe.transpose(bank[7][:, 128:170], crow[0:42, 1, :], ident[0:42, 0:42]).then_inc(consts_turned, 1)
            for j in range(4):
                pe.wait_ge(xn_ready, TT)
                if j >= 2:
                    pe.wait_ge(hT_ready, 2 * (j - 1))
                for k in (2 * j, 2 * j + 1):
                    for t in range(TT):
                        c = (k % 2) * 256 + t * P
                        tr = pe.transpose(bank[2 + j % 2][:, c:c + P], xn[:, t, k * P:(k + 1) * P], ident[:, :])
                tr.then_inc(xn_turned, 1)
            pe.wait_ge(hT_ready, KD)

            def channel_unit(u, w, c):
                unit(u, [(w[:, k, c:c + P], hT[:, k, :]) for k in range(KD)], S)

            landed(("qi",))
            for m in range(4):
                channel_unit(("qi", m), block512(("qi",)), m * P)
            landed(("small",))
            channel_unit(("ki", 0), small, 0)
            for t in range(TT):
                mm = unit(("small", t), [(hT[:, k, t * P:(t + 1) * P], small[:, k, P:P + N_SMALL])
                                         for k in range(KD)], N_SMALL)
            for m in range(8):
                if m % 4 == 0:
                    landed(("q", m // 4))
                channel_unit(("q", m), block512(("q", m // 4)), m % 4 * P)

            pe.wait_ge(dA_ready, 1)
            for t in range(TT):
                pe.matmul(bank[7][:, t * HEADS:(t + 1) * HEADS], tri[:, :], dA[:, t, :], start=True, stop=True)
            pe.matmul(bank[7][:, 64:96], below[:, :], dA[:, 0, :], start=True, stop=True).then_inc(acs_done, 1)

            pe.wait_ge(c_ready, 1)
            for r in range(2):
                for t in range(TT):
                    c = r * 256 + t * P
                    tr = pe.transpose(bank[4][:, c:c + P], c_tok[:, t, r * P:(r + 1) * P], ident[:, :])
            tr.then_inc(c_turned, 1)

            pe.wait_ge(unit_taken[0], unit_no[("ki", 0)] // 2 + 1)
            pe.wait_ge(unit_taken[1], unit_no[("qi", 3)] // 2 + 1)
            for h in range(IDX_HEADS):
                if h >= 2:
                    pe.wait_ge(relu_ready, h - 1)
                r = slice(64 * (h % 2), 64 * (h % 2) + 64)
                for t, (a, b) in enumerate(KEYS):
                    mm = pe.matmul(bank[2 + h % 2][:, a:b], qiT[r, h // 2, t * P:(t + 1) * P], kiT[r, 0:b - a],
                                   start=True, stop=True)
                mm.then_inc(index_done, 1)

            landed(("ukv",))
            pe.wait_ge(cT_ready, 2)
            for m in range(8):
                unit(("k", m), [(w_k[:, r, m * P:(m + 1) * P], cT[:, r, :]) for r in range(2)], S)
            for n in range(4):
                t, half = n // 2, n % 2
                mm = unit(("v", n), [(cT[:, r, t * P:(t + 1) * P], w_v[:, r, half * 512:(half + 1) * 512])
                                     for r in range(2)], 512)

            def logits(h):
                if h == 0:
                    pe.wait_ge(unit_taken[0], (unit_no[("v", 3)]) // 2 + 1)
                    pe.wait_ge(unit_taken[1], (unit_no[("v", 3)] + 1) // 2)
                    pe.wait_ge(relu_ready, IDX_HEADS)
                if h >= 2:
                    pe.wait_ge(att_biased, h - 1)
                r = slice(64 * (h % 2), 64 * (h % 2) + 64)
                for t, (a, b) in enumerate(KEYS):
                    mm = pe.matmul(bank[2 + h % 2][:, a:b], qT[r, h // 2, t * P:(t + 1) * P], kT[r, h // 2, 0:b - a],
                                   start=True, stop=True)
                mm.then_inc(logits_done, 1)

            def turn_prob(h):
                pe.wait_ge(prob_ready, h + 1)
                if h >= 1:
                    pe.wait_ge(probT_ready, h)
                for c in range(3):
                    tr = pe.transpose(bank[4][:, c * P:(c + 1) * P], prob[:, h % 2, c * P:(c + 1) * P], ident[:, :])
                tr.then_inc(prob_turned, 1)

            def pv(h):
                pe.wait_ge(probT_ready, h + 1)
                if h >= 2:
                    pe.wait_ge(attT_ready, h - 1)
                r = slice(64 * (h % 2), 64 * (h % 2) + 64)
                o = bank[5 + h % 2][r, 0:S]
                pe.matmul(o, v_tok[:, 0, h * HD:(h + 1) * HD], probT[:, h % 2, 0:256], start=True, stop=False)
                pe.matmul(o[:, P:S], v_tok[:, 1, h * HD:(h + 1) * HD], probT[:, h % 2, 256:384],
                          start=False, stop=True).then_inc(pv_done, 1)

            for i in range(24):
                m = CONV_ORDER[i]
                job = ("xbc", m // 4)
                if i % 4 == 0:
                    landed(job)
                channel_unit(("xbc", i), block512(job), m % 4 * P)
                if i < ATT_HEADS:
                    logits(i)
                if 1 <= i <= ATT_HEADS:
                    turn_prob(i - 1)
                if 2 <= i <= ATT_HEADS + 1:
                    pv(i - 2)

            def ssd_a(q):
                c, g = q // GROUPS, q % GROUPS
                ts = slice(c * P, (c + 1) * P)
                if q == 0:
                    pe.wait_ge(xc_ready, 24)
                    pe.wait_ge(attT_ready, ATT_HEADS)
                if q >= 1:
                    pe.wait_ge(xdt_ready, q)
                for j in range(4):
                    tr = pe.transpose(bank[5][:, j * P:(j + 1) * P], xcT[:, 4 * g + j, ts], ident[:, :])
                tr.then_inc(xs_turned, 1)
                if q >= 1:
                    pe.wait_ge(cb_ready, q)
                    if c == 0:
                        pe.wait_ge(b_tok_ready, q)
                if c == 0:
                    pe.transpose(bank[4][:, 256:384], xcT[:, 16 + g, ts], ident[:, :])
                pe.matmul(bank[4][:, 0:P], xcT[:, 16 + g, ts], xcT[:, 20 + g, ts], start=True, stop=True)\
                    .then_inc(cb_done, 1)
                pe.wait_ge(seg_in_ready, q + 1)
                if q >= 1:
                    pe.wait_ge(decay_ready, q)
                for j in range(2):
                    mm = pe.matmul(bank[2 + j][:, :], below[:, :], seg_in[:, j * 512:(j + 1) * 512], start=True, stop=True)
                mm.then_inc(seg_done, 1)

            def ssd_b(q):
                c, g = q // GROUPS, q % GROUPS
                pe.wait_ge(wts_ready, q + 1)
                if q >= 1:
                    pe.wait_ge(y_ready, q)
                for h in range(HPG):
                    col = (g * HPG + h) * HD
                    mm = pe.matmul(bank[6][:, h * HD:(h + 1) * HD], decay[:, h * P:(h + 1) * P],
                                   xdt3[:, c, col:col + HD], start=True, stop=True)
                mm.then_inc(y_diag_done, 1)
                if c == 0:
                    pe.wait_ge(b_tok_ready, q + 1)
                    if q >= 1:
                        pe.wait_ge(state_ready, q)
                    pe.matmul(bank[7][:, :], cbm[:, 1, :], xdec, start=True, stop=True).then_inc(state_done, 1)
                else:
                    pe.wait_ge(state_ready, GROUPS)
                    pe.matmul(bank[7][:, :], xcT[:, 20 + g, P:S], stateT[:, g, :], start=True, stop=True)\
                        .then_inc(y_off_done, 1)

            for m in range(16):
                job = ("gate", m // 4)
                if m % 4 == 0:
                    landed(job)
                channel_unit(("gate", m), block512(job), m % 4 * P)
                ssd_a(m // 2) if m % 2 == 0 else ssd_b(m // 2)

            for n in range(8):
                g, t = n // 2, n % 2
                job = ("z", g)
                if t == 0:
                    landed(job)
                mm = unit(("z", n), [(hT[:, k, t * P:(t + 1) * P], block512(job)[:, k, :]) for k in range(KD)], 512)

            def turn_y(j):
                pe.wait_ge(y_normed, 8)
                if j >= 2:
                    pe.wait_ge(yT_ready, 2 * (j - 1))
                for m in (2 * j, 2 * j + 1):
                    for t in range(TT):
                        c = (m % 2) * 256 + t * P
                        tr = pe.transpose(bank[2 + j % 2][:, c:c + P], y[:, t, m * P:(m + 1) * P], ident[:, :])
                tr.then_inc(y_turned, 1)

            for m in range(8):
                job = ("att", m // 4)
                if m % 4 == 0:
                    landed(job)
                w = block512(job)
                mm = unit(("att", m), [(w[:, k, m % 4 * P:(m % 4 + 1) * P], attT[:, k, :]) for k in range(8)], S)
                if m >= 1:
                    turn_y(m - 1)
            turn_y(7)
            pe.wait_ge(yT_ready, 16)
            for m in range(8):
                job = ("ssm", m // 2)
                if m % 2 == 0:
                    landed(job)
                w = slot(job).rearrange("p (k n) -> p k n", k=16)
                mm = unit(("ssm", m), [(w[:, k, m % 2 * P:(m % 2 + 1) * P], yT[:, k, :]) for k in range(16)], S)
            pe.wait_ge(mix_ready, 8)
            for n in range(4):
                half, t = n // 2, n % 2
                job = ("out", half)
                if t == 0:
                    landed(job)
                mm = unit(("out", n), [(mixT[:, k, t * P:(t + 1) * P], block512(job)[:, k, :]) for k in range(KD)], 512)

            pe.wait_ge(h2_ready, TT)
            for j in range(4):
                if j >= 2:
                    pe.wait_ge(h2T_ready, 2 * (j - 1))
                for k in (2 * j, 2 * j + 1):
                    for t in range(TT):
                        c = (k % 2) * 256 + t * P
                        tr = pe.transpose(bank[2 + j % 2][:, c:c + P], h2[:, t, k:D:KD], ident[:, :])
                tr.then_inc(h2_turned, 1)
            pe.wait_ge(h2T_ready, KD)
            pe.wait_ge(vecs_landed, VECS)
            for t in range(TT):
                for o, n, w in ((0, MG, lambda k: w_grp[:, k, :]), (64, MG * ME, lambda k: w_rt[:, :, k, :])):
                    c = t * P + o
                    for k in range(KD):
                        mm = pe.matmul(bank[7][:, c:c + n], h2T[:, k, t * P:(t + 1) * P], w(k),
                                       start=(k == 0), stop=(k == KD - 1))
            mm.then_inc(route_done, 1)
            pe.wait_ge(onehot_ready, 1)
            oh = rt[:, 0:8].rearrange("p (t g) -> p t g", t=TT)
            pe.matmul(bank[6][:, 0:MG], above[:, :], oh[:, 0, :], start=True, stop=True)
            pe.matmul(bank[6][:, 8:8 + MG], above[:, :], oh[:, 1, :], start=True, stop=False)
            pe.matmul(bank[6][:, 8:8 + MG], ones[:, :], oh[:, 0, :], start=False, stop=True)
            pe.matmul(bank[6][:, 16:16 + MG], ones[:, :], oh[:, 0, :], start=True, stop=False)
            pe.matmul(bank[6][:, 16:16 + MG], ones[:, :], oh[:, 1, :], start=False, stop=True).then_inc(rank_done, 1)

            def up(it, e, ks):
                s = e % 4
                if ks[0] == 0:
                    if e >= 2:
                        pe.wait_ge(hid_ready, it * ME + (e - 1))
                    pe.wait_ge(e13_landed[s], it * 64 + 32 * (e // 4 + 1))
                for k in ks:
                    mm = pe.matmul(bank[e % 2][:, :].rearrange("p (w f) -> p w f", w=2), xgT[:, k, :],
                                   e13[s][:, :, k, :], start=(k == 0), stop=(k == KD - 1))
                if ks[-1] == KD - 1:
                    mm.then_inc(up_done, 1)

            def turn_hid(it, e):
                pe.wait_ge(hid_ready, it * ME + (e + 1))
                for f in range(2):
                    c = f * P
                    tr = pe.transpose(bank[7 if e % 2 else 2][:, c:c + P], hid[:, e % 2, f * P:(f + 1) * P], ident[:, :])
                tr.then_inc(hid_turned, 1)

            def down(it, e):
                pe.wait_ge(hidT_ready, it * ME + (e + 1))
                pe.wait_ge(e2_landed[e % 4], it * 32 + 16 * (e // 4 + 1))
                for half in range(2):
                    for f in range(2):
                        mm = pe.matmul(bank[5 + half][:, :], hidT[:, e % 2, f, :],
                                       e2[e % 4][:, f, half * 512:(half + 1) * 512],
                                       start=(e == 0 and f == 0), stop=(e == ME - 1 and f == 1))
                mm.then_inc(down_done, 1)

            def group_pass(it):
                pe.wait_ge(perm_ready, it + 1)
                for k in range(KD):
                    c = (k % 4) * P
                    for t in range(TT):
                        mm = pe.matmul(bank[3 + k // 4][:, c:c + P], h2[:, t, k:D:KD], perm_cur[:, t, :],
                                       start=(t == 0), stop=(t == TT - 1))
                    if k % 4 == 3:
                        mm.then_inc(gathered, 1)
                for t in range(TT):
                    pe.matmul(bank[7][:, 0:ME], perm_cur[:, t, :], gate_cur[:, t, :], start=(t == 0), stop=(t == 1))
                for t in range(TT):
                    tr = pe.transpose(bank[7][:, P + t * P:2 * P + t * P], perm_cur[:, t, :], ident[:, :])
                tr.then_inc(places_done, 1)
                pe.wait_ge(xgT_ready_a, it + 1)
                pe.wait_ge(xgT_ready_v, it + 1)
                up(it, 0, range(KD))
                for e in range(1, ME):
                    up(it, e, range(0, 6))
                    turn_hid(it, e - 1)
                    up(it, e, range(6, KD))
                    down(it, e - 1)
                turn_hid(it, ME - 1)
                down(it, ME - 1)
                pe.wait_ge(places_ready, it + 1)
                for n in range(4):
                    t, half = n // 2, n % 2
                    if n < 2:
                        pe.wait_ge(y_grp_ready, it * 2 + (n + 1))
                    else:
                        pe.wait_ge(added, it * 4 + (n - 1))
                    pe.matmul(bank[3 + half][:, :], permT[:, t, :], y_grp[:, half * 512:(half + 1) * 512],
                              start=True, stop=True).then_inc(scattered, 1)

            with pe.Fori(0, MG) as it:
                group_pass(it)
            pe.wait_ge(route_ready, 1)
            over = pe.value_load(n_over_i[0:1, 0:1], min_val=0, max_val=1)
            with pe.If(over):
                group_pass(MG)

        @block.scalar
        def _(act):
            step = Steps(act, a_step)
            A = nc.scalar.activation
            cw = conv_w[0].rearrange("j (m c) -> (j m) c", c=P)
            one = lambda a: a.rearrange("(m c) -> m c", c=P)
            for dst, src in ((crow[0:96, 0, :], cw), (crow[96:120, 0, :], one(conv_b[0])),
                             (crow[0:8, 1, :], one(norm_mix_g[0])), (crow[8:24, 1, :], one(ssm_norm_g[0])),
                             (crow[24:40, 1, :], gate_b[0].rearrange("b (m c) -> (b m) c", c=P)),
                             (crow[40:42, 1, :], one(kv_norm_g[0]))):
                act.dma_start(dst, src).then_inc(rows_landed, 16)
            row = lambda a, n: a.rearrange("(o n) -> o n", o=1).to_broadcast([P, n])
            for i, v in enumerate((dt_bias, a_log, d_skip)):
                act.dma_start(hvec[:, i, :], row(v[0], HEADS)).then_inc(vecs_landed, 16)
            act.dma_start(b_route[:, 0:MG], row(b_group[0], MG)).then_inc(vecs_landed, 16)
            act.dma_start(b_route[:, MG:], row(b_router[0].rearrange("g e -> (g e)"), MG * ME)).then_inc(vecs_landed, 16)
            act.dma_start(g_ffn[:, :], norm_ffn_g[0].rearrange("(p k) -> p k", k=KD)).then_inc(vecs_landed, 16)
            act.dma_start(w_grp[:, :, :], w_group[0].rearrange("(p k) g -> p k g", k=KD)).then_inc(vecs_landed, 16)
            act.dma_start(w_rt[:, :, :, :].rearrange("p g k e -> p g (k e)"),
                           w_router[0].rearrange("g (p k) e -> p g (k e)", k=KD)).then_inc(vecs_landed, 16)

            act.wait_ge(x_landed, 32)
            for t in range(TT):
                A(xn[:, t, :], x_in[:, t, :], ACT.Square, accum_out=st[:, t:t + 1]).then_inc(ss_ready, 1)
            act.wait_ge(ss_ready, TT + 1)
            A(st[:, 2:4], st[:, 0:2], ACT.Sqrt, bias=st[:, 63:64], scale=1.0 / D).then_inc(rms_ready, 1)

            for u in [("qi", m) for m in range(4)] + [("ki", 0)]:
                wait_unit(act, u)
                if u == ("qi", 0):
                    act.wait_ge(hT_ready, KD)
                took(A(qiT[:, u[1], :] if u[0] == "qi" else kiT, acc(u)[:, 0:S], ACT.Copy), u)
            act.wait_ge(ckv_ss_ready, TT)
            A(st[:, 6:8], st[:, 4:6], ACT.Sqrt, bias=st[:, 63:64], scale=1.0 / LATENT).then_inc(ckv_rms_ready, 1)
            act.wait_ge(vecs_landed, VECS)
            step(A(hvec[:, 1, :], hvec[:, 1, :], ACT.Exp))
            nc.scalar.mul(hvec[:, 1, :], hvec[:, 1, :], -1.0).then_inc(negA_ready, 1)
            act.wait_ge(dt_abs_ready, 1)
            A(sp_t[:, 1, :, :], sp_t[:, 1, :, :], ACT.Exp, scale=-1.0).then_inc(dt_exp_ready, 1)
            act.wait_ge(dt_u_ready, 1)
            A(sp_t[:, 3, :, :], sp_t[:, 2, :, :], ACT.Ln).then_inc(dt_ln_ready, 1)
            for m in range(8):
                u = ("q", m)
                wait_unit(act, u)
                took(A(qT[:, m, :], acc(u)[:, 0:S], ACT.Copy, scale=HD ** -0.5), u)
            act.wait_ge(acs_done, 1)
            A(eacs[:, :, :].rearrange("p t h -> p (t h)"), bank[7][:, 0:64], ACT.Exp)
            A(dec[:, :], bank[7][:, 64:96], ACT.Exp).then_inc(eacs_ready, 1)
            act.wait_ge(c_turned, 1)
            for r in range(2):
                A(cT[:, r, :], bank[4][:, r * 256:(r + 1) * 256], ACT.Copy, scale=g_kv(r)).then_inc(cT_ready, 1)
            for h in range(IDX_HEADS):
                act.wait_ge(index_done, h + 1)
                if h >= 2:
                    act.wait_ge(relu_used, h - 1)
                A(relu[:, h % 2, :], bank[2 + h % 2][:, 0:384], ACT.Relu, scale=HD ** -0.5).then_inc(relu_ready, 1)
            for m in range(8):
                u = ("k", m)
                wait_unit(act, u)
                took(A(kT[:, m, :], acc(u)[:, 0:S], ACT.Copy), u)
            for n in range(4):
                u = ("v", n)
                wait_unit(act, u)
                took(A(v_tok[:, n // 2, n % 2 * 512:(n % 2 + 1) * 512], acc(u)[:, :], ACT.Copy), u)

            def tanh_of(i):
                act.wait_ge(conv_ready, i + 1)
                if i >= 2:
                    act.wait_ge(xc_ready, i - 1)
                A(th[:, i % 2, 0:S], xcT[:, CONV_ORDER[i], :], ACT.Tanh).then_inc(tanh_ready, 1)

            for i in range(25):
                if i < 24:
                    m = CONV_ORDER[i]
                    wait_unit(act, ("xbc", i))
                    A(xcT[:, m, :], acc(("xbc", i))[:, 0:S], ACT.Identity, bias=conv_bias(m), scale=tap(3, m))\
                        .then_inc(first_tap_ready, 1)
                if i >= 1:
                    tanh_of(i - 1)
                if i < ATT_HEADS:
                    act.wait_ge(att_biased, i + 1)
                    for t, (a, b) in enumerate(KEYS):
                        c = 8 + 2 * (i % 2) + t
                        A(prob[:, i % 2, a:b], prob[:, i % 2, a:b], ACT.Exp, bias=st[:, c:c + 1], scale=-1.0,
                          accum_out=st[:, c + 8:c + 9]).then_inc(exp_ready, 1)
                if 1 <= i <= ATT_HEADS:
                    h = i - 1
                    act.wait_ge(prob_turned, h + 1)
                    if h >= 2:
                        act.wait_ge(pv_done, h - 1)
                    A(probT[:, h % 2, :], bank[4][:, 0:384], ACT.Copy).then_inc(probT_ready, 1)
                if 2 <= i <= ATT_HEADS + 1:
                    h = i - 2
                    r = slice(64 * (h % 2), 64 * (h % 2) + 64)
                    act.wait_ge(pv_done, h + 1)
                    A(attT[r, h // 2, :], bank[5 + h % 2][r, 0:S], ACT.Copy).then_inc(attT_ready, 1)

            for m in range(16):
                u = ("gate", m)
                wait_unit(act, u)
                ins = A(gT[:, m, :], acc(u)[:, 0:S], ACT.Tanh, bias=b_gate(m), scale=0.5)
                took(ins, u)
                q = m // 2
                if m % 2 == 0:
                    act.wait_ge(seg_done, q + 1)
                    if q >= 1:
                        act.wait_ge(y_diag_done, q)
                    for j in range(2):
                        ins = A(decay[:, j * 512:(j + 1) * 512], bank[2 + j][:, :], ACT.Exp)
                    ins.then_inc(decay_ready, 1)
                elif q < GROUPS:
                    act.wait_ge(state_done, q + 1)
                    A(stateT[:, q, :], bank[7][:, :], ACT.Copy).then_inc(state_ready, 1)

            for n in range(8):
                g, t = n // 2, n % 2
                wait_unit(act, ("z", n))
                if n >= 2:
                    act.wait_ge(y_gated, n - 1)
                A(th[:, n % 2, :], acc(("z", n))[:, :], ACT.Tanh, scale=0.5).then_inc(z_tanh_ready, 1)
                act.wait_ge(y_gated, n + 1)
                A(y_off, y[:, t, g * 512:(g + 1) * 512], ACT.Square, accum_out=st[:, 24 + n:25 + n])\
                    .then_inc(y_ss_ready, 1)
            act.wait_ge(y_ss_ready, 8)
            A(st[:, 32:40], st[:, 24:32], ACT.Sqrt, bias=st[:, 63:64], scale=1.0 / 512).then_inc(y_rms_ready, 1)
            for j in range(8):
                act.wait_ge(y_turned, j + 1)
                for m in (2 * j, 2 * j + 1):
                    c = (m % 2) * 256
                    A(yT[:, m, :], bank[2 + j % 2][:, c:c + S], ACT.Copy, scale=g_ssm(m)).then_inc(yT_ready, 1)

            for t in range(TT):
                act.wait_ge(x2_ready, 4)
                A(h2[:, t, :], x2[:, t, :], ACT.Square, accum_out=st[:, 40 + t:41 + t]).then_inc(x2_ss_ready, 1)
            act.wait_ge(x2_ss_ready, TT)
            A(st[:, 42:44], st[:, 40:42], ACT.Sqrt, bias=st[:, 63:64], scale=1.0 / D).then_inc(x2_rms_ready, 1)
            act.wait_ge(route_in, 1)
            A(rt[:, 16:24], rt[:, 16:24], ACT.Exp)
            A(rt[:, 480:482], rt[:, 480:482], ACT.Exp).then_inc(route_exp, 1)

            def group_pass(it):
                act.wait_ge(gathered, it * 2 + 1)
                for k in range(4):
                    ins = A(xgT[:, k, :], bank[3][:, k * P:(k + 1) * P], ACT.Copy, scale=g_ffn[:, k:k + 1])
                ins.then_inc(xgT_ready_a, 1)
                act.wait_ge(places_done, it + 1)
                A(gate_g, bank[7][:, 0:ME], ACT.Copy)
                A(permT[:, :, :].rearrange("p t s -> p (t s)"), bank[7][:, P:3 * P], ACT.Copy).then_inc(places_ready, 1)
                for e in range(ME + 1):
                    if e < ME:
                        act.wait_ge(up_done, it * ME + (e + 1))
                        if e >= 2:
                            act.wait_ge(hid_ready, it * ME + (e - 1))
                        A(sil[:, e % 2, :], bank[e % 2][:, 0:FF], ACT.Silu).then_inc(silu_ready, 1)
                    if e >= 1:
                        d = e - 1
                        act.wait_ge(hid_turned, it * ME + (d + 1))
                        if d >= 2:
                            act.wait_ge(down_done, it * ME + (d - 1))
                        A(hidT[:, d % 2, :, :].rearrange("p f s -> p (f s)"),
                          bank[7 if d % 2 else 2][:, 0:256], ACT.Copy).then_inc(hidT_ready, 1)
                act.wait_ge(down_done, it * ME + ME)
                for half in range(2):
                    A(y_grp[:, half * 512:(half + 1) * 512], bank[5 + half][:, :], ACT.Copy).then_inc(y_grp_ready, 1)

            with act.Fori(0, MG) as it:
                group_pass(it)
            act.wait_ge(route_ready, 1)
            over = act.value_load(n_over_i[0:1, 0:1], min_val=0, max_val=1)
            with act.If(over):
                group_pass(MG)
            act.wait_ge(fin_ss_ready, TT)
            A(st[:, 50:52], st[:, 48:50], ACT.Sqrt, bias=st[:, 63:64], scale=1.0 / D).then_inc(fin_rms_ready, 1)

        @block.vector
        def _(dve):
            v = nc.vector
            step = Steps(dve, v_step)
            v.memset(st[:, 63:64], EPS).then_inc(ss_ready, 1)

            dve.wait_ge(consts_turned, 1)
            v.tensor_scalar(ccol[:, 0, 0:120], bank[7][:, 0:120], 0.5, None, ALU.mult)
            step(v.tensor_copy(ccol[:, 1, 0:42], bank[7][:, 128:170]))
            step(v.tensor_scalar(ccol[:, 1, 24:40], ccol[:, 1, 24:40], 0.5, None, ALU.mult))

            dve.wait_ge(rms_ready, 1)
            step(v.reciprocal(st[:, 2:4], st[:, 2:4]))
            for t in range(TT):
                v.tensor_scalar(xn[:, t, :], x_in[:, t, :], st[:, 2 + t:3 + t], None, ALU.mult).then_inc(xn_ready, 1)
            for j in range(4):
                dve.wait_ge(xn_turned, j + 1)
                for k in (2 * j, 2 * j + 1):
                    c = (k % 2) * 256
                    v.tensor_scalar(hT[:, k, :], bank[2 + j % 2][:, c:c + S], g_mix(k), None, ALU.mult)\
                        .then_inc(hT_ready, 1)

            dve.wait_ge(iota_made, 1)
            step(v.scalar_tensor_tensor(out=dist, in0=dist, scalar=-1.0, in1=dist, op0=ALU.mult, op1=ALU.max))

            dve.wait_ge(vecs_landed, VECS)
            for t in range(TT):
                u = ("small", t)
                wait_unit(dve, u)
                v.tensor_scalar(wi[:, t, :], acc(u)[:, 0:8], IDX_HEADS ** -0.5, None, ALU.mult)
                v.tensor_copy(c_tok[:, t, :], acc(u)[:, 8:264])
                ins = v.tensor_tensor(sp_t[:, 0, t, :], acc(u)[:, 264:296], hvec[:, 0, :], ALU.add)
                took(ins, u)
                dve.wait_ge(unit_taken[unit_no[u] % 2], unit_no[u] // 2 + 1)
                v.tensor_tensor_reduce(out=bias[:, 0:256], in0=c_tok[:, t, :], in1=c_tok[:, t, :], scale=1.0, scalar=0.0,
                                       op0=ALU.mult, op1=ALU.add, accum_out=st[:, 4 + t:5 + t]).then_inc(ckv_ss_ready, 1)
            v.scalar_tensor_tensor(out=sp_t[:, 1, :, :], in0=sp_t[:, 0, :, :], scalar=-1.0, in1=sp_t[:, 0, :, :],
                                   op0=ALU.mult, op1=ALU.max).then_inc(dt_abs_ready, 1)
            dve.wait_ge(ckv_rms_ready, 1)
            step(v.reciprocal(st[:, 6:8], st[:, 6:8]))
            for t in range(TT):
                ins = v.tensor_scalar(c_tok[:, t, :], c_tok[:, t, :], st[:, 6 + t:7 + t], None, ALU.mult)
            ins.then_inc(c_ready, 1)
            dve.wait_ge(dt_exp_ready, 1)
            v.tensor_scalar(sp_t[:, 2, :, :], sp_t[:, 1, :, :], 1.0, None, ALU.add).then_inc(dt_u_ready, 1)
            dve.wait_ge(dt_u_ready, 1)
            step(v.tensor_scalar(dt[:, :, :], sp_t[:, 2, :, :], 1.0, None, ALU.subtract))
            step(v.tensor_tensor(sp_t[:, 1, :, :], sp_t[:, 1, :, :], dt[:, :, :], ALU.subtract))
            step(v.reciprocal(dt[:, :, :], sp_t[:, 2, :, :]))
            step(v.tensor_tensor(sp_t[:, 1, :, :], sp_t[:, 1, :, :], dt[:, :, :], ALU.mult))
            step(v.scalar_tensor_tensor(out=sp_t[:, 1, :, :], in0=sp_t[:, 0, :, :], scalar=0.0, in1=sp_t[:, 1, :, :],
                                        op0=ALU.max, op1=ALU.add))
            dve.wait_ge(dt_ln_ready, 1)
            step(v.tensor_tensor(dt[:, :, :], sp_t[:, 1, :, :], sp_t[:, 3, :, :], ALU.add))
            dve.wait_ge(negA_ready, 1)
            for t in range(TT):
                ins = v.tensor_tensor(dA[:, t, :], dt[:, t, :], hvec[:, 1, :], ALU.mult)
            ins.then_inc(dA_ready, 1)

            score = sel_work
            for h in range(IDX_HEADS):
                dve.wait_ge(relu_ready, h + 1)
                for t, (a, b) in enumerate(KEYS):
                    if h == 0:
                        ins = v.tensor_scalar(score[:, a:b], relu[:, 0, a:b], wi[:, t, 0:1], None, ALU.mult)
                    else:
                        ins = v.scalar_tensor_tensor(out=score[:, a:b], in0=relu[:, h % 2, a:b],
                                                     scalar=wi[:, t, h:h + 1], in1=score[:, a:b],
                                                     op0=ALU.mult, op1=ALU.add)
                ins.then_inc(relu_used, 1)
                dve.wait_ge(relu_used, h + 1)
            v.memset(score[0:64, 64:128], LEAST)
            step(v.memset(score[0:64, 320:384], LEAST))
            for r in range(TOPK // 8):
                for t, (a, b) in enumerate(KEYS):
                    ins = v.max(top8[:, t, :], score[:, a:b])
                step(ins)
                for t, (a, b) in enumerate(KEYS):
                    ins = v.match_replace(score[:, a:b], top8[:, t, :], score[:, a:b], TAKEN)
                step(ins)
            step(v.tensor_scalar(unsel, score, TAKEN / 1.5, LEAST, ALU.is_gt, ALU.mult))

            def scale_prob(h):
                dve.wait_ge(exp_ready, 2 * h + 2)
                c = 16 + 2 * (h % 2)
                step(v.reciprocal(st[:, c:c + 2], st[:, c:c + 2]))
                for t, (a, b) in enumerate(KEYS):
                    ins = v.tensor_scalar(prob[:, h % 2, a:b], prob[:, h % 2, a:b], st[:, c + t:c + t + 1], None, ALU.mult)
                ins.then_inc(prob_ready, 1)

            def silu_of(i):
                m = CONV_ORDER[i]
                dve.wait_ge(tanh_ready, i + 1)
                v.scalar_tensor_tensor(out=xcT[:, m, :], in0=th[:, i % 2, 0:S], scalar=1.0, in1=xcT[:, m, :],
                                       op0=ALU.add, op1=ALU.mult).then_inc(xc_ready, 1)

            for i in range(25):
                if 1 <= i <= ATT_HEADS:
                    scale_prob(i - 1)
                if i < ATT_HEADS:
                    slope = 2.0 ** (-8.0 * (i + 1) / ATT_HEADS)
                    step(v.scalar_tensor_tensor(out=bias, in0=dist, scalar=-slope, in1=unsel, op0=ALU.mult, op1=ALU.add))
                if i < 24:
                    m = CONV_ORDER[i]
                    u = ("xbc", i)
                    dve.wait_ge(first_tap_ready, i + 1)
                    for d in range(1, TAPS):
                        ins = v.scalar_tensor_tensor(out=xcT[:, m, d:S], in0=acc(u)[:, 0:S - d], scalar=tap(3 - d, m),
                                                     in1=xcT[:, m, d:S], op0=ALU.mult, op1=ALU.add)
                        if d < TAPS - 1:
                            step(ins)
                    took(ins, u)
                    dve.wait_ge(unit_taken[unit_no[u] % 2], unit_no[u] // 2 + 1)
                    dve.sem_inc(conv_ready, 1)
                if i < ATT_HEADS:
                    dve.wait_ge(logits_done, i + 1)
                    if i >= 2:
                        dve.wait_ge(prob_turned, i - 1)
                    for t, (a, b) in enumerate(KEYS):
                        c = 8 + 2 * (i % 2) + t
                        ins = v.tensor_tensor_reduce(out=prob[:, i % 2, a:b], in0=bank[2 + i % 2][:, a:b], in1=bias[:, a:b],
                                                     scale=-1.0, scalar=3e38, op0=ALU.add, op1=ALU.min,
                                                     accum_out=st[:, c:c + 1])
                    ins.then_inc(att_biased, 1)
                if i >= 1:
                    silu_of(i - 1)

            def bcast(a, n):
                return a.unsqueeze(2).to_broadcast([P, HPG, n])

            def make_seg_in(q):
                c, g = q // GROUPS, q % GROUPS
                v.tensor_tensor(seg_in.rearrange("p (h l) -> p h l", h=HPG),
                                tri[:, :].unsqueeze(1).to_broadcast([P, HPG, P]),
                                bcast(dA[:, c, g * HPG:(g + 1) * HPG], P), ALU.mult).then_inc(seg_in_ready, 1)

            dve.wait_ge(attT_ready, ATT_HEADS)
            make_seg_in(0)
            for q in range(8):
                c, g = q // GROUPS, q % GROUPS
                hs = slice(g * HPG, (g + 1) * HPG)
                cols = slice(g * 512, (g + 1) * 512)
                src = bank[5][:, :].rearrange("p (h d) -> p h d", h=HPG)
                dve.wait_ge(xs_turned, q + 1)
                if q == 0:
                    dve.wait_ge(eacs_ready, 1)
                v.tensor_tensor(y[:, c, cols].rearrange("p (h d) -> p h d", h=HPG), src, bcast(hvec[:, 2, hs], HD), ALU.mult)
                v.tensor_tensor(xdt3[:, c, cols].rearrange("p (h d) -> p h d", h=HPG), src, bcast(dt[:, c, hs], HD), ALU.mult)\
                    .then_inc(xdt_ready, 1)
                dve.wait_ge(xdt_ready, q + 1)
                if c == 0:
                    if q >= 1:
                        dve.wait_ge(state_done, q)
                    v.tensor_tensor(xdec.rearrange("p (h d) -> p h d", h=HPG),
                                    xdt3[:, c, cols].rearrange("p (h d) -> p h d", h=HPG), bcast(dec[:, hs], HD), ALU.mult)
                dve.wait_ge(cb_done, q + 1)
                if c == 0:
                    v.tensor_copy(cbm[:, 1, :], bank[4][:, 256:384]).then_inc(b_tok_ready, 1)
                v.tensor_tensor(cbm[:, 0, :], bank[4][:, 0:P], tri[:, :], ALU.mult).then_inc(cb_ready, 1)
                dve.wait_ge(cb_ready, q + 1)
                dve.wait_ge(decay_ready, q + 1)
                v.tensor_tensor(decay.rearrange("p (h l) -> p h l", h=HPG), decay.rearrange("p (h l) -> p h l", h=HPG),
                                cbm[:, 0, :].unsqueeze(1).to_broadcast([P, HPG, P]), ALU.mult).then_inc(wts_ready, 1)
                if q < 7:
                    dve.wait_ge(seg_done, q + 1)
                    make_seg_in(q + 1)
                dve.wait_ge(y_diag_done, q + 1)
                ins = v.tensor_tensor(y[:, c, cols], y[:, c, cols], bank[6][:, :], ALU.add)
                if c == 1:
                    step(ins)
                    dve.wait_ge(y_off_done, g + 1)
                    step(v.tensor_tensor(y_off.rearrange("p (h d) -> p h d", h=HPG),
                                         bank[7][:, :].rearrange("p (h d) -> p h d", h=HPG),
                                         bcast(eacs[:, c, hs], HD), ALU.mult))
                    ins = v.tensor_tensor(y[:, c, cols], y[:, c, cols], y_off, ALU.add)
                ins.then_inc(y_ready, 1)
            dve.wait_ge(y_ready, 8)

            for n in range(8):
                g, t = n // 2, n % 2
                cols = slice(g * 512, (g + 1) * 512)
                u = ("z", n)
                dve.wait_ge(z_tanh_ready, n + 1)
                ins = v.scalar_tensor_tensor(out=th[:, n % 2, :], in0=th[:, n % 2, :], scalar=1.0, in1=acc(u)[:, :],
                                             op0=ALU.add, op1=ALU.mult)
                took(ins, u)
                dve.wait_ge(unit_taken[unit_no[u] % 2], unit_no[u] // 2 + 1)
                v.scalar_tensor_tensor(out=y[:, t, cols], in0=th[:, n % 2, :], scalar=0.5, in1=y[:, t, cols],
                                       op0=ALU.mult, op1=ALU.mult).then_inc(y_gated, 1)
            dve.wait_ge(y_rms_ready, 1)
            step(v.reciprocal(st[:, 32:40], st[:, 32:40]))
            for n in range(8):
                g, t = n // 2, n % 2
                v.tensor_scalar(y[:, t, g * 512:(g + 1) * 512], y[:, t, g * 512:(g + 1) * 512], st[:, 32 + n:33 + n],
                                None, ALU.mult).then_inc(y_normed, 1)

            dve.wait_ge(gate_ready, 16)
            for m in range(8):
                u = ("att", m)
                wait_unit(dve, u)
                took(v.tensor_tensor(gT[:, 8 + m, :], acc(u)[:, 0:S], gT[:, 8 + m, :], ALU.mult), u)
            for m in range(8):
                u = ("ssm", m)
                wait_unit(dve, u)
                took(v.tensor_tensor(th[:, m % 2, 0:S], acc(u)[:, 0:S], gT[:, m, :], ALU.mult), u)
                dve.wait_ge(unit_taken[unit_no[u] % 2], unit_no[u] // 2 + 1)
                v.tensor_tensor(mixT[:, m, :], th[:, m % 2, 0:S], gT[:, 8 + m, :], ALU.add).then_inc(mix_ready, 1)
            dve.wait_ge(x_again_landed, 32)
            for n in range(4):
                half, t = n // 2, n % 2
                u = ("out", n)
                wait_unit(dve, u)
                cols = slice(half * 512, (half + 1) * 512)
                ins = v.tensor_tensor(x2[:, t, cols], acc(u)[:, :], x_again[:, t, cols], ALU.add)
                took(ins, u)
                dve.wait_ge(unit_taken[unit_no[u] % 2], unit_no[u] // 2 + 1)
                dve.sem_inc(x2_ready, 1)

            dve.wait_ge(x2_rms_ready, 1)
            step(v.reciprocal(st[:, 42:44], st[:, 42:44]))
            for t in range(TT):
                v.tensor_scalar(h2[:, t, :], x2[:, t, :], st[:, 42 + t:43 + t], None, ALU.mult).then_inc(h2_ready, 1)
            for j in range(4):
                dve.wait_ge(h2_turned, j + 1)
                for k in (2 * j, 2 * j + 1):
                    c = (k % 2) * 256
                    v.tensor_scalar(h2T[:, k, :], bank[2 + j % 2][:, c:c + S], g_ffn[:, k:k + 1], None, ALU.mult)\
                        .then_inc(h2T_ready, 1)

            T4 = lambda a, n=MG: rt[:, a:a + TT * n].rearrange("p (t n) -> p t n", t=TT)
            small2 = lambda a: rt[:, a:a + TT]
            per = lambda a, n: a.unsqueeze(2).to_broadcast([P, TT, n])
            rev = rt[:, 400:432]
            step(v.tensor_scalar(rev, iota[:, 0:32], -1.0, 32.0, ALU.mult, ALU.add))

            def largest(dst, vals, n, mx, best):
                step(v.tensor_reduce(mx, vals, AX.X, ALU.max))
                step(v.tensor_tensor(dst, vals, per(mx, n), ALU.is_equal))
                step(v.tensor_tensor(dst, dst, rev[:, 0:n].unsqueeze(1).to_broadcast([P, TT, n]), ALU.mult))
                step(v.tensor_reduce(best, dst, AX.X, ALU.max))
                step(v.tensor_tensor(dst, dst, per(best, n), ALU.is_equal))

            oh, ge, gl, el, oh1, oh2, scr, gate = T4(0), T4(16), T4(32), T4(64, 32), T4(128, 32), T4(192, 32), T4(256, 32), T4(320, 32)
            dve.wait_ge(route_done, 1)
            lg = bank[7][:, 0:256].rearrange("p (t c) -> p t c", t=TT)
            v.tensor_tensor(gl, lg[:, :, 0:MG], b_route[:, 0:MG].unsqueeze(1).to_broadcast([P, TT, MG]), ALU.add)
            step(v.tensor_tensor(el, lg[:, :, 64:96], b_route[:, MG:].unsqueeze(1).to_broadcast([P, TT, 32]), ALU.add))
            largest(oh, gl, MG, small2(482), small2(484))
            dve.sem_inc(onehot_ready, 1)
            step(v.tensor_tensor(ge, gl, per(small2(482), MG), ALU.subtract))
            step(v.tensor_scalar(gl, oh, 1.0, -LEAST, ALU.subtract, ALU.mult))
            for t in range(TT):
                ins = v.tensor_tensor(el[:, t, :].rearrange("p (g e) -> p g e", g=MG), el[:, t, :].rearrange("p (g e) -> p g e", g=MG),
                                      gl[:, t, :].unsqueeze(2).to_broadcast([P, MG, ME]), ALU.add)
            step(ins)
            largest(oh1, el, 32, small2(486), small2(488))
            step(v.scalar_tensor_tensor(out=el, in0=oh1, scalar=LEAST, in1=el, op0=ALU.mult, op1=ALU.add))
            largest(oh2, el, 32, small2(490), small2(492))
            step(v.tensor_tensor(small2(480), small2(490), small2(486), ALU.subtract))
            dve.sem_inc(route_in, 1)
            dve.wait_ge(route_exp, 1)
            step(v.tensor_reduce(small2(494), ge, AX.X, ALU.add))
            step(v.scalar_tensor_tensor(out=small2(494), in0=small2(480), scalar=1.0, in1=small2(494), op0=ALU.add, op1=ALU.mult))
            step(v.reciprocal(small2(494), small2(494)))
            step(v.tensor_tensor(small2(496), small2(494), small2(480), ALU.mult))
            step(v.tensor_tensor(gate, oh1, per(small2(494), 32), ALU.mult))
            step(v.tensor_tensor(scr, oh2, per(small2(496), 32), ALU.mult))
            step(v.tensor_tensor(gate, gate, scr, ALU.add))
            dve.wait_ge(rank_done, 1)
            rank = T4(440)
            v.tensor_copy(rank, bank[6][:, 0:16].rearrange("p (t c) -> p t c", t=TT)[:, :, 0:MG])
            step(v.tensor_scalar(rt[:, 452:456], bank[6][:, 16:16 + MG], float(P), None, ALU.is_gt))
            v.tensor_reduce(rt[:, 456:457], rt[:, 452:456], AX.X, ALU.add)
            step(v.tensor_tensor(rt[:, 460:464], rt[:, 452:456], iota[:, 0:MG], ALU.mult))
            step(v.tensor_reduce(rt[:, 457:458], rt[:, 460:464], AX.X, ALU.add))
            v.tensor_copy(n_over_i[:, :], rt[:, 456:458]).then_inc(route_ready, 1)
            for t in range(TT):
                for g in range(MG):
                    ins = v.tensor_scalar(perm[:, t, g, :], iota[:, :], rank[:, t, g:g + 1], oh[:, t, g:g + 1],
                                          ALU.is_equal, ALU.mult)
            step(ins)

            def group_pass(it):
                dve.wait_ge(gathered, it * 2 + 2)
                for k in range(4, KD):
                    ins = v.tensor_scalar(xgT[:, k, :], bank[4][:, (k - 4) * P:(k - 3) * P], g_ffn[:, k:k + 1], None, ALU.mult)
                ins.then_inc(xgT_ready_v, 1)
                dve.wait_ge(places_ready, it + 1)
                for e in range(ME):
                    dve.wait_ge(silu_ready, it * ME + (e + 1))
                    if e >= 2:
                        dve.wait_ge(hid_turned, it * ME + (e - 1))
                    v.scalar_tensor_tensor(out=hid[:, e % 2, :], in0=bank[e % 2][:, FF:2 * FF], scalar=gate_g[:, e:e + 1],
                                           in1=sil[:, e % 2, :], op0=ALU.mult, op1=ALU.mult).then_inc(hid_ready, 1)
                for n in range(4):
                    t, half = n // 2, n % 2
                    cols = slice(half * 512, (half + 1) * 512)
                    dve.wait_ge(scattered, it * 4 + (n + 1))
                    v.tensor_tensor(x2[:, t, cols], x2[:, t, cols], bank[3 + half][:, :], ALU.add).then_inc(added, 1)

            with dve.Fori(0, MG) as it:
                v.tensor_copy(perm_cur, perm.rearrange("p t g s -> p t (g s)")[:, :, bass.ds(it * P, P)]).then_inc(perm_copied, 1)
                v.tensor_copy(gate_cur, gate[:, :, bass.ds(it * ME, ME)])\
                    .then_inc(perm_ready, 1)
                group_pass(it)
            over = dve.value_load(n_over_i[0:1, 0:1], min_val=0, max_val=1)
            with dve.If(over):
                sel4 = rt[:, 452:456]
                both = lambda: sel4.unsqueeze(1).to_broadcast([P, TT, MG])
                step(v.tensor_tensor(T4(460), oh, both(), ALU.mult))
                step(v.tensor_reduce(small2(470), T4(460), AX.X, ALU.add))
                step(v.tensor_tensor(T4(460), T4(460), rank, ALU.mult))
                step(v.tensor_reduce(small2(472), T4(460), AX.X, ALU.add))
                step(v.tensor_scalar(small2(472), small2(472), float(P), None, ALU.subtract))
                for t in range(TT):
                    v.tensor_scalar(perm_cur[:, t, :], iota[:, :], rt[:, 472 + t:473 + t], rt[:, 470 + t:471 + t],
                                    ALU.is_equal, ALU.mult)
                    step(v.tensor_scalar(gate_cur[:, t, :], gate[:, t, 0:ME], sel4[:, 0:1], None, ALU.mult))
                    for g in range(1, MG):
                        ins = v.scalar_tensor_tensor(out=gate_cur[:, t, :], in0=gate[:, t, g * ME:(g + 1) * ME],
                                                     scalar=sel4[:, g:g + 1], in1=gate_cur[:, t, :],
                                                     op0=ALU.mult, op1=ALU.add)
                        step(ins)
                dve.sem_inc(perm_ready, 1)
                group_pass(MG)
                dve.wait_ge(added, 4 * (MG + 1))

            dve.wait_ge(added, 4 * MG)
            for t in range(TT):
                v.tensor_tensor_reduce(out=h2[:, t, :], in0=x2[:, t, :], in1=x2[:, t, :], scale=1.0, scalar=0.0,
                                       op0=ALU.mult, op1=ALU.add, accum_out=st[:, 48 + t:49 + t]).then_inc(fin_ss_ready, 1)
            dve.wait_ge(fin_rms_ready, 1)
            dve.wait_ge(fin_ss_ready, TT)
            v.reciprocal(st[:, 50:52], st[:, 50:52]).then_inc(fin_rms_ready, 1)
            dve.wait_ge(fin_rms_ready, 2)
            dve.wait_ge(g_fin_landed, 16)
            for t in range(TT):
                v.scalar_tensor_tensor(out=x2[:, t, :], in0=x2[:, t, :], scalar=st[:, 50 + t:51 + t], in1=g_fin,
                                       op0=ALU.mult, op1=ALU.mult).then_inc(out_ready, 1)


_INS = ['x', 'norm_mix_g', 'w_in', 'conv_w', 'conv_b', 'dt_bias', 'a_log', 'd_skip', 'ssm_norm_g', 'kv_norm_g',
        'w_uk', 'w_uv', 'gate_b', 'w_branch_ssm', 'w_branch_att', 'w_out', 'norm_ffn_g', 'w_group', 'b_group',
        'w_router', 'b_router', 'w_e1', 'w_e3', 'w_e2', 'norm_final_g']


def kernel(**inputs):
    import numpy as _np
    import concourse.bacc as _bacc
    from concourse import mybir as _mybir
    from concourse.bass_utils import run_bass_kernel_spmd as _run

    nc = _bacc.Bacc("TRN2", target_bir_lowering=False, num_devices=1)
    arrays, args = {}, []
    for name in _INS:
        a = _np.ascontiguousarray(inputs[name])
        arrays[f"in_{name}_dram"] = a
        args.append(nc.dram_tensor(f"in_{name}_dram", a.shape, _mybir.dt.from_np(a.dtype), kind="ExternalInput").ap())
    args.append(nc.dram_tensor("out_dram", (1, S, D), F32, kind="ExternalOutput").ap())
    hybrid_block(nc, *args)
    r = _run(nc, [arrays], core_ids=[0])
    return r.results[0]["out_dram"]
```

```python
from contextlib import ExitStack

import concourse.bass as bass
from concourse import mybir

F32 = mybir.dt.float32
I32 = mybir.dt.int32
ALU = mybir.AluOpType
ACT = mybir.ActivationFunctionType
AX = mybir.AxisListType

P = 128
D = 1024
S = 256
TT = S // P
KD = D // P
EPS = 1e-6
D_INNER = 2 * D
HEADS = 32
HD = 64
GROUPS = 4
HPG = HEADS // GROUPS
XBC = D_INNER + 2 * GROUPS * P
TAPS = 4
ATT_HEADS = 16
LATENT = 256
IDX_HEADS = 8
TOPK = 64
MG = 4
ME = 8
FF = 256
LEAST = -1e30
TAKEN = -3e38

C_Z = 0
C_XBC = C_Z + D_INNER
C_DT = C_XBC + XBC
C_Q = C_DT + HEADS
C_CKV = C_Q + ATT_HEADS * HD
C_QI = C_CKV + LATENT
C_KI = C_QI + IDX_HEADS * HD
C_WI = C_KI + HD
C_GATE = C_WI + IDX_HEADS

N_SMALL = IDX_HEADS + LATENT + HEADS
SLOT = 4096
NSLOTS = 5
EB = 4
PLACES = P // EB
BATCHES = MG * ME // EB
CHUNKS = 6
MAX_OVER = 16
CONV_ORDER = list(range(16, 24)) + list(range(16))


def hybrid_block(nc, x, norm_mix_g, w_in, conv_w, conv_b, dt_bias, a_log, d_skip, ssm_norm_g,
                 kv_norm_g, w_uk, w_uv, gate_b, w_branch_ssm, w_branch_att, w_out, norm_ffn_g,
                 w_group, b_group, w_router, b_router, w_e1, w_e3, w_e2, norm_final_g, out):
    ctx = ExitStack()
    with ctx:
        def sb(name, shape, dt=F32):
            return ctx.enter_context(nc.sbuf_tensor(name, shape, dt))

        def sem(name):
            return ctx.enter_context(nc.semaphore(name))

        ring = sb("ring", [P, NSLOTS * SLOT])
        hT = sb("hT", [P, KD, S])
        xcT = sb("xcT", [P, 24, S])
        xs = sb("xs", [P, TT * D_INNER])
        xdt = sb("xdt", [P, TT * D_INNER])
        kv = sb("kv", [P, 16, S])
        qT = sb("qT", [P, 8, S])
        work = sb("work", [P, 5120])
        ident = sb("ident", [P, P])
        tri = sb("tri", [P, P])
        below = sb("below", [P, P])
        above = sb("above", [P, P])
        ones = sb("ones", [P, P])
        iota_i = sb("iota_i", [P, S], I32)
        iota = sb("iota", [P, P])
        crow = sb("crow", [P, 2, P])
        ccol = sb("ccol", [P, 2, P])
        g_ffn = sb("g_ffn", [P, KD])
        hvec = sb("hvec", [P, 3, HEADS])
        b_route = sb("b_route", [P, MG + MG * ME])
        w_grp = sb("w_grp", [P, KD, MG])
        w_rt = sb("w_rt", [P, MG, KD, ME])
        st = sb("st", [P, 64])
        sp_t = sb("sp_t", [P, 4, TT, HEADS])
        dt = sb("dt", [P, TT, HEADS])
        dA = sb("dA", [P, TT, HEADS])
        eacs = sb("eacs", [P, TT, HEADS])
        dec = sb("dec", [P, HEADS])
        rt = sb("rt", [P, 1024])
        wi = sb("wi", [P, TT, IDX_HEADS])
        top8 = sb("top8", [P, TT, 8])
        n_over_i = sb("n_over_i", [P, 2], I32)

        xn = xdt[:, 0:TT * D].rearrange("p (t d) -> p t d", t=TT)
        x_in = xs[:, 0:TT * D].rearrange("p (t d) -> p t d", t=TT)
        y = xs[:, :].rearrange("p (t d) -> p t d", t=TT)
        xdt3 = xdt[:, :].rearrange("p (t d) -> p t d", t=TT)
        yT = xcT[:, 0:16, :]
        mixT = hT
        kT = kv[:, 0:8, :]
        v_tok = kv[:, 8:16, :].rearrange("p (t a) b -> p t (a b)", t=TT)
        gT = kv
        attT = qT
        qiT = work[:, 0:1024].rearrange("p (m s) -> p m s", m=4)
        kiT = work[:, 1024:1280]
        c_tok = work[:, 1280:1792].rearrange("p (t r) -> p t r", t=TT)
        cT = work[:, 1792:2304].rearrange("p (r s) -> p r s", r=2)
        prob = work[:, 2304:3072].rearrange("p (b s) -> p b s", b=2)
        probT = work[:, 3072:3840].rearrange("p (b s) -> p b s", b=2)
        bias = work[:, 3840:4224]
        dist = work[:, 4224:4608]
        unsel = work[:, 4608:4992]
        stateT = work[:, 0:2048].rearrange("p (g d) -> p g d", g=GROUPS)
        seg_in = work[:, 2048:3072]
        decay = work[:, 3072:4096]
        xdec = work[:, 4096:4608]
        y_off = work[:, 4608:5120]
        th = sb("th", [P, 2, 512])
        cbm = sb("cbm", [P, 2, P])
        sel_work = rt[:, 0:384]
        relu = xs[:, 0:768].rearrange("p (b s) -> p b s", b=2)
        x_again = xdt[:, 0:2048].rearrange("p (t d) -> p t d", t=TT)
        h2T = xdt[:, 2048:4096].rearrange("p (k s) -> p k s", k=KD)
        x2 = xs[:, 0:2048].rearrange("p (t d) -> p t d", t=TT)
        h2 = xs[:, 2048:4096].rearrange("p (t d) -> p t d", t=TT)
        kvf = kv[:, :, :].rearrange("p a b -> p (a b)")
        xgT = kvf[:, 0:1024].rearrange("p (k s) -> p k s", k=KD)
        hid = kvf[:, 1024:1536].rearrange("p (b s) -> p b s", b=2)
        sil = kvf[:, 1536:2048].rearrange("p (b s) -> p b s", b=2)
        hidT = kvf[:, 2048:2560].rearrange("p (b f s) -> p b f s", b=2, f=2)
        y_grp = kvf[:, 2560:3584]
        gateT = kvf[:, 3584:3840].rearrange("p (t s) -> p t s", t=TT)
        hf = hT[:, :, :].rearrange("p a b -> p (a b)")
        perm = hf[:, 0:256].rearrange("p (t s) -> p t s", t=TT)
        pgate = hf[:, 256:512].rearrange("p (t s) -> p t s", t=TT)
        rank1 = hf[:, 512:576].rearrange("p (t e) -> p t e", t=TT)
        flags = hf[:, 576:640]
        before = hf[:, 640:768].rearrange("p (b n) -> p b n", b=2)
        over_at = hf[:, 768:832]
        entry = hf[:, 832:864].rearrange("p (a n) -> p a n", a=2)
        over_now = hf[:, 864:872]
        iota1 = sb("iota1", [P, P])
        iota1x = hf[:, 1024:1280].rearrange("p (t e s) -> p t e s", t=TT, e=EB)
        entry_i = sb("entry_i", [P, MAX_OVER], I32)
        g_fin = xdt[:, 0:D]
        xcf = xcT[:, :, :].rearrange("p a b -> p (a b)")
        cslots = [ring[:, n * SLOT:(n + 1) * SLOT] for n in range(NSLOTS)] + [xcf[:, 0:SLOT]]
        c_up = [c.rearrange("p (w e k f) -> p w e k f", w=2, e=EB, k=2) for c in cslots]
        c_down = [c.rearrange("p (e d) -> p e d", e=EB) for c in cslots]
        o_up = cslots[0].rearrange("p (w k f) -> p w k f", w=2, k=KD)
        o_down = cslots[1][:, 0:2048].rearrange("p (k d) -> p k d", k=2)

        def tap(j, m):
            return ccol[:, 0, j * 24 + m:j * 24 + m + 1]

        def conv_bias(m):
            return ccol[:, 0, 96 + m:97 + m]

        def g_mix(k):
            return ccol[:, 1, k:k + 1]

        def g_ssm(m):
            return ccol[:, 1, 8 + m:9 + m]

        def b_gate(m):
            return ccol[:, 1, 24 + m:25 + m]

        def g_kv(r):
            return ccol[:, 1, 40 + r:41 + r]

        bank = [ctx.enter_context(nc.psum_tensor(f"bank{i}", [P, 512], F32)) for i in range(8)]

        jobs = [("qi",), ("small",), ("q", 0), ("q", 1), ("ukv",)]
        jobs += [("xbc", b) for b in (4, 5, 0, 1, 2, 3)]
        jobs += [("gate", b) for b in range(4)] + [("z", b) for b in range(4)]
        jobs += [("att", b) for b in range(2)] + [("ssm", b) for b in range(4)]
        jobs += [("out", b) for b in range(2)]
        job_no = {j: n for n, j in enumerate(jobs)}
        N_JOBS = len(jobs)

        def slot(job):
            n = job_no[job] % NSLOTS
            return ring[:, n * SLOT:(n + 1) * SLOT]

        def block512(job):
            return slot(job).rearrange("p (k n) -> p k n", k=KD)

        small = slot(("small",))[:, 0:KD * 424].rearrange("p (k n) -> p k n", k=KD)
        w_k = slot(("ukv",))[:, 0:2048].rearrange("p (r n) -> p r n", r=2)
        w_v = slot(("ukv",))[:, 2048:4096].rearrange("p (r n) -> p r n", r=2)
        win = w_in[0].rearrange("(k p) n -> p k n", p=P)

        def loads(job):
            kind = job[0]
            b = block512(job) if kind not in ("small", "ukv", "ssm") else None
            if kind == "small":
                return [(small[:, :, 0:64], win[:, :, C_KI:C_KI + 64]),
                        (small[:, :, 64:136], win[:, :, C_KI:C_KI + 72]),
                        (small[:, :, 136:392], win[:, :, C_CKV:C_CKV + LATENT]),
                        (small[:, :, 392:424], win[:, :, C_DT:C_DT + HEADS])]
            if kind == "ukv":
                res = []
                for dst, src in ((w_k, w_uk), (w_v, w_uv)):
                    for r in range(2):
                        res.append((dst[:, r, :].rearrange("p (h d) -> p h d", d=HD),
                                    src[0, :, r * P:(r + 1) * P, :].rearrange("h p d -> p h d")))
                return res
            if kind == "ssm":
                n = job[1]
                return [(slot(job).rearrange("p (k n) -> p k n", k=16),
                         w_branch_ssm[0].rearrange("(k p) n -> p k n", p=P)[:, :, n * 256:(n + 1) * 256])]
            if kind in ("att", "out"):
                w = (w_branch_att if kind == "att" else w_out)[0].rearrange("(k p) n -> p k n", p=P)
                return [(b, w[:, :, job[1] * 512:(job[1] + 1) * 512])]
            c = {"qi": C_QI, "q": C_Q, "xbc": C_XBC, "gate": C_GATE, "z": C_Z}[kind]
            c += 512 * (job[1] if len(job) > 1 else 0)
            return [(b, win[:, :, c:c + 512])]

        landed_at, per_slot = {}, [0] * NSLOTS
        for n, j in enumerate(jobs):
            per_slot[n % NSLOTS] += 16 * len(loads(j))
            landed_at[j] = per_slot[n % NSLOTS]

        units = [("qi", m) for m in range(4)] + [("ki", 0)] + [("small", t) for t in range(2)]
        units += [("q", m) for m in range(8)] + [("k", m) for m in range(8)]
        units += [("v", n) for n in range(4)] + [("xbc", i) for i in range(24)]
        units += [("gate", m) for m in range(16)] + [("z", n) for n in range(8)]
        units += [("att", m) for m in range(8)] + [("ssm", m) for m in range(8)]
        units += [("out", n) for n in range(4)]
        unit_no = {u: n for n, u in enumerate(units)}
        units_per_bank = [0, 0]
        for n in range(len(units)):
            units_per_bank[n % 2] += 1

        last_unit = {("qi",): ("qi", 3), ("small",): ("small", 1), ("ukv",): ("v", 3)}
        for n in range(4):
            last_unit[("gate", n)] = ("gate", 4 * n + 3)
            last_unit[("z", n)] = ("z", 2 * n + 1)
            last_unit[("ssm", n)] = ("ssm", 2 * n + 1)
        for n in range(2):
            last_unit[("q", n)] = ("q", 4 * n + 3)
            last_unit[("att", n)] = ("att", 4 * n + 3)
            last_unit[("out", n)] = ("out", 2 * n + 1)
        for i in range(3, 24, 4):
            last_unit[("xbc", CONV_ORDER[i] // 4)] = ("xbc", i)
        units_until = [unit_no[last_unit[j]] + 1 for j in jobs]

        def acc(u):
            return bank[unit_no[u] % 2]

        block_landed = [sem(f"block_landed{i}") for i in range(NSLOTS)]
        x_landed = sem("x_landed")
        rows_landed = sem("rows_landed")
        vecs_landed = sem("vecs_landed")
        g_fin_landed = sem("g_fin_landed")
        x_again_landed = sem("x_again_landed")
        masks_ready = sem("masks_ready")
        iota_made = sem("iota_made")
        consts_turned = sem("consts_turned")
        consts_ready = sem("consts_ready")
        ss_ready = sem("ss_ready")
        rms_ready = sem("rms_ready")
        xn_ready = sem("xn_ready")
        xn_turned = sem("xn_turned")
        hT_ready = sem("hT_ready")
        unit_done = sem("unit_done")
        unit_taken = [sem("unit_taken0"), sem("unit_taken1")]
        negA_ready = sem("negA_ready")
        ckv_ss_ready = sem("ckv_ss_ready")
        ckv_rms_ready = sem("ckv_rms_ready")
        c_ready = sem("c_ready")
        c_turned = sem("c_turned")
        cT_ready = sem("cT_ready")
        dt_abs_ready = sem("dt_abs_ready")
        dt_exp_ready = sem("dt_exp_ready")
        dt_u_ready = sem("dt_u_ready")
        dt_ln_ready = sem("dt_ln_ready")
        dA_ready = sem("dA_ready")
        acs_done = sem("acs_done")
        eacs_ready = sem("eacs_ready")
        index_done = sem("index_done")
        relu_ready = sem("relu_ready")
        relu_used = sem("relu_used")
        sel_ready = sem("sel_ready")
        logits_done = sem("logits_done")
        att_biased = sem("att_biased")
        exp_ready = sem("exp_ready")
        prob_ready = sem("prob_ready")
        prob_turned = sem("prob_turned")
        probT_ready = sem("probT_ready")
        pv_done = sem("pv_done")
        attT_ready = sem("attT_ready")
        first_tap_ready = sem("first_tap_ready")
        conv_ready = sem("conv_ready")
        tanh_ready = sem("tanh_ready")
        xc_ready = sem("xc_ready")
        gate_ready = sem("gate_ready")
        seg_in_ready = sem("seg_in_ready")
        seg_done = sem("seg_done")
        xs_turned = sem("xs_turned")
        xdt_ready = sem("xdt_ready")
        cb_done = sem("cb_done")
        cb_ready = sem("cb_ready")
        b_tok_ready = sem("b_tok_ready")
        decay_ready = sem("decay_ready")
        wts_ready = sem("wts_ready")
        y_diag_done = sem("y_diag_done")
        state_done = sem("state_done")
        state_ready = sem("state_ready")
        y_off_done = sem("y_off_done")
        y_ready = sem("y_ready")
        z_tanh_ready = sem("z_tanh_ready")
        y_gated = sem("y_gated")
        y_ss_ready = sem("y_ss_ready")
        y_rms_ready = sem("y_rms_ready")
        y_normed = sem("y_normed")
        y_turned = sem("y_turned")
        yT_ready = sem("yT_ready")
        mix_ready = sem("mix_ready")
        x2_ready = sem("x2_ready")
        x2_ss_ready = sem("x2_ss_ready")
        x2_rms_ready = sem("x2_rms_ready")
        h2_ready = sem("h2_ready")
        h2_turned = sem("h2_turned")
        h2T_ready = sem("h2T_ready")
        route_done = sem("route_done")
        route_in = sem("route_in")
        route_exp = sem("route_exp")
        onehot_ready = sem("onehot_ready")
        rank_done = sem("rank_done")
        route_ready = sem("route_ready")
        chunk_landed = [sem(f"chunk_landed{i}") for i in range(CHUNKS)]
        chunk_used = sem("chunk_used")
        over_turn = sem("over_turn")
        over_picked = sem("over_picked")
        over_up_landed = sem("over_up_landed")
        over_down_landed = sem("over_down_landed")
        perm_ready = sem("perm_ready")
        gathered = sem("gathered")
        places_done = sem("places_done")
        xgT_ready_a = sem("xgT_ready_a")
        xgT_ready_v = sem("xgT_ready_v")
        silu_ready = sem("silu_ready")
        hid_ready = sem("hid_ready")
        hid_turned = sem("hid_turned")
        hidT_ready = sem("hidT_ready")
        y_grp_ready = sem("y_grp_ready")
        scattered = sem("scattered")
        added = sem("added")
        fin_ss_ready = sem("fin_ss_ready")
        fin_rms_ready = sem("fin_rms_ready")
        out_ready = sem("out_ready")
        out_stored = sem("out_stored")
        v_step = sem("v_step")
        a_step = sem("a_step")
        p_step = sem("p_step")

        class Steps:

            def __init__(self, eng, own):
                self.eng, self.own, self.n = eng, own, 0

            def __call__(self, ins):
                self.n += 1
                ins.then_inc(self.own, 1)
                self.eng.wait_ge(self.own, self.n)

        def wait_unit(eng, u):
            eng.wait_ge(unit_done, unit_no[u] + 1)

        def took(ins, u):
            ins.then_inc(unit_taken[unit_no[u] % 2], 1)

        KEYS = [(0, 128), (128, 384)]
        e1_v = w_e1[0].rearrange("g e (p k) f -> (g e) p k f", k=KD)
        e3_v = w_e3[0].rearrange("g e (p k) f -> (g e) p k f", k=KD)
        e2_v = w_e2[0].rearrange("g e (k p) d -> (g e) p k d", p=P)

        def up_used(i):
            return i * CHUNKS + 4

        def down_used(i):
            return i * CHUNKS + CHUNKS

        N_BATCH = BATCHES * CHUNKS

        def over_up_used(r):
            return r * 2 + (N_BATCH + 1)

        def over_down_used(r):
            return r * 2 + (N_BATCH + 2)

        block = ctx.enter_context(nc.Block())

        @block.sync
        def _(sp):
            for t in range(TT):
                sp.dma_start(x_in[:, t, :], x[0, t * P:(t + 1) * P, :]).then_inc(x_landed, 16)
            for n, job in enumerate(jobs):
                if n >= NSLOTS:
                    sp.wait_ge(unit_done, units_until[n - NSLOTS])
                for dst, src in loads(job):
                    sp.dma_start(dst, src).then_inc(block_landed[n % NSLOTS], 16)

            def load_chunk(b, c):
                four = bass.ds(b * EB, EB)
                if c < 4:
                    for w, src in ((0, e1_v), (1, e3_v)):
                        sp.dma_start(c_up[c][:, w, :, :, :].rearrange("p e k f -> p e (k f)"),
                                     src[four, :, 2 * c:2 * c + 2, :].rearrange("e p k f -> p e (k f)"))\
                            .then_inc(chunk_landed[c], 16)
                else:
                    sp.dma_start(c_down[c], e2_v[four, :, c - 4, :].rearrange("e p d -> p e d"))\
                        .then_inc(chunk_landed[c], 16)

            ssm_last = N_JOBS - 3
            for c in [(N_JOBS + i) % NSLOTS for i in range(NSLOTS)]:
                sp.wait_ge(unit_done, units_until[max(n for n in range(N_JOBS) if n % NSLOTS == c)])
                load_chunk(0, c)
                if c == ssm_last % NSLOTS:
                    load_chunk(0, 5)
            with sp.Fori(0, BATCHES - 1) as b:
                for c in range(CHUNKS):
                    sp.wait_ge(chunk_used, b * CHUNKS + (c + 1))
                    load_chunk(b + 1, c)
            sp.wait_ge(route_ready, 1)
            over = sp.value_load(n_over_i[0:1, 0:1], min_val=0, max_val=MAX_OVER)
            with sp.If(over):
                with sp.Fori(0, over) as r:
                    ex = sp.value_load(entry_i[0:1, bass.ds(r, 1)], min_val=0, max_val=MG * ME - 1)
                    sp.wait_ge(chunk_used, (BATCHES - 1) * CHUNKS + 2)
                    sp.wait_ge(over_turn, r + 1)
                    for w, src in ((0, e1_v), (1, e3_v)):
                        sp.dma_start(o_up[:, w, :, :], src[bass.ds(ex, 1)].rearrange("o p k f -> p (o k) f"))\
                            .then_inc(over_up_landed, 16)
                    sp.dma_start(o_down, e2_v[bass.ds(ex, 1)].rearrange("o p k d -> p (o k) d"))\
                        .then_inc(over_down_landed, 16)
            for t in range(TT):
                sp.wait_ge(out_ready, t + 1)
                sp.dma_start(out[0, t * P:(t + 1) * P, :], x2[:, t, :]).then_inc(out_stored, 16)
            sp.wait_ge(out_stored, 16 * TT)

        @block.gpsimd
        def _(pool):
            pool.memset(ones[:, :], 1.0).then_inc(masks_ready, 1)
            for m in (ident, tri, below, above):
                pool.memset(m[:, :], 0.0 if m is ident else 1.0).then_inc(p_step, 1)
            pool.wait_ge(p_step, 4)
            for m, cmp, fill, mult, step in ((ident, ALU.not_equal, 1.0, 1, -1), (tri, ALU.is_ge, 0.0, -1, 1),
                                             (below, ALU.is_gt, 0.0, 1, -1), (above, ALU.is_gt, 0.0, -1, 1)):
                pool.affine_select(out=m[:, :], in_=m[:, :], compare_op=cmp, fill=fill, base=0,
                                   pattern=[[step, P]], channel_multiplier=mult).then_inc(masks_ready, 1)
            for dst, base, mult, n in ((dist[:, 0:128], 0, 1, P), (dist[:, 128:384], P, 1, S)):
                pool.iota(iota_i[:, 0:n], pattern=[[-1, n]], base=base, channel_multiplier=mult).then_inc(p_step, 1)
                pool.wait_ge(p_step, 5 if n == P else 7)
                pool.tensor_copy(dst, iota_i[:, 0:n]).then_inc(p_step, 1)
                pool.wait_ge(p_step, 6 if n == P else 8)
            pool.iota(iota_i[:, 0:P], pattern=[[1, P]], base=0, channel_multiplier=0).then_inc(p_step, 1)
            pool.wait_ge(p_step, 9)
            pool.tensor_copy(iota[:, :], iota_i[:, 0:P]).then_inc(iota_made, 1)
            row = lambda a, n: a.rearrange("(o n) -> o n", o=1).to_broadcast([P, n])
            for m in range(16):
                i = unit_no[("gate", m)]
                pool.wait_ge(unit_taken[i % 2], i // 2 + 1)
                pool.tensor_scalar(gT[:, m, :], gT[:, m, :], 1.0, 0.5, ALU.add, ALU.mult).then_inc(gate_ready, 1)
            pool.wait_ge(y_ready, 8)
            for t in range(TT):
                pool.dma_start(x_again[:, t, :], x[0, t * P:(t + 1) * P, :]).then_inc(x_again_landed, 16)
            pool.wait_ge(x_again_landed, 32)
            pool.wait_ge(x2_ready, 4)
            pool.dma_start(g_fin, row(norm_final_g, D)).then_inc(g_fin_landed, 16)
        VECS = 16 * 8

        @block.tensor
        def _(pe):
            def unit(u, pairs, n, m=P):
                i = unit_no[u]
                if i >= 2:
                    pe.wait_ge(unit_taken[i % 2], i // 2)
                for k, (lhsT, rhs) in enumerate(pairs):
                    mm = pe.matmul(bank[i % 2][0:m, 0:n], lhsT, rhs, start=(k == 0), stop=(k == len(pairs) - 1))
                mm.then_inc(unit_done, 1)
                return mm

            def landed(job):
                pe.wait_ge(block_landed[job_no[job] % NSLOTS], landed_at[job])

            pe.wait_ge(masks_ready, 5)
            pe.wait_ge(rows_landed, 16 * 6)
            pe.transpose(bank[7][:, 0:120], crow[0:120, 0, :], ident[0:120, 0:120])
            pe.transpose(bank[7][:, 128:170], crow[0:42, 1, :], ident[0:42, 0:42]).then_inc(consts_turned, 1)
            for j in range(4):
                pe.wait_ge(xn_ready, TT)
                if j >= 2:
                    pe.wait_ge(hT_ready, 2 * (j - 1))
                for k in (2 * j, 2 * j + 1):
                    for t in range(TT):
                        c = (k % 2) * 256 + t * P
                        tr = pe.transpose(bank[2 + j % 2][:, c:c + P], xn[:, t, k * P:(k + 1) * P], ident[:, :])
                tr.then_inc(xn_turned, 1)
            pe.wait_ge(hT_ready, KD)

            def channel_unit(u, w, c):
                unit(u, [(w[:, k, c:c + P], hT[:, k, :]) for k in range(KD)], S)

            landed(("qi",))
            for m in range(4):
                channel_unit(("qi", m), block512(("qi",)), m * P)
            landed(("small",))
            channel_unit(("ki", 0), small, 0)
            for t in range(TT):
                mm = unit(("small", t), [(hT[:, k, t * P:(t + 1) * P], small[:, k, P:P + N_SMALL])
                                         for k in range(KD)], N_SMALL)
            for m in range(8):
                if m % 4 == 0:
                    landed(("q", m // 4))
                channel_unit(("q", m), block512(("q", m // 4)), m % 4 * P)

            pe.wait_ge(dA_ready, 1)
            for t in range(TT):
                pe.matmul(bank[7][:, t * HEADS:(t + 1) * HEADS], tri[:, :], dA[:, t, :], start=True, stop=True)
            pe.matmul(bank[7][:, 64:96], below[:, :], dA[:, 0, :], start=True, stop=True).then_inc(acs_done, 1)

            pe.wait_ge(c_ready, 1)
            for r in range(2):
                for t in range(TT):
                    c = r * 256 + t * P
                    tr = pe.transpose(bank[4][:, c:c + P], c_tok[:, t, r * P:(r + 1) * P], ident[:, :])
            tr.then_inc(c_turned, 1)

            pe.wait_ge(unit_taken[0], unit_no[("ki", 0)] // 2 + 1)
            pe.wait_ge(unit_taken[1], unit_no[("qi", 3)] // 2 + 1)
            for h in range(IDX_HEADS):
                if h >= 2:
                    pe.wait_ge(relu_ready, h - 1)
                r = slice(64 * (h % 2), 64 * (h % 2) + 64)
                for t, (a, b) in enumerate(KEYS):
                    mm = pe.matmul(bank[2 + h % 2][:, a:b], qiT[r, h // 2, t * P:(t + 1) * P], kiT[r, 0:b - a],
                                   start=True, stop=True)
                mm.then_inc(index_done, 1)

            landed(("ukv",))
            pe.wait_ge(cT_ready, 2)
            for m in range(8):
                unit(("k", m), [(w_k[:, r, m * P:(m + 1) * P], cT[:, r, :]) for r in range(2)], S)
            for n in range(4):
                t, half = n // 2, n % 2
                mm = unit(("v", n), [(cT[:, r, t * P:(t + 1) * P], w_v[:, r, half * 512:(half + 1) * 512])
                                     for r in range(2)], 512)

            def logits(h):
                if h == 0:
                    pe.wait_ge(unit_taken[0], (unit_no[("v", 3)]) // 2 + 1)
                    pe.wait_ge(unit_taken[1], (unit_no[("v", 3)] + 1) // 2)
                    pe.wait_ge(relu_ready, IDX_HEADS)
                if h >= 2:
                    pe.wait_ge(att_biased, h - 1)
                r = slice(64 * (h % 2), 64 * (h % 2) + 64)
                for t, (a, b) in enumerate(KEYS):
                    mm = pe.matmul(bank[2 + h % 2][:, a:b], qT[r, h // 2, t * P:(t + 1) * P], kT[r, h // 2, 0:b - a],
                                   start=True, stop=True)
                mm.then_inc(logits_done, 1)

            def turn_prob(h):
                pe.wait_ge(prob_ready, h + 1)
                if h >= 1:
                    pe.wait_ge(probT_ready, h)
                for c in range(3):
                    tr = pe.transpose(bank[4][:, c * P:(c + 1) * P], prob[:, h % 2, c * P:(c + 1) * P], ident[:, :])
                tr.then_inc(prob_turned, 1)

            def pv(h):
                pe.wait_ge(probT_ready, h + 1)
                if h >= 2:
                    pe.wait_ge(attT_ready, h - 1)
                r = slice(64 * (h % 2), 64 * (h % 2) + 64)
                o = bank[5 + h % 2][r, 0:S]
                pe.matmul(o, v_tok[:, 0, h * HD:(h + 1) * HD], probT[:, h % 2, 0:256], start=True, stop=False)
                pe.matmul(o[:, P:S], v_tok[:, 1, h * HD:(h + 1) * HD], probT[:, h % 2, 256:384],
                          start=False, stop=True).then_inc(pv_done, 1)

            for i in range(24):
                m = CONV_ORDER[i]
                job = ("xbc", m // 4)
                if i % 4 == 0:
                    landed(job)
                channel_unit(("xbc", i), block512(job), m % 4 * P)
                if i < ATT_HEADS:
                    logits(i)
                if 1 <= i <= ATT_HEADS:
                    turn_prob(i - 1)
                if 2 <= i <= ATT_HEADS + 1:
                    pv(i - 2)

            def ssd_a(q):
                c, g = q // GROUPS, q % GROUPS
                ts = slice(c * P, (c + 1) * P)
                if q == 0:
                    pe.wait_ge(xc_ready, 24)
                    pe.wait_ge(attT_ready, ATT_HEADS)
                if q >= 1:
                    pe.wait_ge(xdt_ready, q)
                for j in range(4):
                    tr = pe.transpose(bank[5][:, j * P:(j + 1) * P], xcT[:, 4 * g + j, ts], ident[:, :])
                tr.then_inc(xs_turned, 1)
                if q >= 1:
                    pe.wait_ge(cb_ready, q)
                    if c == 0:
                        pe.wait_ge(b_tok_ready, q)
                if c == 0:
                    pe.transpose(bank[4][:, 256:384], xcT[:, 16 + g, ts], ident[:, :])
                pe.matmul(bank[4][:, 0:P], xcT[:, 16 + g, ts], xcT[:, 20 + g, ts], start=True, stop=True)\
                    .then_inc(cb_done, 1)
                pe.wait_ge(seg_in_ready, q + 1)
                if q >= 1:
                    pe.wait_ge(decay_ready, q)
                for j in range(2):
                    mm = pe.matmul(bank[2 + j][:, :], below[:, :], seg_in[:, j * 512:(j + 1) * 512], start=True, stop=True)
                mm.then_inc(seg_done, 1)

            def ssd_b(q):
                c, g = q // GROUPS, q % GROUPS
                pe.wait_ge(wts_ready, q + 1)
                if q >= 1:
                    pe.wait_ge(y_ready, q)
                for h in range(HPG):
                    col = (g * HPG + h) * HD
                    mm = pe.matmul(bank[6][:, h * HD:(h + 1) * HD], decay[:, h * P:(h + 1) * P],
                                   xdt3[:, c, col:col + HD], start=True, stop=True)
                mm.then_inc(y_diag_done, 1)
                if c == 0:
                    pe.wait_ge(b_tok_ready, q + 1)
                    if q >= 1:
                        pe.wait_ge(state_ready, q)
                    pe.matmul(bank[7][:, :], cbm[:, 1, :], xdec, start=True, stop=True).then_inc(state_done, 1)
                else:
                    pe.wait_ge(state_ready, GROUPS)
                    pe.matmul(bank[7][:, :], xcT[:, 20 + g, P:S], stateT[:, g, :], start=True, stop=True)\
                        .then_inc(y_off_done, 1)

            for m in range(16):
                job = ("gate", m // 4)
                if m % 4 == 0:
                    landed(job)
                channel_unit(("gate", m), block512(job), m % 4 * P)
                ssd_a(m // 2) if m % 2 == 0 else ssd_b(m // 2)

            for n in range(8):
                g, t = n // 2, n % 2
                job = ("z", g)
                if t == 0:
                    landed(job)
                mm = unit(("z", n), [(hT[:, k, t * P:(t + 1) * P], block512(job)[:, k, :]) for k in range(KD)], 512)

            def turn_y(j):
                pe.wait_ge(y_normed, 8)
                if j >= 2:
                    pe.wait_ge(yT_ready, 2 * (j - 1))
                for m in (2 * j, 2 * j + 1):
                    for t in range(TT):
                        c = (m % 2) * 256 + t * P
                        tr = pe.transpose(bank[2 + j % 2][:, c:c + P], y[:, t, m * P:(m + 1) * P], ident[:, :])
                tr.then_inc(y_turned, 1)

            for m in range(8):
                job = ("att", m // 4)
                if m % 4 == 0:
                    landed(job)
                w = block512(job)
                mm = unit(("att", m), [(w[:, k, m % 4 * P:(m % 4 + 1) * P], attT[:, k, :]) for k in range(8)], S)
                if m >= 1:
                    turn_y(m - 1)
            turn_y(7)
            pe.wait_ge(yT_ready, 16)
            for m in range(8):
                job = ("ssm", m // 2)
                if m % 2 == 0:
                    landed(job)
                w = slot(job).rearrange("p (k n) -> p k n", k=16)
                mm = unit(("ssm", m), [(w[:, k, m % 2 * P:(m % 2 + 1) * P], yT[:, k, :]) for k in range(16)], S)
            pe.wait_ge(mix_ready, 8)
            for n in range(4):
                half, t = n // 2, n % 2
                job = ("out", half)
                if t == 0:
                    landed(job)
                mm = unit(("out", n), [(mixT[:, k, t * P:(t + 1) * P], block512(job)[:, k, :]) for k in range(KD)], 512)

            pe.wait_ge(h2_ready, TT)
            for j in range(4):
                if j >= 2:
                    pe.wait_ge(h2T_ready, 2 * (j - 1))
                for k in (2 * j, 2 * j + 1):
                    for t in range(TT):
                        c = (k % 2) * 256 + t * P
                        tr = pe.transpose(bank[2 + j % 2][:, c:c + P], h2[:, t, k:D:KD], ident[:, :])
                tr.then_inc(h2_turned, 1)
            pe.wait_ge(h2T_ready, KD)
            pe.wait_ge(vecs_landed, VECS)
            for t in range(TT):
                for o, n, w in ((0, MG, lambda k: w_grp[:, k, :]), (64, MG * ME, lambda k: w_rt[:, :, k, :])):
                    c = t * P + o
                    for k in range(KD):
                        mm = pe.matmul(bank[7][:, c:c + n], h2T[:, k, t * P:(t + 1) * P], w(k),
                                       start=(k == 0), stop=(k == KD - 1))
            mm.then_inc(route_done, 1)
            pe.wait_ge(onehot_ready, 1)
            NE = MG * ME
            oh = rt[:, 256:320].rearrange("p (t e) -> p t e", t=TT)
            pe.matmul(bank[6][:, 0:NE], above[:, :], oh[:, 0, :], start=True, stop=True)
            pe.matmul(bank[6][:, NE:2 * NE], above[:, :], oh[:, 1, :], start=True, stop=False)
            pe.matmul(bank[6][:, NE:2 * NE], ones[:, :], oh[:, 0, :], start=False, stop=True)
            pe.matmul(bank[6][:, 2 * NE:3 * NE], ones[:, :], oh[:, 0, :], start=True, stop=False)
            pe.matmul(bank[6][:, 2 * NE:3 * NE], ones[:, :], oh[:, 1, :], start=False, stop=True).then_inc(rank_done, 1)

            def places(i):
                pe.wait_ge(perm_ready, i * 2 + 1)
                for k in range(KD):
                    c = (k % 4) * P
                    for t in range(TT):
                        mm = pe.matmul(bank[3 + k // 4][:, c:c + P], h2[:, t, k:D:KD], perm[:, t, :],
                                       start=(t == 0), stop=(t == TT - 1))
                    if k % 4 == 3:
                        mm.then_inc(gathered, 1)
                pe.wait_ge(perm_ready, i * 2 + 2)
                for t in range(TT):
                    tr = pe.transpose(bank[7][:, t * P:(t + 1) * P], pgate[:, t, :], ident[:, :])
                tr.then_inc(places_done, 1)
                pe.wait_ge(xgT_ready_a, i + 1)
                pe.wait_ge(xgT_ready_v, i + 1)

            def turn_hid(i):
                pe.wait_ge(hid_ready, i + 1)
                for f in range(2):
                    tr = pe.transpose(bank[2][:, f * P:(f + 1) * P], hid[:, 0, f * P:(f + 1) * P], ident[:, :])
                tr.then_inc(hid_turned, 1)
                pe.wait_ge(hidT_ready, i + 1)

            def scatter(i):
                for n in range(4):
                    t, half = n // 2, n % 2
                    if n < 2:
                        pe.wait_ge(y_grp_ready, i * 2 + (n + 1))
                    else:
                        pe.wait_ge(added, i * 4 + (n - 1))
                    pe.matmul(bank[3 + half][:, :], gateT[:, t, :], y_grp[:, half * 512:(half + 1) * 512],
                              start=True, stop=True).then_inc(scattered, 1)

            with pe.Fori(0, BATCHES) as b:
                places(b)
                for c in range(4):
                    pe.wait_ge(chunk_landed[c], b * 32 + 32)
                    for k in (2 * c, 2 * c + 1):
                        for e in range(EB):
                            r = slice(e * PLACES, (e + 1) * PLACES)
                            mm = pe.matmul(bank[0][r, :].rearrange("p (w f) -> p w f", w=2), xgT[:, k, r],
                                           c_up[c][:, :, e, k % 2, :], start=(k == 0), stop=(k == KD - 1))
                    mm.then_inc(chunk_used, 1)
                turn_hid(b)
                for c in (4, 5):
                    f = c - 4
                    pe.wait_ge(chunk_landed[c], b * 16 + 16)
                    for half in range(2):
                        for e in range(EB):
                            r = slice(e * PLACES, (e + 1) * PLACES)
                            mm = pe.matmul(bank[5 + half][r, :], hidT[:, 0, f, r],
                                           c_down[c][:, e, half * 512:(half + 1) * 512], start=(f == 0), stop=(f == 1))
                    mm.then_inc(chunk_used, 1)
                scatter(b)
            pe.wait_ge(route_ready, 1)
            over = pe.value_load(n_over_i[0:1, 0:1], min_val=0, max_val=MAX_OVER)
            with pe.If(over):
                with pe.Fori(0, over) as r:
                    i = r + BATCHES
                    places(i)
                    pe.wait_ge(over_up_landed, r * 32 + 32)
                    for k in range(KD):
                        mm = pe.matmul(bank[0][:, :].rearrange("p (w f) -> p w f", w=2), xgT[:, k, :], o_up[:, :, k, :],
                                       start=(k == 0), stop=(k == KD - 1))
                    mm.then_inc(chunk_used, 1)
                    turn_hid(i)
                    pe.wait_ge(over_down_landed, r * 16 + 16)
                    for half in range(2):
                        for f in range(2):
                            mm = pe.matmul(bank[5 + half][:, :], hidT[:, 0, f, :], o_down[:, f, half * 512:(half + 1) * 512],
                                           start=(f == 0), stop=(f == 1))
                    mm.then_inc(chunk_used, 1)
                    scatter(i)

        @block.scalar
        def _(act):
            step = Steps(act, a_step)
            A = nc.scalar.activation
            cw = conv_w[0].rearrange("j (m c) -> (j m) c", c=P)
            one = lambda a: a.rearrange("(m c) -> m c", c=P)
            for dst, src in ((crow[0:96, 0, :], cw), (crow[96:120, 0, :], one(conv_b[0])),
                             (crow[0:8, 1, :], one(norm_mix_g[0])), (crow[8:24, 1, :], one(ssm_norm_g[0])),
                             (crow[24:40, 1, :], gate_b[0].rearrange("b (m c) -> (b m) c", c=P)),
                             (crow[40:42, 1, :], one(kv_norm_g[0]))):
                act.dma_start(dst, src).then_inc(rows_landed, 16)
            row = lambda a, n: a.rearrange("(o n) -> o n", o=1).to_broadcast([P, n])
            for i, v in enumerate((dt_bias, a_log, d_skip)):
                act.dma_start(hvec[:, i, :], row(v[0], HEADS)).then_inc(vecs_landed, 16)
            act.dma_start(b_route[:, 0:MG], row(b_group[0], MG)).then_inc(vecs_landed, 16)
            act.dma_start(b_route[:, MG:], row(b_router[0].rearrange("g e -> (g e)"), MG * ME)).then_inc(vecs_landed, 16)
            act.dma_start(g_ffn[:, :], norm_ffn_g[0].rearrange("(p k) -> p k", k=KD)).then_inc(vecs_landed, 16)
            act.dma_start(w_grp[:, :, :], w_group[0].rearrange("(p k) g -> p k g", k=KD)).then_inc(vecs_landed, 16)
            act.dma_start(w_rt[:, :, :, :].rearrange("p g k e -> p g (k e)"),
                           w_router[0].rearrange("g (p k) e -> p g (k e)", k=KD)).then_inc(vecs_landed, 16)

            act.wait_ge(x_landed, 32)
            for t in range(TT):
                A(xn[:, t, :], x_in[:, t, :], ACT.Square, accum_out=st[:, t:t + 1]).then_inc(ss_ready, 1)
            act.wait_ge(ss_ready, TT + 1)
            A(st[:, 2:4], st[:, 0:2], ACT.Sqrt, bias=st[:, 63:64], scale=1.0 / D).then_inc(rms_ready, 1)

            for u in [("qi", m) for m in range(4)] + [("ki", 0)]:
                wait_unit(act, u)
                if u == ("qi", 0):
                    act.wait_ge(hT_ready, KD)
                took(A(qiT[:, u[1], :] if u[0] == "qi" else kiT, acc(u)[:, 0:S], ACT.Copy), u)
            act.wait_ge(ckv_ss_ready, TT)
            A(st[:, 6:8], st[:, 4:6], ACT.Sqrt, bias=st[:, 63:64], scale=1.0 / LATENT).then_inc(ckv_rms_ready, 1)
            act.wait_ge(vecs_landed, VECS)
            step(A(hvec[:, 1, :], hvec[:, 1, :], ACT.Exp))
            nc.scalar.mul(hvec[:, 1, :], hvec[:, 1, :], -1.0).then_inc(negA_ready, 1)
            act.wait_ge(dt_abs_ready, 1)
            A(sp_t[:, 1, :, :], sp_t[:, 1, :, :], ACT.Exp, scale=-1.0).then_inc(dt_exp_ready, 1)
            act.wait_ge(dt_u_ready, 1)
            A(sp_t[:, 3, :, :], sp_t[:, 2, :, :], ACT.Ln).then_inc(dt_ln_ready, 1)
            for m in range(8):
                u = ("q", m)
                wait_unit(act, u)
                took(A(qT[:, m, :], acc(u)[:, 0:S], ACT.Copy, scale=HD ** -0.5), u)
            act.wait_ge(acs_done, 1)
            A(eacs[:, :, :].rearrange("p t h -> p (t h)"), bank[7][:, 0:64], ACT.Exp)
            A(dec[:, :], bank[7][:, 64:96], ACT.Exp).then_inc(eacs_ready, 1)
            act.wait_ge(c_turned, 1)
            for r in range(2):
                A(cT[:, r, :], bank[4][:, r * 256:(r + 1) * 256], ACT.Copy, scale=g_kv(r)).then_inc(cT_ready, 1)
            for h in range(IDX_HEADS):
                act.wait_ge(index_done, h + 1)
                if h >= 2:
                    act.wait_ge(relu_used, h - 1)
                A(relu[:, h % 2, :], bank[2 + h % 2][:, 0:384], ACT.Relu, scale=HD ** -0.5).then_inc(relu_ready, 1)
            for m in range(8):
                u = ("k", m)
                wait_unit(act, u)
                took(A(kT[:, m, :], acc(u)[:, 0:S], ACT.Copy), u)
            for n in range(4):
                u = ("v", n)
                wait_unit(act, u)
                took(A(v_tok[:, n // 2, n % 2 * 512:(n % 2 + 1) * 512], acc(u)[:, :], ACT.Copy), u)

            def tanh_of(i):
                act.wait_ge(conv_ready, i + 1)
                if i >= 2:
                    act.wait_ge(xc_ready, i - 1)
                A(th[:, i % 2, 0:S], xcT[:, CONV_ORDER[i], :], ACT.Tanh).then_inc(tanh_ready, 1)

            for i in range(25):
                if i < 24:
                    m = CONV_ORDER[i]
                    wait_unit(act, ("xbc", i))
                    A(xcT[:, m, :], acc(("xbc", i))[:, 0:S], ACT.Identity, bias=conv_bias(m), scale=tap(3, m))\
                        .then_inc(first_tap_ready, 1)
                if i >= 1:
                    tanh_of(i - 1)
                if i < ATT_HEADS:
                    act.wait_ge(att_biased, i + 1)
                    for t, (a, b) in enumerate(KEYS):
                        c = 8 + 2 * (i % 2) + t
                        A(prob[:, i % 2, a:b], prob[:, i % 2, a:b], ACT.Exp, bias=st[:, c:c + 1], scale=-1.0,
                          accum_out=st[:, c + 8:c + 9]).then_inc(exp_ready, 1)
                if 1 <= i <= ATT_HEADS:
                    h = i - 1
                    act.wait_ge(prob_turned, h + 1)
                    if h >= 2:
                        act.wait_ge(pv_done, h - 1)
                    A(probT[:, h % 2, :], bank[4][:, 0:384], ACT.Copy).then_inc(probT_ready, 1)
                if 2 <= i <= ATT_HEADS + 1:
                    h = i - 2
                    r = slice(64 * (h % 2), 64 * (h % 2) + 64)
                    act.wait_ge(pv_done, h + 1)
                    A(attT[r, h // 2, :], bank[5 + h % 2][r, 0:S], ACT.Copy).then_inc(attT_ready, 1)

            for m in range(16):
                u = ("gate", m)
                wait_unit(act, u)
                ins = A(gT[:, m, :], acc(u)[:, 0:S], ACT.Tanh, bias=b_gate(m), scale=0.5)
                took(ins, u)
                q = m // 2
                if m % 2 == 0:
                    act.wait_ge(seg_done, q + 1)
                    if q >= 1:
                        act.wait_ge(y_diag_done, q)
                    for j in range(2):
                        ins = A(decay[:, j * 512:(j + 1) * 512], bank[2 + j][:, :], ACT.Exp)
                    ins.then_inc(decay_ready, 1)
                elif q < GROUPS:
                    act.wait_ge(state_done, q + 1)
                    A(stateT[:, q, :], bank[7][:, :], ACT.Copy).then_inc(state_ready, 1)

            for n in range(8):
                g, t = n // 2, n % 2
                wait_unit(act, ("z", n))
                if n >= 2:
                    act.wait_ge(y_gated, n - 1)
                A(th[:, n % 2, :], acc(("z", n))[:, :], ACT.Tanh, scale=0.5).then_inc(z_tanh_ready, 1)
                act.wait_ge(y_gated, n + 1)
                A(y_off, y[:, t, g * 512:(g + 1) * 512], ACT.Square, accum_out=st[:, 24 + n:25 + n])\
                    .then_inc(y_ss_ready, 1)
            act.wait_ge(y_ss_ready, 8)
            A(st[:, 32:40], st[:, 24:32], ACT.Sqrt, bias=st[:, 63:64], scale=1.0 / 512).then_inc(y_rms_ready, 1)
            for j in range(8):
                act.wait_ge(y_turned, j + 1)
                for m in (2 * j, 2 * j + 1):
                    c = (m % 2) * 256
                    A(yT[:, m, :], bank[2 + j % 2][:, c:c + S], ACT.Copy, scale=g_ssm(m)).then_inc(yT_ready, 1)

            for t in range(TT):
                act.wait_ge(x2_ready, 4)
                A(h2[:, t, :], x2[:, t, :], ACT.Square, accum_out=st[:, 40 + t:41 + t]).then_inc(x2_ss_ready, 1)
            act.wait_ge(x2_ss_ready, TT)
            A(st[:, 42:44], st[:, 40:42], ACT.Sqrt, bias=st[:, 63:64], scale=1.0 / D).then_inc(x2_rms_ready, 1)
            act.wait_ge(route_in, 1)
            A(rt[:, 16:24], rt[:, 16:24], ACT.Exp)
            A(rt[:, 480:482], rt[:, 480:482], ACT.Exp).then_inc(route_exp, 1)

            def moe_pass(i, up_value, down_value):
                act.wait_ge(gathered, i * 2 + 1)
                for k in range(4):
                    ins = A(xgT[:, k, :], bank[3][:, k * P:(k + 1) * P], ACT.Copy, scale=g_ffn[:, k:k + 1])
                ins.then_inc(xgT_ready_a, 1)
                act.wait_ge(places_done, i + 1)
                A(gateT[:, :, :].rearrange("p t s -> p (t s)"), bank[7][:, 0:2 * P], ACT.Copy)
                act.wait_ge(chunk_used, up_value)
                A(sil[:, 0, :], bank[0][:, 0:FF], ACT.Silu).then_inc(silu_ready, 1)
                act.wait_ge(hid_turned, i + 1)
                A(hidT[:, 0, :, :].rearrange("p f s -> p (f s)"), bank[2][:, 0:2 * P], ACT.Copy).then_inc(hidT_ready, 1)
                act.wait_ge(chunk_used, down_value)
                for half in range(2):
                    A(y_grp[:, half * 512:(half + 1) * 512], bank[5 + half][:, :], ACT.Copy).then_inc(y_grp_ready, 1)

            with act.Fori(0, BATCHES) as b:
                moe_pass(b, up_used(b), down_used(b))
            act.wait_ge(route_ready, 1)
            over = act.value_load(n_over_i[0:1, 0:1], min_val=0, max_val=MAX_OVER)
            with act.If(over):
                with act.Fori(0, over) as r:
                    moe_pass(r + BATCHES, over_up_used(r), over_down_used(r))
            act.wait_ge(fin_ss_ready, TT)
            A(st[:, 50:52], st[:, 48:50], ACT.Sqrt, bias=st[:, 63:64], scale=1.0 / D).then_inc(fin_rms_ready, 1)

        @block.vector
        def _(dve):
            v = nc.vector
            step = Steps(dve, v_step)
            v.memset(st[:, 63:64], EPS).then_inc(ss_ready, 1)

            dve.wait_ge(consts_turned, 1)
            v.tensor_scalar(ccol[:, 0, 0:120], bank[7][:, 0:120], 0.5, None, ALU.mult)
            step(v.tensor_copy(ccol[:, 1, 0:42], bank[7][:, 128:170]))
            step(v.tensor_scalar(ccol[:, 1, 24:40], ccol[:, 1, 24:40], 0.5, None, ALU.mult))

            dve.wait_ge(rms_ready, 1)
            step(v.reciprocal(st[:, 2:4], st[:, 2:4]))
            for t in range(TT):
                v.tensor_scalar(xn[:, t, :], x_in[:, t, :], st[:, 2 + t:3 + t], None, ALU.mult).then_inc(xn_ready, 1)
            for j in range(4):
                dve.wait_ge(xn_turned, j + 1)
                for k in (2 * j, 2 * j + 1):
                    c = (k % 2) * 256
                    v.tensor_scalar(hT[:, k, :], bank[2 + j % 2][:, c:c + S], g_mix(k), None, ALU.mult)\
                        .then_inc(hT_ready, 1)

            dve.wait_ge(iota_made, 1)
            step(v.scalar_tensor_tensor(out=dist, in0=dist, scalar=-1.0, in1=dist, op0=ALU.mult, op1=ALU.max))

            dve.wait_ge(vecs_landed, VECS)
            for t in range(TT):
                u = ("small", t)
                wait_unit(dve, u)
                v.tensor_scalar(wi[:, t, :], acc(u)[:, 0:8], IDX_HEADS ** -0.5, None, ALU.mult)
                v.tensor_copy(c_tok[:, t, :], acc(u)[:, 8:264])
                ins = v.tensor_tensor(sp_t[:, 0, t, :], acc(u)[:, 264:296], hvec[:, 0, :], ALU.add)
                took(ins, u)
                dve.wait_ge(unit_taken[unit_no[u] % 2], unit_no[u] // 2 + 1)
                v.tensor_tensor_reduce(out=bias[:, 0:256], in0=c_tok[:, t, :], in1=c_tok[:, t, :], scale=1.0, scalar=0.0,
                                       op0=ALU.mult, op1=ALU.add, accum_out=st[:, 4 + t:5 + t]).then_inc(ckv_ss_ready, 1)
            v.scalar_tensor_tensor(out=sp_t[:, 1, :, :], in0=sp_t[:, 0, :, :], scalar=-1.0, in1=sp_t[:, 0, :, :],
                                   op0=ALU.mult, op1=ALU.max).then_inc(dt_abs_ready, 1)
            dve.wait_ge(ckv_rms_ready, 1)
            step(v.reciprocal(st[:, 6:8], st[:, 6:8]))
            for t in range(TT):
                ins = v.tensor_scalar(c_tok[:, t, :], c_tok[:, t, :], st[:, 6 + t:7 + t], None, ALU.mult)
            ins.then_inc(c_ready, 1)
            dve.wait_ge(dt_exp_ready, 1)
            v.tensor_scalar(sp_t[:, 2, :, :], sp_t[:, 1, :, :], 1.0, None, ALU.add).then_inc(dt_u_ready, 1)
            dve.wait_ge(dt_u_ready, 1)
            step(v.tensor_scalar(dt[:, :, :], sp_t[:, 2, :, :], 1.0, None, ALU.subtract))
            step(v.tensor_tensor(sp_t[:, 1, :, :], sp_t[:, 1, :, :], dt[:, :, :], ALU.subtract))
            step(v.reciprocal(dt[:, :, :], sp_t[:, 2, :, :]))
            step(v.tensor_tensor(sp_t[:, 1, :, :], sp_t[:, 1, :, :], dt[:, :, :], ALU.mult))
            step(v.scalar_tensor_tensor(out=sp_t[:, 1, :, :], in0=sp_t[:, 0, :, :], scalar=0.0, in1=sp_t[:, 1, :, :],
                                        op0=ALU.max, op1=ALU.add))
            dve.wait_ge(dt_ln_ready, 1)
            step(v.tensor_tensor(dt[:, :, :], sp_t[:, 1, :, :], sp_t[:, 3, :, :], ALU.add))
            dve.wait_ge(negA_ready, 1)
            for t in range(TT):
                ins = v.tensor_tensor(dA[:, t, :], dt[:, t, :], hvec[:, 1, :], ALU.mult)
            ins.then_inc(dA_ready, 1)

            score = sel_work
            for h in range(IDX_HEADS):
                dve.wait_ge(relu_ready, h + 1)
                for t, (a, b) in enumerate(KEYS):
                    if h == 0:
                        ins = v.tensor_scalar(score[:, a:b], relu[:, 0, a:b], wi[:, t, 0:1], None, ALU.mult)
                    else:
                        ins = v.scalar_tensor_tensor(out=score[:, a:b], in0=relu[:, h % 2, a:b],
                                                     scalar=wi[:, t, h:h + 1], in1=score[:, a:b],
                                                     op0=ALU.mult, op1=ALU.add)
                ins.then_inc(relu_used, 1)
                dve.wait_ge(relu_used, h + 1)
            v.memset(score[0:64, 64:128], LEAST)
            step(v.memset(score[0:64, 320:384], LEAST))
            for r in range(TOPK // 8):
                for t, (a, b) in enumerate(KEYS):
                    ins = v.max(top8[:, t, :], score[:, a:b])
                step(ins)
                for t, (a, b) in enumerate(KEYS):
                    ins = v.match_replace(score[:, a:b], top8[:, t, :], score[:, a:b], TAKEN)
                step(ins)
            step(v.tensor_scalar(unsel, score, TAKEN / 1.5, LEAST, ALU.is_gt, ALU.mult))

            def scale_prob(h):
                dve.wait_ge(exp_ready, 2 * h + 2)
                c = 16 + 2 * (h % 2)
                step(v.reciprocal(st[:, c:c + 2], st[:, c:c + 2]))
                for t, (a, b) in enumerate(KEYS):
                    ins = v.tensor_scalar(prob[:, h % 2, a:b], prob[:, h % 2, a:b], st[:, c + t:c + t + 1], None, ALU.mult)
                ins.then_inc(prob_ready, 1)

            def silu_of(i):
                m = CONV_ORDER[i]
                dve.wait_ge(tanh_ready, i + 1)
                v.scalar_tensor_tensor(out=xcT[:, m, :], in0=th[:, i % 2, 0:S], scalar=1.0, in1=xcT[:, m, :],
                                       op0=ALU.add, op1=ALU.mult).then_inc(xc_ready, 1)

            for i in range(25):
                if 1 <= i <= ATT_HEADS:
                    scale_prob(i - 1)
                if i < ATT_HEADS:
                    slope = 2.0 ** (-8.0 * (i + 1) / ATT_HEADS)
                    step(v.scalar_tensor_tensor(out=bias, in0=dist, scalar=-slope, in1=unsel, op0=ALU.mult, op1=ALU.add))
                if i < 24:
                    m = CONV_ORDER[i]
                    u = ("xbc", i)
                    dve.wait_ge(first_tap_ready, i + 1)
                    for d in range(1, TAPS):
                        ins = v.scalar_tensor_tensor(out=xcT[:, m, d:S], in0=acc(u)[:, 0:S - d], scalar=tap(3 - d, m),
                                                     in1=xcT[:, m, d:S], op0=ALU.mult, op1=ALU.add)
                        if d < TAPS - 1:
                            step(ins)
                    took(ins, u)
                    dve.wait_ge(unit_taken[unit_no[u] % 2], unit_no[u] // 2 + 1)
                    dve.sem_inc(conv_ready, 1)
                if i < ATT_HEADS:
                    dve.wait_ge(logits_done, i + 1)
                    if i >= 2:
                        dve.wait_ge(prob_turned, i - 1)
                    for t, (a, b) in enumerate(KEYS):
                        c = 8 + 2 * (i % 2) + t
                        ins = v.tensor_tensor_reduce(out=prob[:, i % 2, a:b], in0=bank[2 + i % 2][:, a:b], in1=bias[:, a:b],
                                                     scale=-1.0, scalar=3e38, op0=ALU.add, op1=ALU.min,
                                                     accum_out=st[:, c:c + 1])
                    ins.then_inc(att_biased, 1)
                if i >= 1:
                    silu_of(i - 1)

            def bcast(a, n):
                return a.unsqueeze(2).to_broadcast([P, HPG, n])

            def make_seg_in(q):
                c, g = q // GROUPS, q % GROUPS
                v.tensor_tensor(seg_in.rearrange("p (h l) -> p h l", h=HPG),
                                tri[:, :].unsqueeze(1).to_broadcast([P, HPG, P]),
                                bcast(dA[:, c, g * HPG:(g + 1) * HPG], P), ALU.mult).then_inc(seg_in_ready, 1)

            dve.wait_ge(attT_ready, ATT_HEADS)
            make_seg_in(0)
            for q in range(8):
                c, g = q // GROUPS, q % GROUPS
                hs = slice(g * HPG, (g + 1) * HPG)
                cols = slice(g * 512, (g + 1) * 512)
                src = bank[5][:, :].rearrange("p (h d) -> p h d", h=HPG)
                dve.wait_ge(xs_turned, q + 1)
                if q == 0:
                    dve.wait_ge(eacs_ready, 1)
                v.tensor_tensor(y[:, c, cols].rearrange("p (h d) -> p h d", h=HPG), src, bcast(hvec[:, 2, hs], HD), ALU.mult)
                v.tensor_tensor(xdt3[:, c, cols].rearrange("p (h d) -> p h d", h=HPG), src, bcast(dt[:, c, hs], HD), ALU.mult)\
                    .then_inc(xdt_ready, 1)
                dve.wait_ge(xdt_ready, q + 1)
                if c == 0:
                    if q >= 1:
                        dve.wait_ge(state_done, q)
                    v.tensor_tensor(xdec.rearrange("p (h d) -> p h d", h=HPG),
                                    xdt3[:, c, cols].rearrange("p (h d) -> p h d", h=HPG), bcast(dec[:, hs], HD), ALU.mult)
                dve.wait_ge(cb_done, q + 1)
                if c == 0:
                    v.tensor_copy(cbm[:, 1, :], bank[4][:, 256:384]).then_inc(b_tok_ready, 1)
                v.tensor_tensor(cbm[:, 0, :], bank[4][:, 0:P], tri[:, :], ALU.mult).then_inc(cb_ready, 1)
                dve.wait_ge(cb_ready, q + 1)
                dve.wait_ge(decay_ready, q + 1)
                v.tensor_tensor(decay.rearrange("p (h l) -> p h l", h=HPG), decay.rearrange("p (h l) -> p h l", h=HPG),
                                cbm[:, 0, :].unsqueeze(1).to_broadcast([P, HPG, P]), ALU.mult).then_inc(wts_ready, 1)
                if q < 7:
                    dve.wait_ge(seg_done, q + 1)
                    make_seg_in(q + 1)
                dve.wait_ge(y_diag_done, q + 1)
                ins = v.tensor_tensor(y[:, c, cols], y[:, c, cols], bank[6][:, :], ALU.add)
                if c == 1:
                    step(ins)
                    dve.wait_ge(y_off_done, g + 1)
                    step(v.tensor_tensor(y_off.rearrange("p (h d) -> p h d", h=HPG),
                                         bank[7][:, :].rearrange("p (h d) -> p h d", h=HPG),
                                         bcast(eacs[:, c, hs], HD), ALU.mult))
                    ins = v.tensor_tensor(y[:, c, cols], y[:, c, cols], y_off, ALU.add)
                ins.then_inc(y_ready, 1)
            dve.wait_ge(y_ready, 8)

            for n in range(8):
                g, t = n // 2, n % 2
                cols = slice(g * 512, (g + 1) * 512)
                u = ("z", n)
                dve.wait_ge(z_tanh_ready, n + 1)
                ins = v.scalar_tensor_tensor(out=th[:, n % 2, :], in0=th[:, n % 2, :], scalar=1.0, in1=acc(u)[:, :],
                                             op0=ALU.add, op1=ALU.mult)
                took(ins, u)
                dve.wait_ge(unit_taken[unit_no[u] % 2], unit_no[u] // 2 + 1)
                v.scalar_tensor_tensor(out=y[:, t, cols], in0=th[:, n % 2, :], scalar=0.5, in1=y[:, t, cols],
                                       op0=ALU.mult, op1=ALU.mult).then_inc(y_gated, 1)
            dve.wait_ge(y_rms_ready, 1)
            step(v.reciprocal(st[:, 32:40], st[:, 32:40]))
            for n in range(8):
                g, t = n // 2, n % 2
                v.tensor_scalar(y[:, t, g * 512:(g + 1) * 512], y[:, t, g * 512:(g + 1) * 512], st[:, 32 + n:33 + n],
                                None, ALU.mult).then_inc(y_normed, 1)

            dve.wait_ge(gate_ready, 16)
            for m in range(8):
                u = ("att", m)
                wait_unit(dve, u)
                took(v.tensor_tensor(gT[:, 8 + m, :], acc(u)[:, 0:S], gT[:, 8 + m, :], ALU.mult), u)
            for m in range(8):
                u = ("ssm", m)
                wait_unit(dve, u)
                took(v.tensor_tensor(th[:, m % 2, 0:S], acc(u)[:, 0:S], gT[:, m, :], ALU.mult), u)
                dve.wait_ge(unit_taken[unit_no[u] % 2], unit_no[u] // 2 + 1)
                v.tensor_tensor(mixT[:, m, :], th[:, m % 2, 0:S], gT[:, 8 + m, :], ALU.add).then_inc(mix_ready, 1)
            dve.wait_ge(x_again_landed, 32)
            for n in range(4):
                half, t = n // 2, n % 2
                u = ("out", n)
                wait_unit(dve, u)
                cols = slice(half * 512, (half + 1) * 512)
                ins = v.tensor_tensor(x2[:, t, cols], acc(u)[:, :], x_again[:, t, cols], ALU.add)
                took(ins, u)
                dve.wait_ge(unit_taken[unit_no[u] % 2], unit_no[u] // 2 + 1)
                dve.sem_inc(x2_ready, 1)

            dve.wait_ge(x2_rms_ready, 1)
            step(v.reciprocal(st[:, 42:44], st[:, 42:44]))
            for t in range(TT):
                v.tensor_scalar(h2[:, t, :], x2[:, t, :], st[:, 42 + t:43 + t], None, ALU.mult).then_inc(h2_ready, 1)
            for j in range(4):
                dve.wait_ge(h2_turned, j + 1)
                for k in (2 * j, 2 * j + 1):
                    c = (k % 2) * 256
                    v.tensor_scalar(h2T[:, k, :], bank[2 + j % 2][:, c:c + S], g_ffn[:, k:k + 1], None, ALU.mult)\
                        .then_inc(h2T_ready, 1)

            T4 = lambda a, n=MG: rt[:, a:a + TT * n].rearrange("p (t n) -> p t n", t=TT)
            small2 = lambda a: rt[:, a:a + TT]
            per = lambda a, n: a.unsqueeze(2).to_broadcast([P, TT, n])
            rev = rt[:, 400:432]
            v.tensor_scalar(iota1[:, :], iota[:, :], 1.0, None, ALU.add).then_inc(over_turn, 1)
            v.tensor_tensor(iota1x, iota[:, 0:PLACES].unsqueeze(1).to_broadcast([P, TT * EB, PLACES]).rearrange("p (t e) s -> p t e s", t=TT), ones[:, 0:TT * EB].unsqueeze(2).to_broadcast([P, TT * EB, PLACES]).rearrange("p (t e) s -> p t e s", t=TT), ALU.add)
            step(v.tensor_scalar(rev, iota[:, 0:32], -1.0, 32.0, ALU.mult, ALU.add))

            def largest(dst, vals, n, mx, best):
                step(v.tensor_reduce(mx, vals, AX.X, ALU.max))
                step(v.tensor_tensor(dst, vals, per(mx, n), ALU.is_equal))
                step(v.tensor_tensor(dst, dst, rev[:, 0:n].unsqueeze(1).to_broadcast([P, TT, n]), ALU.mult))
                step(v.tensor_reduce(best, dst, AX.X, ALU.max))
                step(v.tensor_tensor(dst, dst, per(best, n), ALU.is_equal))

            oh, ge, gl, el, oh1, oh2, scr, gate = T4(0), T4(16), T4(32), T4(64, 32), T4(128, 32), T4(192, 32), T4(256, 32), T4(320, 32)
            dve.wait_ge(route_done, 1)
            lg = bank[7][:, 0:256].rearrange("p (t c) -> p t c", t=TT)
            v.tensor_tensor(gl, lg[:, :, 0:MG], b_route[:, 0:MG].unsqueeze(1).to_broadcast([P, TT, MG]), ALU.add)
            step(v.tensor_tensor(el, lg[:, :, 64:96], b_route[:, MG:].unsqueeze(1).to_broadcast([P, TT, 32]), ALU.add))
            largest(oh, gl, MG, small2(482), small2(484))
            step(v.tensor_tensor(ge, gl, per(small2(482), MG), ALU.subtract))
            step(v.tensor_scalar(gl, oh, 1.0, -LEAST, ALU.subtract, ALU.mult))
            for t in range(TT):
                ins = v.tensor_tensor(el[:, t, :].rearrange("p (g e) -> p g e", g=MG), el[:, t, :].rearrange("p (g e) -> p g e", g=MG),
                                      gl[:, t, :].unsqueeze(2).to_broadcast([P, MG, ME]), ALU.add)
            step(ins)
            largest(oh1, el, 32, small2(486), small2(488))
            step(v.scalar_tensor_tensor(out=el, in0=oh1, scalar=LEAST, in1=el, op0=ALU.mult, op1=ALU.add))
            largest(oh2, el, 32, small2(490), small2(492))
            v.tensor_tensor(scr, oh1, oh2, ALU.add).then_inc(onehot_ready, 1)
            step(v.tensor_tensor(small2(480), small2(490), small2(486), ALU.subtract))
            dve.sem_inc(route_in, 1)
            dve.wait_ge(route_exp, 1)
            step(v.tensor_reduce(small2(494), ge, AX.X, ALU.add))
            step(v.scalar_tensor_tensor(out=small2(494), in0=small2(480), scalar=1.0, in1=small2(494), op0=ALU.add, op1=ALU.mult))
            step(v.reciprocal(small2(494), small2(494)))
            step(v.tensor_tensor(small2(496), small2(494), small2(480), ALU.mult))
            step(v.tensor_tensor(gate, oh1, per(small2(494), 32), ALU.mult))
            step(v.tensor_tensor(oh2, oh2, per(small2(496), 32), ALU.mult))
            step(v.tensor_tensor(gate, gate, oh2, ALU.add))
            dve.wait_ge(rank_done, 1)
            NE = MG * ME
            step(v.scalar_tensor_tensor(out=rank1, in0=bank[6][:, 0:2 * NE].rearrange("p (t e) -> p t e", t=TT),
                                        scalar=1.0, in1=scr, op0=ALU.add, op1=ALU.mult))
            v.tensor_scalar(flags[:, 0:NE], bank[6][:, 2 * NE:3 * NE], float(PLACES), None, ALU.is_gt)
            step(v.tensor_scalar(flags[:, NE:2 * NE], bank[6][:, 2 * NE:3 * NE], float(PLACES + P), None, ALU.is_gt))
            step(v.tensor_copy(before[:, 0, :], flags))
            for n in range(6):
                a, b, d = n % 2, 1 - n % 2, 1 << n
                v.tensor_copy(before[:, b, 0:d], before[:, a, 0:d])
                step(v.tensor_tensor(before[:, b, d:64], before[:, a, d:64], before[:, a, 0:64 - d], ALU.add))
            v.tensor_copy(n_over_i[:, 0:1], before[:, 0, 63:64])
            step(v.tensor_tensor(over_at, before[:, 0, :], flags, ALU.mult))
            hit = th[:, :, :].rearrange("p a b -> p (a b)").rearrange("p (j i) -> p j i", j=MAX_OVER)
            step(v.tensor_tensor(hit, over_at.unsqueeze(1).to_broadcast([P, MAX_OVER, 64]),
                                 iota1[:, 0:MAX_OVER].unsqueeze(2).to_broadcast([P, MAX_OVER, 64]), ALU.is_equal))
            step(v.tensor_tensor(hit, hit, iota[:, 0:64].unsqueeze(1).to_broadcast([P, MAX_OVER, 64]), ALU.mult))
            step(v.tensor_reduce(entry[:, 1, :], hit, AX.X, ALU.add))
            step(v.tensor_scalar(entry[:, 0, :], entry[:, 1, :], float(NE), float(P), ALU.is_ge, ALU.mult))
            step(v.scalar_tensor_tensor(out=entry[:, 1, :], in0=entry[:, 0, :], scalar=-float(NE) / P, in1=entry[:, 1, :],
                                        op0=ALU.mult, op1=ALU.add))
            step(v.tensor_copy(entry_i[:, :], entry[:, 1, :]))
            v.tensor_scalar(entry[:, 0, :], entry[:, 0, :], float(PLACES), None, ALU.add).then_inc(route_ready, 1)
            dve.wait_ge(route_ready, 1)

            def moe_pass(i):
                dve.wait_ge(gathered, i * 2 + 2)
                for k in range(4, KD):
                    ins = v.tensor_scalar(xgT[:, k, :], bank[4][:, (k - 4) * P:(k - 3) * P], g_ffn[:, k:k + 1], None, ALU.mult)
                ins.then_inc(xgT_ready_v, 1)
                dve.wait_ge(silu_ready, i + 1)
                v.tensor_tensor(hid[:, 0, :], bank[0][:, FF:2 * FF], sil[:, 0, :], ALU.mult).then_inc(hid_ready, 1)
                for n in range(4):
                    t, half = n // 2, n % 2
                    cols = slice(half * 512, (half + 1) * 512)
                    dve.wait_ge(scattered, i * 4 + (n + 1))
                    v.tensor_tensor(x2[:, t, cols], x2[:, t, cols], bank[3 + half][:, :], ALU.add).then_inc(added, 1)

            with dve.Fori(0, BATCHES) as b:
                mine = bass.ds(b * EB, EB)
                four = lambda a: a.rearrange("p t (e s) -> p t e s", e=EB)
                grow = lambda a: a[:, :, mine].unsqueeze(3).to_broadcast([P, TT, EB, PLACES])
                v.tensor_tensor(four(perm), iota1x, grow(rank1), ALU.is_equal).then_inc(perm_ready, 1)
                dve.wait_ge(perm_ready, b * 2 + 1)
                v.tensor_tensor(four(pgate), four(perm), grow(gate), ALU.mult).then_inc(perm_ready, 1)
                moe_pass(b)
            over = dve.value_load(n_over_i[0:1, 0:1], min_val=0, max_val=MAX_OVER)
            with dve.If(over):
                with dve.Fori(0, over) as r:
                    ex = dve.value_load(entry_i[0:1, bass.ds(r, 1)], min_val=0, max_val=NE - 1)
                    own = over_now[:, 0:4].rearrange("p (a t) -> p a t", a=2)
                    v.tensor_copy(own[:, 0, :].unsqueeze(2), rank1[:, :, bass.ds(ex, 1)])
                    v.tensor_copy(own[:, 1, :].unsqueeze(2), gate[:, :, bass.ds(ex, 1)])
                    v.tensor_copy(over_now[:, 4:5], entry[:, 0, bass.ds(r, 1)]).then_inc(over_picked, 1)
                    dve.wait_ge(over_picked, r * 2 + 1)
                    v.tensor_scalar(own[:, 0, :], own[:, 0, :], over_now[:, 4:5], None, ALU.subtract).then_inc(over_picked, 1)
                    dve.wait_ge(over_picked, r * 2 + 2)
                    for t in range(TT):
                        ins = v.tensor_scalar(perm[:, t, :], iota1[:, :], over_now[:, t:t + 1], None, ALU.is_equal)
                    ins.then_inc(perm_ready, 1)
                    dve.wait_ge(perm_ready, r * 2 + (2 * BATCHES + 1))
                    for t in range(TT):
                        ins = v.tensor_scalar(pgate[:, t, :], perm[:, t, :], over_now[:, 2 + t:3 + t], None, ALU.mult)
                    ins.then_inc(perm_ready, 1)
                    moe_pass(r + BATCHES)
                    dve.wait_ge(added, r * 4 + 4 * (BATCHES + 1))
                    dve.sem_inc(over_turn, 1)

            dve.wait_ge(added, 4 * BATCHES)
            for t in range(TT):
                v.tensor_tensor_reduce(out=h2[:, t, :], in0=x2[:, t, :], in1=x2[:, t, :], scale=1.0, scalar=0.0,
                                       op0=ALU.mult, op1=ALU.add, accum_out=st[:, 48 + t:49 + t]).then_inc(fin_ss_ready, 1)
            dve.wait_ge(fin_rms_ready, 1)
            dve.wait_ge(fin_ss_ready, TT)
            v.reciprocal(st[:, 50:52], st[:, 50:52]).then_inc(fin_rms_ready, 1)
            dve.wait_ge(fin_rms_ready, 2)
            dve.wait_ge(g_fin_landed, 16)
            for t in range(TT):
                v.scalar_tensor_tensor(out=x2[:, t, :], in0=x2[:, t, :], scalar=st[:, 50 + t:51 + t], in1=g_fin,
                                       op0=ALU.mult, op1=ALU.mult).then_inc(out_ready, 1)


_INS = ['x', 'norm_mix_g', 'w_in', 'conv_w', 'conv_b', 'dt_bias', 'a_log', 'd_skip', 'ssm_norm_g', 'kv_norm_g',
        'w_uk', 'w_uv', 'gate_b', 'w_branch_ssm', 'w_branch_att', 'w_out', 'norm_ffn_g', 'w_group', 'b_group',
        'w_router', 'b_router', 'w_e1', 'w_e3', 'w_e2', 'norm_final_g']


def kernel(**inputs):
    import numpy as _np
    import concourse.bacc as _bacc
    from concourse import mybir as _mybir
    from concourse.bass_utils import run_bass_kernel_spmd as _run

    nc = _bacc.Bacc("TRN2", target_bir_lowering=False, num_devices=1)
    arrays, args = {}, []
    for name in _INS:
        a = _np.ascontiguousarray(inputs[name])
        arrays[f"in_{name}_dram"] = a
        args.append(nc.dram_tensor(f"in_{name}_dram", a.shape, _mybir.dt.from_np(a.dtype), kind="ExternalInput").ap())
    args.append(nc.dram_tensor("out_dram", (1, S, D), F32, kind="ExternalOutput").ap())
    hybrid_block(nc, *args)
    r = _run(nc, [arrays], core_ids=[0])
    return r.results[0]["out_dram"]
```

```python
from contextlib import ExitStack

import concourse.bass as bass
from concourse import mybir

F32 = mybir.dt.float32
F32R = mybir.dt.float32r
I32 = mybir.dt.int32
ALU = mybir.AluOpType
ACT = mybir.ActivationFunctionType
AX = mybir.AxisListType

P = 128
D = 1024
S = 256
TT = S // P
KD = D // P
EPS = 1e-6
D_INNER = 2 * D
HEADS = 32
HD = 64
GROUPS = 4
HPG = HEADS // GROUPS
XBC = D_INNER + 2 * GROUPS * P
TAPS = 4
ATT_HEADS = 16
LATENT = 256
IDX_HEADS = 8
TOPK = 64
MG = 4
ME = 8
FF = 256
LEAST = -1e30
TAKEN = -3e38

C_Z = 0
C_XBC = C_Z + D_INNER
C_DT = C_XBC + XBC
C_Q = C_DT + HEADS
C_CKV = C_Q + ATT_HEADS * HD
C_QI = C_CKV + LATENT
C_KI = C_QI + IDX_HEADS * HD
C_WI = C_KI + HD
C_GATE = C_WI + IDX_HEADS

HALF = 256
RAW = 2048
NRAW = 5
SLOT = 4096
NSLOTS = 5
EB = 4
PLACES = P // EB
BATCHES = MG * ME // EB
EARLY = 2
CHUNKS = 6
MAX_OVER = 16
CONV_ORDER = list(range(16, 24)) + list(range(16))


def hybrid_block(nc, x, norm_mix_g, w_in, conv_w, conv_b, dt_bias, a_log, d_skip, ssm_norm_g,
                 kv_norm_g, w_uk, w_uv, gate_b, w_branch_ssm, w_branch_att, w_out, norm_ffn_g,
                 w_group, b_group, w_router, b_router, w_e1, w_e3, w_e2, norm_final_g, out):
    ctx = ExitStack()
    with ctx:
        def sb(name, shape, dt=F32):
            return ctx.enter_context(nc.sbuf_tensor(name, shape, dt))

        def sem(name):
            return ctx.enter_context(nc.semaphore(name))

        at0 = (nc.sbuf_base + 31) // 32 * 32
        sb("arena", [P, 192 * 256])

        def at(name, kib, shape, dt=F32):
            return nc.alloc_sbuf_tensor_at(name, shape, dt, offset=at0 + kib * 1024)

        raw = at("raw", 0, [P, NRAW * RAW])
        w_hi = [at(f"w_hi{i}", 40 + 8 * i, [P, RAW], F32R) for i in range(2)]
        w_lo = [at(f"w_lo{i}", 56 + 8 * i, [P, RAW], F32R) for i in range(2)]
        ring = at("ring", 0, [P, NSLOTS * SLOT])
        hT_lo = at("hT_lo", 72, [P, KD, S], F32R)
        hT_hi = at("hT_hi", 80, [P, KD, S], F32R)
        moe_small = at("moe_small", 80, [P, 2048])
        xcT = at("xcT", 88, [P, 24, S])
        yT_hi = at("yT_hi", 88, [P, 16, S], F32R)
        xs = at("xs", 112, [P, TT * D_INNER])
        xdt = at("xdt", 128, [P, TT * D_INNER])
        yT_lo = at("yT_lo", 128, [P, 16, S], F32R)
        kv = at("kv", 144, [P, 16, S])
        qT = at("qT", 160, [P, 8, S])
        work = at("work", 168, [P, 5120])
        ident = sb("ident", [P, P])
        tri = sb("tri", [P, P])
        above = sb("above", [P, P])
        ones = sb("ones", [P, P])
        iota_i = sb("iota_i", [P, S], I32)
        iota = sb("iota", [P, P])
        crow = sb("crow", [P, 2, P])
        ccol = sb("ccol", [P, 2, P])
        g_ffn = sb("g_ffn", [P, KD])
        hvec = sb("hvec", [P, 3, HEADS])
        b_route = sb("b_route", [P, MG + MG * ME])
        w_route = sb("w_route", [P, KD, MG + MG * ME])
        st = sb("st", [P, 64])
        sp_t = sb("sp_t", [P, 4, TT, HEADS])
        dt = sb("dt", [P, TT, HEADS])
        dA = sb("dA", [P, TT, HEADS])
        dA_hi = sb("dA_hi", [P, TT, HEADS], F32R)
        dA_lo = sb("dA_lo", [P, TT, HEADS], F32R)
        below_r = sb("below_r", [P, P], F32R)
        eacs = sb("eacs", [P, TT, HEADS])
        dec = sb("dec", [P, HEADS])
        rt = at("rt", 188, [P, 1024])
        wi = sb("wi", [P, TT, IDX_HEADS])
        top8 = sb("top8", [P, TT, 8])
        n_over_i = sb("n_over_i", [P, 3], I32)

        xn = xdt[:, 0:TT * D].rearrange("p (t d) -> p t d", t=TT)
        x_in = xs[:, 0:TT * D].rearrange("p (t d) -> p t d", t=TT)
        y = xs[:, :].rearrange("p (t d) -> p t d", t=TT)
        xdt3 = xdt[:, :].rearrange("p (t d) -> p t d", t=TT)
        kT = kv[:, 0:8, :]
        v_tok = kv[:, 8:16, :].rearrange("p (t a) b -> p t (a b)", t=TT)
        gT = kv
        attT = qT
        attT_lo = at("attT_lo", 160, [P, 8, S], F32R)
        attT_hi = at("attT_hi", 168, [P, 8, S], F32R)
        qiT = work[:, 0:1024].rearrange("p (m s) -> p m s", m=4)
        kiT = work[:, 1024:1280]
        c_tok = work[:, 1280:1792].rearrange("p (t r) -> p t r", t=TT)
        cT_lo = at("cT_lo", 168 + 5, [P, 2, S], F32R)
        cT_hi = at("cT_hi", 168 + 7, [P, 2, S], F32R)
        prob = work[:, 2304:3072].rearrange("p (b s) -> p b s", b=2)
        probT = work[:, 3072:3840].rearrange("p (b s) -> p b s", b=2)
        bias = work[:, 3840:4224]
        dist = work[:, 4224:4608]
        unsel = work[:, 4608:4992]
        bias2 = [bias, work[:, 0:384]]
        stateT = work[:, 0:2048].rearrange("p (g d) -> p g d", g=GROUPS)
        seg_in = [at("seg_in_hi", 176, [P, 1024], F32R), at("seg_in_lo", 188, [P, 1024], F32R)]
        decay = work[:, 3072:4096]
        xdec = work[:, 4096:4608]
        y_off = work[:, 4608:5120]
        th = sb("th", [P, 2, 512])
        smallT = th[:, 0, 0:S]
        below = th[:, 1, 0:P]
        cbm = sb("cbm", [P, 2, P])
        sel_work = rt[:, 0:384]
        relu = xs[:, 0:768].rearrange("p (b s) -> p b s", b=2)
        x_again = work[:, 2048:4096].rearrange("p (t d) -> p t d", t=TT)
        x2T = xcT[:, 16:24, :]
        x2 = xs[:, 0:2048].rearrange("p (t d) -> p t d", t=TT)
        h2 = xs[:, 2048:4096].rearrange("p (t d) -> p t d", t=TT)
        kvf = kv[:, :, :].rearrange("p a b -> p (a b)")
        xgT = kvf[:, 0:1024].rearrange("p (k s) -> p k s", k=KD)
        xg_flat = kvf[:, 0:1024]
        hid = kvf[:, 1024:1280]
        sil = kvf[:, 1280:1536]
        hidT = kvf[:, 1536:1792].rearrange("p (f s) -> p f s", f=2)
        gateT = kvf[:, 1792:2048].rearrange("p (t s) -> p t s", t=TT)
        y_grp = kvf[:, 2048:3072]
        hf = moe_small
        perm = hf[:, 0:256].rearrange("p (t s) -> p t s", t=TT)
        pgate = hf[:, 256:512].rearrange("p (t s) -> p t s", t=TT)
        rank1 = hf[:, 512:576].rearrange("p (t e) -> p t e", t=TT)
        flags = hf[:, 576:640]
        before = hf[:, 640:768].rearrange("p (b n) -> p b n", b=2)
        over_at = hf[:, 768:832]
        entry = hf[:, 832:866].rearrange("p (a n) -> p a n", a=2)
        over_now = hf[:, 872:880]
        iota1 = hf[:, 1280:1408]
        iota1x = hf[:, 1024:1280].rearrange("p (t e s) -> p t e s", t=TT, e=EB)
        entry_i = sb("entry_i", [P, MAX_OVER + 1], I32)
        g_fin = work[:, 2048:3072]
        xcf = xcT[:, :, :].rearrange("p a b -> p (a b)")
        cslots = [ring[:, n * SLOT:(n + 1) * SLOT] for n in range(NSLOTS)] + [xcf[:, 0:SLOT]]
        extra = [at("extra0", 160, [P, SLOT]), at("extra1", 128, [P, SLOT])]
        c_up = [c.rearrange("p (w e k f) -> p w e k f", w=2, e=EB, k=2) for c in cslots]
        c_down = [c.rearrange("p (e k d) -> p e k d", e=EB, k=2) for c in cslots]
        c_early = [[c.rearrange("p (w e k f) -> p w e k f", w=2, e=EB, k=2) for c in (extra[n], cslots[n])]
                   for n in range(EARLY)]
        o_e1 = [a.rearrange("p (k f) -> p k f", k=4) for a in (kvf[:, 3072:4096], work[:, 4096:5120])]
        o_e3 = work[:, 2048:4096].rearrange("p (k f) -> p k f", k=KD)
        o_down = xcf[:, SLOT:SLOT + 2048].rearrange("p (k d) -> p k d", k=2)

        def tap(j, m):
            return ccol[:, 0, j * 24 + m:j * 24 + m + 1]

        def conv_bias(m):
            return ccol[:, 0, 96 + m:97 + m]

        def g_mix(k):
            return ccol[:, 1, k:k + 1]

        def g_ssm(m):
            return ccol[:, 1, 8 + m:9 + m]

        def b_gate(m):
            return ccol[:, 1, 24 + m:25 + m]

        def g_kv(r):
            return ccol[:, 1, 40 + r:41 + r]

        def g_ffn_k(k):
            return ccol[:, 1, 42 + k:43 + k]

        bank = [ctx.enter_context(nc.psum_tensor(f"bank{i}", [P, 512], F32)) for i in range(8)]

        jobs = [("qi", 0), ("qi", 1), ("small",), ("ckv",)] + [("q", b) for b in range(4)] + [("uk",), ("uv",)]
        jobs += [("xbc", b) for b in (8, 9, 10, 11, 0, 1, 2, 3, 4, 5, 6, 7)]
        jobs += [("gate", b) for b in range(8)] + [("z", b) for b in range(8)]
        jobs += [("att", b) for b in range(4)] + [("ssm", b) for b in range(8)]
        jobs += [("out", b) for b in range(4)]
        job_no = {j: n for n, j in enumerate(jobs)}

        def slot(job):
            n = job_no[job] % NRAW
            return raw[:, n * RAW:(n + 1) * RAW]

        N_SMALL, S_WI, S_DT = P, HD, P - HEADS

        def columns(a, job):
            if job[0] == "small":
                return a[:, 0:KD * N_SMALL].rearrange("p (k n) -> p k n", k=KD)
            if job[0] in ("uk", "uv"):
                return a.rearrange("p (k n) -> p k n", k=2)
            return a.rearrange("p (k n) -> p k n", k=KD)

        win = w_in[0].rearrange("(k p) n -> p k n", p=P)

        def loads(job):
            kind = job[0]
            if kind in ("uk", "uv"):
                dst, src = columns(slot(job), job), w_uk if kind == "uk" else w_uv
                return [(dst[:, r, :].rearrange("p (h d) -> p h d", d=HD),
                         src[0, :, r * P:(r + 1) * P, :].rearrange("h p d -> p h d")) for r in range(2)]
            b = columns(slot(job), job)
            if kind == "small":
                return [(b[:, :, 0:S_DT], win[:, :, C_KI:C_KI + S_DT]),
                        (b[:, :, S_DT:], win[:, :, C_DT:C_DT + HEADS])]
            if kind == "ssm":
                n, kh = job[1] // 2, job[1] % 2
                w = w_branch_ssm[0].rearrange("(k p) n -> p k n", p=P)
                return [(b, w[:, kh * 8:kh * 8 + 8, n * HALF:(n + 1) * HALF])]
            if kind in ("att", "out"):
                w = (w_branch_att if kind == "att" else w_out)[0].rearrange("(k p) n -> p k n", p=P)
                return [(b, w[:, :, job[1] * HALF:(job[1] + 1) * HALF])]
            c = {"qi": C_QI, "ckv": C_CKV, "q": C_Q, "xbc": C_XBC, "gate": C_GATE, "z": C_Z}[kind]
            c += HALF * (job[1] if len(job) > 1 else 0)
            return [(b, win[:, :, c:c + HALF])]

        landed_at, per_slot = {}, [0] * NRAW
        for n, j in enumerate(jobs):
            per_slot[n % NRAW] += 16 * len(loads(j))
            landed_at[j] = per_slot[n % NRAW]

        units = [("qi", m) for m in range(4)] + [("ki", 0)] + [("ckv", t) for t in range(2)]
        units += [("q", m) for m in range(8)] + [("k", m) for m in range(8)]
        units += [("v", n) for n in range(4)] + [("xbc", i) for i in range(24)]
        units += [("gate", m) for m in range(16)] + [("z", n) for n in range(8)]
        units += [("att", m) for m in range(8)] + [("ssm", m) for m in range(8)]
        units += [("out", n) for n in range(4)]
        unit_no = {u: n for n, u in enumerate(units)}
        units_per_bank = [0, 0]
        for n in range(len(units)):
            units_per_bank[n % 2] += 1

        def block_of(u):
            kind, n = u
            if kind in ("qi", "q", "gate", "att"):
                return (kind, n // 2)
            if kind == "xbc":
                return (kind, CONV_ORDER[n] // 2)
            return {"ki": ("small",), "ckv": ("ckv",), "k": ("uk",), "v": ("uv",),
                    "z": ("z", n // 2 * 2 + 1), "ssm": ("ssm", n // 2 * 2 + 1), "out": ("out", n // 2 * 2 + 1)}[kind]

        units_until = {block_of(u): n + 1 for n, u in enumerate(units)}
        firsts = [j for j in jobs if j not in units_until]
        first_no = {j: n for n, j in enumerate(firsts)}

        def wait_used(eng, job):
            if job in units_until:
                eng.wait_ge(unit_done, units_until[job])
            else:
                eng.wait_ge(first_used, first_no[job] + 1)

        def acc(u):
            return bank[unit_no[u] % 2]

        block_landed = [sem(f"block_landed{i}") for i in range(NRAW)]
        hi_ready = sem("hi_ready")
        lo_ready = sem("lo_ready")
        first_used = sem("first_used")
        hT_hi_ready = sem("hT_hi_ready")
        mix_sum_ready = sem("mix_sum_ready")
        mix_hi_ready = sem("mix_hi_ready")
        yT_hi_ready = sem("yT_hi_ready")
        attT_hi_ready = sem("attT_hi_ready")
        attT_lo_ready = sem("attT_lo_ready")
        x_landed = sem("x_landed")
        rows_landed = sem("rows_landed")
        vecs_landed = sem("vecs_landed")
        g_fin_landed = sem("g_fin_landed")
        x_again_landed = sem("x_again_landed")
        masks_ready = sem("masks_ready")
        iota_made = sem("iota_made")
        consts_turned = sem("consts_turned")
        consts_ready = sem("consts_ready")
        ss_ready = sem("ss_ready")
        rms_ready = sem("rms_ready")
        rs_ready = sem("rs_ready")
        xn_ready = sem("xn_ready")
        xn_turned = sem("xn_turned")
        hT_ready = sem("hT_ready")
        unit_done = sem("unit_done")
        unit_taken = [sem("unit_taken0"), sem("unit_taken1")]
        negA_ready = sem("negA_ready")
        ckv_ss_ready = sem("ckv_ss_ready")
        ckv_rms_ready = sem("ckv_rms_ready")
        c_ready = sem("c_ready")
        c_turned = sem("c_turned")
        cT_hi_ready = sem("cT_hi_ready")
        cT_ready = sem("cT_ready")
        dt_abs_ready = sem("dt_abs_ready")
        dt_exp_ready = sem("dt_exp_ready")
        dt_u_ready = sem("dt_u_ready")
        dt_ln_ready = sem("dt_ln_ready")
        dA_ready = sem("dA_ready")
        acs_done = sem("acs_done")
        eacs_ready = sem("eacs_ready")
        small_turned = sem("small_turned")
        kiT_ready = sem("kiT_ready")
        index_done = sem("index_done")
        relu_ready = sem("relu_ready")
        relu_used = sem("relu_used")
        logits_done = sem("logits_done")
        att_biased = sem("att_biased")
        exp_ready = sem("exp_ready")
        prob_ready = sem("prob_ready")
        prob_turned = sem("prob_turned")
        probT_ready = sem("probT_ready")
        pv_done = sem("pv_done")
        attT_ready = sem("attT_ready")
        first_tap_ready = sem("first_tap_ready")
        conv_ready = sem("conv_ready")
        tanh_ready = sem("tanh_ready")
        xc_ready = sem("xc_ready")
        gate_ready = sem("gate_ready")
        seg_in_ready = sem("seg_in_ready")
        seg_done = sem("seg_done")
        xs_turned = sem("xs_turned")
        xdt_ready = sem("xdt_ready")
        cb_done = sem("cb_done")
        cb_ready = sem("cb_ready")
        b_tok_ready = sem("b_tok_ready")
        decay_ready = sem("decay_ready")
        wts_ready = sem("wts_ready")
        y_diag_done = sem("y_diag_done")
        state_done = sem("state_done")
        state_ready = sem("state_ready")
        y_off_done = sem("y_off_done")
        y_ready = sem("y_ready")
        z_tanh_ready = sem("z_tanh_ready")
        y_gated = sem("y_gated")
        y_ss_ready = sem("y_ss_ready")
        y_rms_ready = sem("y_rms_ready")
        y_normed = sem("y_normed")
        y_turned = sem("y_turned")
        yT_ready = sem("yT_ready")
        mix_ready = sem("mix_ready")
        x2_ready = sem("x2_ready")
        x2_ss_ready = sem("x2_ss_ready")
        x2_rms_ready = sem("x2_rms_ready")
        rs2_ready = sem("rs2_ready")
        h2_ready = sem("h2_ready")
        x2_turned = sem("x2_turned")
        x2T_ready_a = sem("x2T_ready_a")
        x2T_ready_v = sem("x2T_ready_v")
        route_done = sem("route_done")
        route_in = sem("route_in")
        route_exp = sem("route_exp")
        onehot_ready = sem("onehot_ready")
        rank_done = sem("rank_done")
        route_ready = sem("route_ready")
        early_landed = [[sem(f"chunk{c}_landed_even"), sem(f"chunk{c}_landed_odd")] for c in range(EARLY)]
        chunk_landed = [None] * EARLY + [sem(f"chunk_landed{c}") for c in range(EARLY, CHUNKS)]
        over_turn = sem("over_turn")
        first_over_ready = sem("first_over_ready")
        over_picked = sem("over_picked")
        over_up_landed = sem("over_up_landed")
        over_down_landed = sem("over_down_landed")

        class PassSems:

            def __init__(self, kind):
                self.perm_ready = sem(f"{kind}_perm_ready")
                self.gathered = sem(f"{kind}_gathered")
                self.places_done = sem(f"{kind}_places_done")
                self.xgT_ready_a = sem(f"{kind}_xgT_ready_a")
                self.xgT_ready_v = sem(f"{kind}_xgT_ready_v")
                self.chunk_used = sem(f"{kind}_chunk_used")
                self.silu_ready = sem(f"{kind}_silu_ready")
                self.hid_ready = sem(f"{kind}_hid_ready")
                self.hid_turned = sem(f"{kind}_hid_turned")
                self.hidT_ready = sem(f"{kind}_hidT_ready")
                self.y_grp_ready = sem(f"{kind}_y_grp_ready")
                self.scattered = sem(f"{kind}_scattered")
                self.added = sem(f"{kind}_added")

        batch = PassSems("batch")
        further = PassSems("further")
        fin_ss_ready = sem("fin_ss_ready")
        fin_rms_ready = sem("fin_rms_ready")
        fin_gained = sem("fin_gained")
        out_ready_a = sem("out_ready_a")
        out_ready_v = sem("out_ready_v")
        out_stored = sem("out_stored")
        v_step = sem("v_step")
        a_step = sem("a_step")
        p_step = sem("p_step")

        class Steps:

            def __init__(self, eng, own):
                self.eng, self.own, self.n = eng, own, 0

            def __call__(self, ins):
                self.n += 1
                ins.then_inc(self.own, 1)
                self.eng.wait_ge(self.own, self.n)

        def wait_unit(eng, u):
            eng.wait_ge(unit_done, unit_no[u] + 1)

        def took(ins, u):
            ins.then_inc(unit_taken[unit_no[u] % 2], 1)

        KEYS = [(0, 128), (128, 384)]
        PAIRS = ATT_HEADS // 2
        e1_v = w_e1[0].rearrange("g e (p k) f -> (g e) p k f", k=KD)
        e3_v = w_e3[0].rearrange("g e (p k) f -> (g e) p k f", k=KD)
        e2_v = w_e2[0].rearrange("g e (k p) d -> (g e) p k d", p=P)

        def used(i, c):
            return i * CHUNKS + (c + 1)

        cw = conv_w[0].rearrange("j (m c) -> (j m) c", c=P)
        one = lambda a: a.rearrange("(m c) -> m c", c=P)
        row = lambda a, n: a.rearrange("(o n) -> o n", o=1).to_broadcast([P, n])
        ROWS = ((crow[0:96, 0, :], cw), (crow[96:120, 0, :], one(conv_b[0])),
                (crow[0:8, 1, :], one(norm_mix_g[0])), (crow[8:24, 1, :], one(ssm_norm_g[0])),
                (crow[24:40, 1, :], gate_b[0].rearrange("b (m c) -> (b m) c", c=P)),
                (crow[40:42, 1, :], one(kv_norm_g[0])), (crow[42:50, 1, :], one(norm_ffn_g[0])))
        VECS = tuple((hvec[:, i, :], row(a[0], HEADS)) for i, a in enumerate((dt_bias, a_log, d_skip)))
        VECS += ((b_route[:, 0:MG], row(b_group[0], MG)),
                 (b_route[:, MG:], row(b_router[0].rearrange("g e -> (g e)"), MG * ME)),
                 (g_ffn[:, :], norm_ffn_g[0].rearrange("(p k) -> p k", k=KD)),
                 (w_route[:, :, 0:MG], w_group[0].rearrange("(k p) g -> p k g", p=P)))
        VECS += tuple((w_route[:, :, MG + g * ME:MG + (g + 1) * ME], w_router[0, g].rearrange("(k p) e -> p k e", p=P))
                      for g in range(MG))

        block = ctx.enter_context(nc.Block())

        @block.sync
        def _(sp):
            def load_chunk(b, c, parity=0):
                four = bass.ds(b * EB, EB)
                if c < 4:
                    dst, landed = (c_early[c][parity], early_landed[c][parity]) if c < EARLY else (c_up[c], chunk_landed[c])
                    for w, src in ((0, e1_v), (1, e3_v)):
                        sp.dma_start(dst[:, w, :, :, :].rearrange("p e k f -> p e (k f)"),
                                     src[four, :, 2 * c:2 * c + 2, :].rearrange("e p k f -> p e (k f)"))\
                            .then_inc(landed, 16)
                else:
                    cols = slice((c - 4) * 512, (c - 3) * 512)
                    for k in range(2):
                        sp.dma_start(c_down[c][:, :, k, :], e2_v[four, :, k, cols].rearrange("e p d -> p e d"))\
                            .then_inc(chunk_landed[c], 16)

            for t in range(TT):
                sp.dma_start(x_in[:, t, :], x[0, t * P:(t + 1) * P, :]).then_inc(x_landed, 16)
            for n, job in enumerate(jobs):
                if n == 1:
                    for dst, src in ROWS:
                        sp.dma_start(dst, src).then_inc(rows_landed, 16)
                if n == NRAW:
                    for dst, src in VECS:
                        sp.dma_start(dst, src).then_inc(vecs_landed, 16)
                if job == ("att", 0):
                    sp.wait_ge(y_ready, 8)
                    for t in range(TT):
                        sp.dma_start(x_again[:, t, :], x[0, t * P:(t + 1) * P, :]).then_inc(x_again_landed, 16)
                if job == ("ssm", 4):
                    sp.wait_ge(unit_done, units_until[("att", 3)])
                    load_chunk(0, 0)
                if n >= NRAW:
                    last = jobs[n - NRAW]
                    sp.wait_ge(hi_ready, job_no[last] + 1)
                    sp.wait_ge(lo_ready, job_no[last] + 1)
                for dst, src in loads(job):
                    sp.dma_start(dst, src).then_inc(block_landed[n % NRAW], 16)

            sp.wait_ge(unit_done, units_until[("ssm", 7)])
            load_chunk(0, 1)
            load_chunk(0, 5)
            for c, job in ((0, ("out", 1)), (1, ("out", 3))):
                sp.wait_ge(hi_ready, job_no[job] + 1)
                sp.wait_ge(lo_ready, job_no[job] + 1)
                load_chunk(1, c, parity=1)
            sp.wait_ge(unit_done, len(units))
            for c in (2, 3, 4):
                load_chunk(0, c)

            def fill(b):
                for c in range(EARLY, CHUNKS):
                    sp.wait_ge(batch.chunk_used, used(b - 1, c))
                    load_chunk(b, c)

            def load_expert(ex):
                for dst, src in ((o_e1[0], e1_v[bass.ds(ex, 1), :, 0:4]), (o_e1[1], e1_v[bass.ds(ex, 1), :, 4:8]),
                                 (o_e3, e3_v[bass.ds(ex, 1)])):
                    sp.dma_start(dst, src.rearrange("o p k f -> p (o k) f")).then_inc(over_up_landed, 16)
                sp.dma_start(o_down, e2_v[bass.ds(ex, 1)].rearrange("o p k d -> p (o k) d")).then_inc(over_down_landed, 16)

            def early_chunks(b, parity):
                for c in range(EARLY):
                    sp.wait_ge(batch.chunk_used, used(b - 2, c))
                    load_chunk(b, c, parity)

            sp.wait_ge(first_over_ready, 1)
            over = sp.value_load(n_over_i[0:1, 0:1], min_val=0, max_val=MAX_OVER)
            more = sp.value_load(n_over_i[0:1, 1:2], min_val=0, max_val=MAX_OVER - 1)
            with sp.If(over):
                load_expert(sp.value_load(n_over_i[0:1, 2:3], min_val=0, max_val=MG * ME - 1))
            fill(1)
            for b in (2, 3):
                early_chunks(b, b % 2)
                fill(b)
            sp.wait_ge(route_ready, 1)
            with sp.If(more):
                with sp.Fori(0, more) as r:
                    ex = sp.value_load(entry_i[0:1, bass.ds(r + 1, 1)], min_val=0, max_val=MG * ME - 1)
                    sp.wait_ge(over_turn, r + 1)
                    load_expert(ex)
            with sp.Fori(0, BATCHES // 2 - 2) as r:
                for parity in range(2):
                    early_chunks(r * 2 + (4 + parity), parity)
                    fill(r * 2 + (4 + parity))
            sp.dma_start(g_fin, norm_final_g.rearrange("(o n) -> o n", o=1).to_broadcast([P, D])).then_inc(g_fin_landed, 16)
            for t in range(TT):
                sp.wait_ge((out_ready_a, out_ready_v)[t], 1)
                sp.dma_start(out[0, t * P:(t + 1) * P, :], h2[:, t, :]).then_inc(out_stored, 16)
            sp.wait_ge(out_stored, 16 * TT)

        @block.gpsimd
        def _(pool):
            pool.memset(ones[:, :], 1.0).then_inc(masks_ready, 1)
            for m in (ident, tri, below, above):
                pool.memset(m[:, :], 0.0 if m is ident else 1.0).then_inc(p_step, 1)
            pool.wait_ge(p_step, 4)
            for m, cmp, fill, mult, step in ((ident, ALU.not_equal, 1.0, 1, -1), (tri, ALU.is_ge, 0.0, -1, 1),
                                             (below, ALU.is_gt, 0.0, 1, -1), (above, ALU.is_gt, 0.0, -1, 1)):
                pool.affine_select(out=m[:, :], in_=m[:, :], compare_op=cmp, fill=fill, base=0,
                                   pattern=[[step, P]], channel_multiplier=mult).then_inc(masks_ready, 1)
            for dst, base, mult, n in ((dist[:, 0:128], 0, 1, P), (dist[:, 128:384], P, 1, S)):
                pool.iota(iota_i[:, 0:n], pattern=[[-1, n]], base=base, channel_multiplier=mult).then_inc(p_step, 1)
                pool.wait_ge(p_step, 5 if n == P else 7)
                pool.tensor_copy(dst, iota_i[:, 0:n]).then_inc(p_step, 1)
                pool.wait_ge(p_step, 6 if n == P else 8)
            pool.iota(iota_i[:, 0:P], pattern=[[1, P]], base=0, channel_multiplier=0).then_inc(p_step, 1)
            pool.wait_ge(p_step, 9)
            pool.tensor_copy(iota[:, :], iota_i[:, 0:P]).then_inc(iota_made, 1)
            for s, job in enumerate(jobs):
                pool.wait_ge(hi_ready, s + 1)
                n = KD * (N_SMALL if job[0] == "small" else HALF)
                pool.tensor_tensor(w_lo[s % 2][:, 0:n], slot(job)[:, 0:n], w_hi[s % 2][:, 0:n].bitcast(F32), ALU.subtract)\
                    .then_inc(lo_ready, 1)
                before_job = jobs[s - 1] if s else None
                if before_job is not None and before_job[0] == "gate":
                    for m in (2 * before_job[1], 2 * before_job[1] + 1):
                        i = unit_no[("gate", m)]
                        pool.wait_ge(unit_taken[i % 2], i // 2 + 1)
                        pool.tensor_scalar(gT[:, m, :], gT[:, m, :], 1.0, 0.5, ALU.add, ALU.mult).then_inc(gate_ready, 1)
            pool.wait_ge(g_fin_landed, 16)
            pool.wait_ge(batch.added, 4 * BATCHES - 1)
            pool.tensor_tensor(h2[:, 0, :], x2[:, 0, :], g_fin, ALU.mult).then_inc(fin_gained, 1)

        @block.tensor
        def _(pe):
            def three(o, job, x, w, start=True, stop=True, w_first=True, fresh=None, passes=(0, 1, 2)):
                s = job_no[job]
                tiles = 2 if job[0] in ("uk", "uv") else KD
                pe.wait_ge(hi_ready, s + 1)
                W = [columns(w_hi[s % 2], job), columns(w_lo[s % 2], job)]
                for n in passes:
                    px, pw = ((0, 0), (1, 0), (0, 1))[n]
                    if pw:
                        pe.wait_ge(lo_ready, s + 1)
                    for k in range(tiles):
                        if fresh and n < 2:
                            pe.wait_ge(fresh[px], fresh[2] + k + 1)
                        a, b = w(W[pw], k), x(px, k)
                        if not w_first:
                            a, b = b, a
                        mm = pe.matmul(o, a, b, start=(start and n == 0 and k == 0), stop=(stop and n == 2 and k == tiles - 1))
                return mm

            def begin(u):
                i = unit_no[u]
                if i >= 2:
                    pe.wait_ge(unit_taken[i % 2], i // 2)
                return bank[i % 2]

            hT = (hT_hi, hT_lo)
            yT = (yT_hi, yT_lo)

            pe.wait_ge(masks_ready, 5)
            pe.wait_ge(rows_landed, 16 * len(ROWS))
            pe.transpose(bank[7][:, 0:120], crow[0:120, 0, :], ident[0:120, 0:120])
            pe.transpose(bank[7][:, 128:178], crow[0:50, 1, :], ident[0:50, 0:50]).then_inc(consts_turned, 1)
            pe.wait_ge(xn_ready, TT)
            for j in range(4):
                for k in (2 * j, 2 * j + 1):
                    for t in range(TT):
                        c = (k % 2) * 256 + t * P
                        tr = pe.transpose(bank[2 + j][:, c:c + P], xn[:, t, k * P:(k + 1) * P], ident[:, :])
                tr.then_inc(xn_turned, 1)

            def channel_unit(u, c, fresh=None):
                three(begin(u)[:, 0:S], block_of(u), lambda p, k: hT[p][:, k, :], lambda w, k: w[:, k, c:c + P], fresh=fresh)\
                    .then_inc(unit_done, 1)

            def token_pair(kind, n, a, fresh=None, between=None):
                us = [(kind, 2 * n + t) for t in range(TT)]
                for side in range(2):
                    for t, u in enumerate(us):
                        o = begin(u) if side == 0 else acc(u)
                        mm = three(o[:, side * HALF:(side + 1) * HALF], (kind, 2 * n + side),
                                   lambda p, k: a[p][:, k, t * P:(t + 1) * P], lambda w, k: w[:, k, :], w_first=False,
                                   fresh=fresh if side == 0 and t == 0 else None)
                        if side == 1:
                            mm.then_inc(unit_done, 1)
                    if side == 0:
                        mm.then_inc(first_used, 1)
                        if between:
                            between()

            for m in range(4):
                channel_unit(("qi", m), m % 2 * P, fresh=(hT_hi_ready, hT_ready, 0) if m == 0 else None)
            channel_unit(("ki", 0), 0)
            for passes in ((0, 1), (2,)):
                for t in range(TT):
                    u = ("ckv", t)
                    mm = three(begin(u)[:, 0:LATENT], block_of(u), lambda p, k: hT[p][:, k, t * P:(t + 1) * P],
                               lambda w, k: w[:, k, :], w_first=False, passes=passes)
                    if passes[-1] == 2:
                        mm.then_inc(unit_done, 1)
            pe.wait_ge(unit_taken[0], unit_no[("ki", 0)] // 2 + 1)
            for t in range(TT):
                pe.transpose(bank[7][:, t * 64:(t + 1) * 64], smallT[64:128, t * P:(t + 1) * P], ident[64:128, 64:128])
            pe.matmul(bank[6][64:128, 0:S], ident[0:64, 0:64], smallT[0:64, :], start=True, stop=True).then_inc(small_turned, 1)
            def index_scores(m):
                if m == 0:
                    pe.wait_ge(unit_taken[1], unit_no[("qi", 3)] // 2 + 1)
                    pe.wait_ge(kiT_ready, 1)
                else:
                    pe.wait_ge(relu_ready, 2 * m)
                for t, (a, b) in enumerate(KEYS):
                    for e in range(2):
                        r = slice(64 * e, 64 * e + 64)
                        mm = pe.matmul(bank[2 + e][:, a:b], qiT[r, m, t * P:(t + 1) * P], (smallT, kiT)[e][r, 0:b - a],
                                       start=True, stop=True)
                mm.then_inc(index_done, 1)

            for m in range(8):
                channel_unit(("q", m), m % 2 * P)
                if m % 2:
                    index_scores(m // 2)
                if m == 1:
                    pe.wait_ge(c_ready, 1)
                    for r in range(2):
                        for t in range(TT):
                            c = r * 256 + t * P
                            tr = pe.transpose(bank[4][:, c:c + P], c_tok[:, t, r * P:(r + 1) * P], ident[:, :])
                    tr.then_inc(c_turned, 1)

            pe.wait_ge(dA_ready, 1)
            for t in range(TT):
                pe.matmul(bank[7][:, t * HEADS:(t + 1) * HEADS], tri[:, :], dA[:, t, :], start=True, stop=True)
            pe.matmul(bank[7][:, 64:96], below_r[:, :], dA_hi[:, 0, :], start=True, stop=False)
            pe.matmul(bank[7][:, 64:96], below_r[:, :], dA_lo[:, 0, :], start=False, stop=True).then_inc(acs_done, 1)

            pe.wait_ge(cT_ready, 2)
            cT = (cT_hi, cT_lo)
            for m in range(8):
                u = ("k", m)
                three(begin(u)[:, 0:S], block_of(u), lambda p, r: cT[p][:, r, :], lambda w, r: w[:, r, m * P:(m + 1) * P])\
                    .then_inc(unit_done, 1)
            for n in range(4):
                u, t, half = ("v", n), n // 2, n % 2
                three(begin(u)[:, :], block_of(u), lambda p, r: cT[p][:, r, t * P:(t + 1) * P],
                      lambda w, r: w[:, r, half * 512:(half + 1) * 512], w_first=False).then_inc(unit_done, 1)

            EACH = [(e, slice(64 * e, 64 * e + 64)) for e in range(2)]

            def logits(j):
                if j == 0:
                    pe.wait_ge(unit_taken[0], (unit_no[("v", 3)]) // 2 + 1)
                    pe.wait_ge(unit_taken[1], (unit_no[("v", 3)] + 1) // 2)
                    pe.wait_ge(relu_ready, IDX_HEADS)
                else:
                    pe.wait_ge(att_biased, j)
                for t, (a, b) in enumerate(KEYS):
                    for e, r in EACH:
                        mm = pe.matmul(bank[2 + e][:, a:b], qT[r, j, t * P:(t + 1) * P], kT[r, j, 0:b - a], start=True, stop=True)
                mm.then_inc(logits_done, 1)

            def turn_prob(j):
                pe.wait_ge(prob_ready, j + 1)
                if j == 0:
                    pe.wait_ge(eacs_ready, 1)
                    pe.wait_ge(cT_ready, 2)
                else:
                    pe.wait_ge(probT_ready, 2 * j)
                for e in range(2):
                    for c in range(3):
                        tr = pe.transpose(bank[4 + 3 * e][:, c * P:(c + 1) * P], prob[:, e, c * P:(c + 1) * P], ident[:, :])
                    tr.then_inc(prob_turned, 1)

            def pv(j):
                pe.wait_ge(probT_ready, 2 * j + 2)
                if j >= 2:
                    pe.wait_ge(attT_ready, j - 1)
                o = bank[5 + j % 2]
                for e, r in EACH:
                    pe.matmul(o[r, 0:S], v_tok[:, 0, (2 * j + e) * HD:(2 * j + e + 1) * HD], probT[:, e, 0:256],
                              start=True, stop=False)
                for e, r in EACH:
                    mm = pe.matmul(o[r, P:S], v_tok[:, 1, (2 * j + e) * HD:(2 * j + e + 1) * HD], probT[:, e, 256:384],
                                   start=False, stop=True)
                mm.then_inc(pv_done, 1)

            for j in range(12):
                for i in (2 * j, 2 * j + 1):
                    channel_unit(("xbc", i), i % 2 * P)
                    if i % 2 == 0:
                        if 1 <= j <= PAIRS:
                            turn_prob(j - 1)
                        if j < PAIRS:
                            logits(j)
                    elif 1 <= j <= PAIRS:
                        pv(j - 1)

            def ssd_a(q):
                c, g = q // GROUPS, q % GROUPS
                ts = slice(c * P, (c + 1) * P)
                if q == 0:
                    pe.wait_ge(xc_ready, 24)
                    pe.wait_ge(attT_ready, PAIRS)
                if q >= 1:
                    pe.wait_ge(xdt_ready, q)
                for j in range(4):
                    tr = pe.transpose(bank[5][:, j * P:(j + 1) * P], xcT[:, 4 * g + j, ts], ident[:, :])
                tr.then_inc(xs_turned, 1)
                if q >= 1:
                    pe.wait_ge(cb_ready, q)
                    if c == 0:
                        pe.wait_ge(b_tok_ready, q)
                if c == 0:
                    pe.transpose(bank[4][:, 256:384], xcT[:, 16 + g, ts], ident[:, :])
                pe.matmul(bank[4][:, 0:P], xcT[:, 16 + g, ts], xcT[:, 20 + g, ts], start=True, stop=True)\
                    .then_inc(cb_done, 1)
                pe.wait_ge(seg_in_ready, q + 1)
                if q >= 1:
                    pe.wait_ge(decay_ready, q)
                for j in range(2):
                    for part in range(2):
                        mm = pe.matmul(bank[2 + j][:, :], below_r[:, :], seg_in[part][:, j * 512:(j + 1) * 512],
                                       start=(part == 0), stop=(part == 1))
                mm.then_inc(seg_done, 1)

            def ssd_b(q):
                c, g = q // GROUPS, q % GROUPS
                pe.wait_ge(wts_ready, q + 1)
                if q >= 1:
                    pe.wait_ge(y_ready, q)
                for h in range(HPG):
                    col = (g * HPG + h) * HD
                    mm = pe.matmul(bank[6][:, h * HD:(h + 1) * HD], decay[:, h * P:(h + 1) * P],
                                   xdt3[:, c, col:col + HD], start=True, stop=True)
                mm.then_inc(y_diag_done, 1)
                if c == 0:
                    pe.wait_ge(b_tok_ready, q + 1)
                    if q >= 1:
                        pe.wait_ge(state_ready, q)
                    pe.matmul(bank[7][:, :], cbm[:, 1, :], xdec, start=True, stop=True).then_inc(state_done, 1)
                else:
                    pe.wait_ge(state_ready, GROUPS)
                    pe.matmul(bank[7][:, :], xcT[:, 20 + g, P:S], stateT[:, g, :], start=True, stop=True)\
                        .then_inc(y_off_done, 1)

            for m in range(16):
                channel_unit(("gate", m), m % 2 * P)
                ssd_a(m // 2) if m % 2 == 0 else ssd_b(m // 2)

            for g in range(GROUPS):
                token_pair("z", g, hT)

            def turn_y(j):
                pe.wait_ge(y_normed, j // 2 * 2 + 2)
                if j >= 2:
                    pe.wait_ge(yT_ready, 2 * (j - 1))
                for m in (2 * j, 2 * j + 1):
                    for t in range(TT):
                        c = (m % 2) * 256 + t * P
                        tr = pe.transpose(bank[2 + j % 2][:, c:c + P], y[:, t, m * P:(m + 1) * P], ident[:, :])
                tr.then_inc(y_turned, 1)

            pe.wait_ge(attT_lo_ready, 1)
            for m in range(8):
                u = ("att", m)
                three(begin(u)[:, 0:S], block_of(u), lambda p, k: (attT_hi, attT_lo)[p][:, k, :],
                      lambda w, k: w[:, k, m % 2 * P:(m % 2 + 1) * P]).then_inc(unit_done, 1)
                if m >= 1:
                    turn_y(m - 1)
            turn_y(7)
            for n in range(4):
                for kh in range(2):
                    for m in (2 * n, 2 * n + 1):
                        u = ("ssm", m)
                        o = begin(u) if kh == 0 else acc(u)
                        mm = three(o[:, 0:S], ("ssm", 2 * n + kh), lambda p, k: yT[p][:, kh * 8 + k, :],
                                   lambda w, k: w[:, k, m % 2 * P:(m % 2 + 1) * P], start=(kh == 0), stop=(kh == 1),
                                   fresh=(yT_hi_ready, yT_ready, kh * 8) if m == 0 else None)
                        if kh == 1:
                            mm.then_inc(unit_done, 1)
                    if kh == 0:
                        mm.then_inc(first_used, 1)
            def turn_x2(half):
                pe.wait_ge(x2_ready, 2 * half + 2)
                for j in range(2):
                    if half:
                        pe.wait_ge((x2T_ready_a, x2T_ready_v)[j], 2)
                    for k in (4 * half + 2 * j, 4 * half + 2 * j + 1):
                        for t in range(TT):
                            c = (k % 2) * 256 + t * P
                            tr = pe.transpose(bank[2 + j][:, c:c + P], x2[:, t, k * P:(k + 1) * P], ident[:, :])
                    tr.then_inc(x2_turned, 1)

            def route(half):
                pe.wait_ge(x2T_ready_a, 2 * half + 2)
                pe.wait_ge(x2T_ready_v, 2 * half + 2)
                for t in range(TT):
                    for k in range(4 * half, 4 * half + 4):
                        mm = pe.matmul(bank[6 + t][:, 0:MG + MG * ME], x2T[:, k, t * P:(t + 1) * P], w_route[:, k, :],
                                       start=(k == 0), stop=(k == KD - 1))
                return mm

            token_pair("out", 0, hT, fresh=(mix_hi_ready, mix_ready, 0))
            token_pair("out", 1, hT, between=lambda: turn_x2(0))
            pe.wait_ge(vecs_landed, 16 * len(VECS))
            route(0)
            turn_x2(1)
            route(1).then_inc(route_done, 1)
            pe.wait_ge(onehot_ready, 1)
            NE = MG * ME
            oh = rt[:, 288:352].rearrange("p (t e) -> p t e", t=TT)
            pe.matmul(bank[6][:, 0:NE], above[:, :], oh[:, 0, :], start=True, stop=True)
            pe.matmul(bank[6][:, NE:2 * NE], above[:, :], oh[:, 1, :], start=True, stop=False)
            pe.matmul(bank[6][:, NE:2 * NE], ones[:, :], oh[:, 0, :], start=False, stop=True)
            pe.matmul(bank[6][:, 2 * NE:3 * NE], ones[:, :], oh[:, 0, :], start=True, stop=False)
            pe.matmul(bank[6][:, 2 * NE:3 * NE], ones[:, :], oh[:, 1, :], start=False, stop=True).then_inc(rank_done, 1)

            pe.wait_ge(h2_ready, TT)

            def places(q, i):
                pe.wait_ge(q.perm_ready, i * 2 + 1)
                for k in range(KD):
                    c = (k % 4) * P
                    for t in range(TT):
                        mm = pe.matmul(bank[1 + k // 4][:, c:c + P], h2[:, t, k:D:KD], perm[:, t, :],
                                       start=(t == 0), stop=(t == TT - 1))
                    if k % 4 == 3:
                        mm.then_inc(q.gathered, 1)
                pe.wait_ge(q.perm_ready, i * 2 + 2)
                for t in range(TT):
                    tr = pe.transpose(bank[7][:, t * P:(t + 1) * P], pgate[:, t, :], ident[:, :])
                tr.then_inc(q.places_done, 1)
                pe.wait_ge(q.xgT_ready_a, i + 1)
                pe.wait_ge(q.xgT_ready_v, i + 1)

            def turn_hid(q, i):
                pe.wait_ge(q.hid_ready, i + 1)
                for f in range(2):
                    tr = pe.transpose(bank[2][:, f * P:(f + 1) * P], hid[:, f * P:(f + 1) * P], ident[:, :])
                tr.then_inc(q.hid_turned, 1)
                pe.wait_ge(q.hidT_ready, i + 1)

            def scatter(q, i, half):
                pe.wait_ge(q.y_grp_ready, i * 2 + (half + 1))
                for t in range(TT):
                    if half:
                        pe.wait_ge(q.added, i * 4 + (t + 1))
                    pe.matmul(bank[3 + t][:, :], gateT[:, t, :], y_grp[:, half * 512:(half + 1) * 512],
                              start=True, stop=True).then_inc(q.scattered, 1)

            def batch_pass(i, parity, nth):
                places(batch, i)
                for c in range(4):
                    if c < EARLY:
                        pe.wait_ge(early_landed[c][parity], nth * 32 + 32)
                    else:
                        pe.wait_ge(chunk_landed[c], i * 32 + 32)
                    w = c_early[c][parity] if c < EARLY else c_up[c]
                    for k in (2 * c, 2 * c + 1):
                        for e in range(EB):
                            r = slice(e * PLACES, (e + 1) * PLACES)
                            mm = pe.matmul(bank[0][r, :].rearrange("p (w f) -> p w f", w=2), xgT[:, k, r],
                                           w[:, :, e, k % 2, :], start=(k == 0), stop=(k == KD - 1))
                    mm.then_inc(batch.chunk_used, 1)
                turn_hid(batch, i)
                for half in range(2):
                    c = 4 + half
                    pe.wait_ge(chunk_landed[c], i * 32 + 32)
                    for f in range(2):
                        for e in range(EB):
                            r = slice(e * PLACES, (e + 1) * PLACES)
                            mm = pe.matmul(bank[5 + half][r, :], hidT[:, f, r], c_down[c][:, e, f, :],
                                           start=(f == 0), stop=(f == 1))
                    mm.then_inc(batch.chunk_used, 1)
                for half in range(2):
                    scatter(batch, i, half)

            for b in range(3):
                batch_pass(b, b % 2, b // 2)
            pe.wait_ge(route_ready, 1)
            over = pe.value_load(n_over_i[0:1, 0:1], min_val=0, max_val=MAX_OVER)
            with pe.If(over):
                with pe.Fori(0, over) as i:
                    places(further, i)
                    pe.wait_ge(over_up_landed, i * 48 + 48)
                    for w in range(2):
                        for k in range(KD):
                            mm = pe.matmul(bank[0][:, w * FF:(w + 1) * FF], xgT[:, k, :], o_e3[:, k, :] if w else o_e1[k // 4][:, k % 4, :],
                                           start=(k == 0), stop=(k == KD - 1))
                    mm.then_inc(further.chunk_used, 1)
                    turn_hid(further, i)
                    pe.wait_ge(over_down_landed, i * 16 + 16)
                    for half in range(2):
                        for f in range(2):
                            mm = pe.matmul(bank[5 + half][:, :], hidT[:, f, :], o_down[:, f, half * 512:(half + 1) * 512],
                                           start=(f == 0), stop=(f == 1))
                        mm.then_inc(further.chunk_used, 1)
                        scatter(further, i, half)
            batch_pass(3, 1, 1)
            with pe.Fori(0, BATCHES // 2 - 2) as r:
                batch_pass(r * 2 + 4, 0, r + 2)
                batch_pass(r * 2 + 5, 1, r + 2)

        @block.scalar
        def _(act):
            step = Steps(act, a_step)
            A = nc.scalar.activation
            made = [0]

            def split_to(job):
                while made[0] <= job_no[job]:
                    n = made[0]
                    act.wait_ge(block_landed[job_no[jobs[n]] % NRAW], landed_at[jobs[n]])
                    if n >= 2:
                        wait_used(act, jobs[n - 2])
                        act.wait_ge(lo_ready, n - 1)
                    c = KD * (N_SMALL if jobs[n][0] == "small" else HALF)
                    A(w_hi[n % 2][:, 0:c], slot(jobs[n])[:, 0:c], ACT.Copy).then_inc(hi_ready, 1)
                    made[0] += 1

            def split_for(u):
                split_to(jobs[job_no[block_of(u)] + 1])

            act.wait_ge(x_landed, 32)
            A(xn[:, 0, :], x_in[:, 0, :], ACT.Square, accum_out=st[:, 0:1]).then_inc(ss_ready, 1)
            act.wait_ge(ss_ready, TT + 1)
            A(st[:, 2:4], st[:, 0:2], ACT.Sqrt, bias=st[:, 63:64], scale=1.0 / D).then_inc(rms_ready, 1)
            act.wait_ge(rs_ready, 1)
            A(xn[:, 0, :], x_in[:, 0, :], ACT.Copy, scale=st[:, 2:3]).then_inc(xn_ready, 1)
            split_to(("qi", 0))
            act.wait_ge(consts_ready, 1)
            for j in range(4):
                act.wait_ge(xn_turned, j + 1)
                for k in (2 * j, 2 * j + 1):
                    c = (k % 2) * 256
                    A(hT_hi[:, k, :], bank[2 + j][:, c:c + S], ACT.Copy, scale=g_mix(k)).then_inc(hT_hi_ready, 1)

            for u in [("qi", m) for m in range(4)] + [("ki", 0)]:
                split_for(u)
                wait_unit(act, u)
                took(A(qiT[:, u[1], :] if u[0] == "qi" else smallT, acc(u)[:, 0:S], ACT.Copy), u)
            split_for(("ckv", 1))
            split_for(("q", 0))
            act.wait_ge(small_turned, 1)
            A(kiT[64:128, :], bank[6][64:128, 0:S], ACT.Copy).then_inc(kiT_ready, 1)
            act.wait_ge(ckv_ss_ready, TT)
            A(st[:, 6:8], st[:, 4:6], ACT.Sqrt, bias=st[:, 63:64], scale=1.0 / LATENT).then_inc(ckv_rms_ready, 1)
            act.wait_ge(vecs_landed, 16 * len(VECS))
            step(A(hvec[:, 1, :], hvec[:, 1, :], ACT.Exp))
            nc.scalar.mul(hvec[:, 1, :], hvec[:, 1, :], -1.0).then_inc(negA_ready, 1)
            act.wait_ge(dt_abs_ready, 1)
            A(sp_t[:, 1, :, :], sp_t[:, 1, :, :], ACT.Exp, scale=-1.0).then_inc(dt_exp_ready, 1)
            act.wait_ge(dt_u_ready, 1)
            A(sp_t[:, 3, :, :], sp_t[:, 2, :, :], ACT.Ln).then_inc(dt_ln_ready, 1)
            for m in range(8):
                u = ("q", m)
                split_for(u)
                wait_unit(act, u)
                took(A(qT[:, m, :], acc(u)[:, 0:S], ACT.Copy, scale=HD ** -0.5), u)
                if m % 2:
                    for h in (m - 1, m):
                        act.wait_ge(index_done, m // 2 + 1)
                        if h >= 2:
                            act.wait_ge(relu_used, h - 1)
                        A(relu[:, h % 2, :], bank[2 + h % 2][:, 0:384], ACT.Relu, scale=HD ** -0.5).then_inc(relu_ready, 1)
                if m == 1:
                    act.wait_ge(c_turned, 1)
                    for r in range(2):
                        A(cT_hi[:, r, :], bank[4][:, r * 256:(r + 1) * 256], ACT.Copy, scale=g_kv(r)).then_inc(cT_hi_ready, 1)
            for m in range(8):
                u = ("k", m)
                split_for(u)
                wait_unit(act, u)
                took(A(kT[:, m, :], acc(u)[:, 0:S], ACT.Copy), u)
            for n in range(4):
                u = ("v", n)
                split_for(u)
                wait_unit(act, u)
                took(A(v_tok[:, n // 2, n % 2 * 512:(n % 2 + 1) * 512], acc(u)[:, :], ACT.Copy), u)

            split_to(jobs[job_no[block_of(("xbc", 0))] + 1])
            act.wait_ge(acs_done, 1)
            A(eacs[:, :, :].rearrange("p t h -> p (t h)"), bank[7][:, 0:64], ACT.Exp)
            A(dec[:, :], bank[7][:, 64:96], ACT.Exp).then_inc(eacs_ready, 1)

            def tanh_of(i):
                act.wait_ge(conv_ready, i + 1)
                if i >= 2:
                    act.wait_ge(xc_ready, i - 1)
                A(th[:, i % 2, 0:S], xcT[:, CONV_ORDER[i], :], ACT.Tanh).then_inc(tanh_ready, 1)

            def first_tap(i):
                m = CONV_ORDER[i]
                wait_unit(act, ("xbc", i))
                A(xcT[:, m, :], acc(("xbc", i))[:, 0:S], ACT.Identity, bias=conv_bias(m), scale=tap(3, m))\
                    .then_inc(first_tap_ready, 1)

            for j in range(13):
                if j < 12:
                    first_tap(2 * j)
                if 1 <= j <= PAIRS:
                    if j >= 2:
                        act.wait_ge(pv_done, j - 1)
                    for e in range(2):
                        act.wait_ge(prob_turned, 2 * (j - 1) + e + 1)
                        A(probT[:, e, :], bank[4 + 3 * e][:, 0:384], ACT.Copy).then_inc(probT_ready, 1)
                if j >= 1:
                    tanh_of(2 * j - 1)
                if j == 12:
                    break
                tanh_of(2 * j)
                if j < PAIRS:
                    act.wait_ge(att_biased, j + 1)
                    for e in range(2):
                        for t, (a, b) in enumerate(KEYS):
                            c = 8 + 2 * e + t
                            A(prob[:, e, a:b], prob[:, e, a:b], ACT.Exp, bias=st[:, c:c + 1], scale=-1.0,
                              accum_out=st[:, c + 8:c + 9]).then_inc(exp_ready, 1)
                first_tap(2 * j + 1)
                split_to(jobs[job_no[block_of(("xbc", 2 * j))] + 2])
                if 1 <= j <= PAIRS:
                    act.wait_ge(pv_done, j)
                    A(attT[:, j - 1, :], bank[5 + (j - 1) % 2][:, 0:S], ACT.Copy).then_inc(attT_ready, 1)

            for m in range(16):
                u = ("gate", m)
                split_for(u)
                wait_unit(act, u)
                ins = A(gT[:, m, :], acc(u)[:, 0:S], ACT.Tanh, bias=b_gate(m), scale=0.5)
                took(ins, u)
                q = m // 2
                if m % 2 == 0:
                    act.wait_ge(seg_done, q + 1)
                    if q >= 1:
                        act.wait_ge(y_diag_done, q)
                    for j in range(2):
                        ins = A(decay[:, j * 512:(j + 1) * 512], bank[2 + j][:, :], ACT.Exp)
                    ins.then_inc(decay_ready, 1)
                elif q < GROUPS:
                    act.wait_ge(state_done, q + 1)
                    A(stateT[:, q, :], bank[7][:, :], ACT.Copy).then_inc(state_ready, 1)

            split_to(("z", 1))
            split_to(("z", 2))
            for n in range(8):
                g, t = n // 2, n % 2
                wait_unit(act, ("z", n))
                if n >= 2:
                    act.wait_ge(y_gated, n - 1)
                A(th[:, n % 2, :], acc(("z", n))[:, :], ACT.Tanh, scale=0.5).then_inc(z_tanh_ready, 1)
                if t == 1:
                    split_to(("z", n + 2) if n < 7 else ("att", 1))
                act.wait_ge(y_gated, n + 1)
                A(y_off, y[:, t, g * 512:(g + 1) * 512], ACT.Square, accum_out=st[:, 24 + n:25 + n])\
                    .then_inc(y_ss_ready, 1)
                if t == 1 and n < 5:
                    split_to(("z", n + 3))
                if n == 3:
                    act.wait_ge(y_ready, 8)
                    A(attT_hi[:, :, :], attT[:, :, :], ACT.Copy).then_inc(attT_hi_ready, 1)
                if n in (5, 7):
                    a, b = (0, 6) if n == 5 else (6, 8)
                    act.wait_ge(y_ss_ready, b)
                    A(st[:, 32 + a:32 + b], st[:, 24 + a:24 + b], ACT.Sqrt, bias=st[:, 63:64], scale=1.0 / 512)\
                        .then_inc(y_rms_ready, 1)
                if n == 5:
                    split_to(("att", 0))
            for j in range(8):
                split_to(jobs[job_no[("att", 0)] + (j + 1) // 2 + 1])
                act.wait_ge(y_turned, j + 1)
                for m in (2 * j, 2 * j + 1):
                    c = (m % 2) * 256
                    A(yT_hi[:, m, :], bank[2 + j % 2][:, c:c + S], ACT.Copy, scale=g_ssm(m)).then_inc(yT_hi_ready, 1)
            for n in range(4):
                split_to(("ssm", 2 * n + 2) if n < 3 else ("out", 0))
                for m in (2 * n, 2 * n + 1):
                    act.wait_ge(mix_sum_ready, m + 1)
                    A(hT_hi[:, m, :], gT[:, 8 + m, :], ACT.Copy).then_inc(mix_hi_ready, 1)
                    if m == 2 * n:
                        if n < 3:
                            split_to(("ssm", 2 * n + 3))
            split_to(("out", 1))
            split_to(("out", 3))

            def x2T_half(half):
                act.wait_ge(x2_turned, 2 * half + 1)
                for k in (4 * half, 4 * half + 1):
                    c = (k % 2) * 256
                    A(x2T[:, k, :], bank[2][:, c:c + S], ACT.Copy, scale=g_ffn_k(k)).then_inc(x2T_ready_a, 1)

            for half in range(2):
                cols = slice(half * 512, (half + 1) * 512)
                for t in range(TT):
                    act.wait_ge(x2_ready, 2 * half + t + 1)
                    A(h2[:, t, cols], x2[:, t, cols], ACT.Square, accum_out=st[:, 40 + 2 * half + t:41 + 2 * half + t])\
                        .then_inc(x2_ss_ready, 1)
                x2T_half(half)
            act.wait_ge(x2_ss_ready, 5)
            A(st[:, 46:48], st[:, 44:46], ACT.Sqrt, bias=st[:, 63:64], scale=1.0 / D).then_inc(x2_rms_ready, 1)
            act.wait_ge(rs2_ready, 1)
            for t in range(TT):
                A(h2[:, t, :], x2[:, t, :], ACT.Copy, scale=st[:, 46 + t:47 + t]).then_inc(h2_ready, 1)
            act.wait_ge(route_in, 1)
            A(rt[:, 72:80], rt[:, 72:80], ACT.Exp)
            A(rt[:, 460:462], rt[:, 460:462], ACT.Exp).then_inc(route_exp, 1)

            def moe_pass(q, i, up_value, down_value):
                act.wait_ge(q.gathered, i * 2 + 1)
                for k in range(4):
                    ins = A(xgT[:, k, :], bank[1][:, k * P:(k + 1) * P], ACT.Copy, scale=g_ffn[:, k:k + 1])
                ins.then_inc(q.xgT_ready_a, 1)
                act.wait_ge(q.places_done, i + 1)
                A(gateT[:, :, :].rearrange("p t s -> p (t s)"), bank[7][:, 0:2 * P], ACT.Copy)
                act.wait_ge(q.chunk_used, up_value)
                A(sil, bank[0][:, 0:FF], ACT.Silu).then_inc(q.silu_ready, 1)
                act.wait_ge(q.hid_turned, i + 1)
                A(hidT.rearrange("p f s -> p (f s)"), bank[2][:, 0:2 * P], ACT.Copy).then_inc(q.hidT_ready, 1)
                for half in range(2):
                    act.wait_ge(q.chunk_used, down_value + half)
                    A(y_grp[:, half * 512:(half + 1) * 512], bank[5 + half][:, :], ACT.Copy).then_inc(q.y_grp_ready, 1)

            for b in range(3):
                moe_pass(batch, b, used(b, 3), used(b, 4))
            act.wait_ge(route_ready, 1)
            over = act.value_load(n_over_i[0:1, 0:1], min_val=0, max_val=MAX_OVER)
            with act.If(over):
                with act.Fori(0, over) as i:
                    moe_pass(further, i, i * 3 + 1, i * 3 + 2)
            with act.Fori(0, BATCHES - 3) as r:
                moe_pass(batch, r + 3, used(r + 3, 3), used(r + 3, 4))
            act.wait_ge(fin_ss_ready, TT)
            A(st[:, 50:52], st[:, 48:50], ACT.Sqrt, bias=st[:, 63:64], scale=1.0 / D).then_inc(fin_rms_ready, 1)
            act.wait_ge(fin_rms_ready, 2)
            act.wait_ge(fin_gained, 1)
            A(h2[:, 0, :], h2[:, 0, :], ACT.Copy, scale=st[:, 50:51]).then_inc(out_ready_a, 1)

        @block.vector
        def _(dve):
            v = nc.vector
            step = Steps(dve, v_step)
            v.memset(st[:, 63:64], EPS).then_inc(ss_ready, 1)

            dve.wait_ge(x_landed, 32)
            v.tensor_tensor_reduce(out=xn[:, 1, :], in0=x_in[:, 1, :], in1=x_in[:, 1, :], scale=1.0, scalar=0.0,
                                   op0=ALU.mult, op1=ALU.add, accum_out=st[:, 1:2]).then_inc(ss_ready, 1)
            dve.wait_ge(rms_ready, 1)
            v.reciprocal(st[:, 2:4], st[:, 2:4]).then_inc(rs_ready, 1)
            dve.wait_ge(rs_ready, 1)
            v.tensor_scalar(xn[:, 1, :], x_in[:, 1, :], st[:, 3:4], None, ALU.mult).then_inc(xn_ready, 1)
            dve.wait_ge(consts_turned, 1)
            v.tensor_scalar(ccol[:, 0, 0:120], bank[7][:, 0:120], 0.5, None, ALU.mult)
            step(v.tensor_copy(ccol[:, 1, 0:50], bank[7][:, 128:178]))
            v.tensor_scalar(ccol[:, 1, 24:40], ccol[:, 1, 24:40], 0.5, None, ALU.mult).then_inc(consts_ready, 1)
            dve.wait_ge(consts_ready, 1)

            for j in range(4):
                dve.wait_ge(hT_hi_ready, 2 * j + 2)
                for k in (2 * j, 2 * j + 1):
                    c = (k % 2) * 256
                    v.scalar_tensor_tensor(out=hT_lo[:, k, :], in0=bank[2 + j][:, c:c + S], scalar=g_mix(k),
                                           in1=hT_hi[:, k, :].bitcast(F32), op0=ALU.mult, op1=ALU.subtract)\
                        .then_inc(hT_ready, 1)

            dve.wait_ge(iota_made, 1)
            v.tensor_copy(below_r[:, :], below)
            step(v.scalar_tensor_tensor(out=dist, in0=dist, scalar=-1.0, in1=dist, op0=ALU.mult, op1=ALU.max))

            dve.wait_ge(vecs_landed, 16 * len(VECS))
            for t in range(TT):
                u = ("ckv", t)
                wait_unit(dve, u)
                took(v.tensor_copy(c_tok[:, t, :], acc(u)[:, 0:LATENT]), u)
                dve.wait_ge(unit_taken[unit_no[u] % 2], unit_no[u] // 2 + 1)
                v.tensor_tensor_reduce(out=bias[:, 0:256], in0=c_tok[:, t, :], in1=c_tok[:, t, :], scale=1.0, scalar=0.0,
                                       op0=ALU.mult, op1=ALU.add, accum_out=st[:, 4 + t:5 + t]).then_inc(ckv_ss_ready, 1)
            dve.wait_ge(small_turned, 1)
            small = bank[7][:, 0:P].rearrange("p (t n) -> p t n", t=TT)
            v.tensor_scalar(wi[:, :, :], small[:, :, 0:IDX_HEADS], IDX_HEADS ** -0.5, None, ALU.mult)
            step(v.tensor_tensor(sp_t[:, 0, :, :], small[:, :, S_DT - S_WI:],
                                 hvec[:, 0, :].unsqueeze(1).to_broadcast([P, TT, HEADS]), ALU.add))
            v.scalar_tensor_tensor(out=sp_t[:, 1, :, :], in0=sp_t[:, 0, :, :], scalar=-1.0, in1=sp_t[:, 0, :, :],
                                   op0=ALU.mult, op1=ALU.max).then_inc(dt_abs_ready, 1)
            dve.wait_ge(ckv_rms_ready, 1)
            step(v.reciprocal(st[:, 6:8], st[:, 6:8]))
            for t in range(TT):
                ins = v.tensor_scalar(c_tok[:, t, :], c_tok[:, t, :], st[:, 6 + t:7 + t], None, ALU.mult)
            ins.then_inc(c_ready, 1)
            dve.wait_ge(dt_exp_ready, 1)
            v.tensor_scalar(sp_t[:, 2, :, :], sp_t[:, 1, :, :], 1.0, None, ALU.add).then_inc(dt_u_ready, 1)
            dve.wait_ge(dt_u_ready, 1)
            step(v.tensor_scalar(dt[:, :, :], sp_t[:, 2, :, :], 1.0, None, ALU.subtract))
            step(v.tensor_tensor(sp_t[:, 1, :, :], sp_t[:, 1, :, :], dt[:, :, :], ALU.subtract))
            step(v.reciprocal(dt[:, :, :], sp_t[:, 2, :, :]))
            step(v.tensor_tensor(sp_t[:, 1, :, :], sp_t[:, 1, :, :], dt[:, :, :], ALU.mult))
            step(v.scalar_tensor_tensor(out=sp_t[:, 1, :, :], in0=sp_t[:, 0, :, :], scalar=0.0, in1=sp_t[:, 1, :, :],
                                        op0=ALU.max, op1=ALU.add))
            dve.wait_ge(dt_ln_ready, 1)
            step(v.tensor_tensor(dt[:, :, :], sp_t[:, 1, :, :], sp_t[:, 3, :, :], ALU.add))
            dve.wait_ge(negA_ready, 1)
            for t in range(TT):
                ins = v.tensor_tensor(dA[:, t, :], dt[:, t, :], hvec[:, 1, :], ALU.mult)
            step(ins)
            step(v.tensor_copy(dA_hi[:, :, :], dA[:, :, :]))
            v.tensor_tensor(dA_lo[:, :, :], dA[:, :, :], dA_hi[:, :, :].bitcast(F32), ALU.subtract).then_inc(dA_ready, 1)
            dve.wait_ge(dA_ready, 1)

            dve.wait_ge(cT_hi_ready, 2)
            for r in range(2):
                v.scalar_tensor_tensor(out=cT_lo[:, r, :], in0=bank[4][:, r * 256:(r + 1) * 256], scalar=g_kv(r),
                                       in1=cT_hi[:, r, :].bitcast(F32), op0=ALU.mult, op1=ALU.subtract).then_inc(cT_ready, 1)

            score = sel_work
            for h in range(IDX_HEADS):
                dve.wait_ge(relu_ready, h + 1)
                for t, (a, b) in enumerate(KEYS):
                    if h == 0:
                        ins = v.tensor_scalar(score[:, a:b], relu[:, 0, a:b], wi[:, t, 0:1], None, ALU.mult)
                    else:
                        ins = v.scalar_tensor_tensor(out=score[:, a:b], in0=relu[:, h % 2, a:b],
                                                     scalar=wi[:, t, h:h + 1], in1=score[:, a:b],
                                                     op0=ALU.mult, op1=ALU.add)
                ins.then_inc(relu_used, 1)
                dve.wait_ge(relu_used, h + 1)
            v.memset(score[0:64, 64:128], LEAST)
            step(v.memset(score[0:64, 320:384], LEAST))
            for r in range(TOPK // 8):
                for t, (a, b) in enumerate(KEYS):
                    ins = v.max(top8[:, t, :], score[:, a:b])
                step(ins)
                for t, (a, b) in enumerate(KEYS):
                    ins = v.match_replace(score[:, a:b], top8[:, t, :], score[:, a:b], TAKEN)
                step(ins)
            step(v.tensor_scalar(unsel, score, TAKEN / 1.5, LEAST, ALU.is_gt, ALU.mult))

            def make_bias(j):
                if j:
                    dve.wait_ge(att_biased, j)
                else:
                    dve.wait_ge(c_turned, 1)
                for e in range(2):
                    slope = 2.0 ** (-8.0 * (2 * j + e + 1) / ATT_HEADS)
                    ins = v.scalar_tensor_tensor(out=bias2[e], in0=dist, scalar=-slope, in1=unsel, op0=ALU.mult, op1=ALU.add)
                step(ins)

            def bias_logits(j):
                dve.wait_ge(logits_done, j + 1)
                for e in range(2):
                    for t, (a, b) in enumerate(KEYS):
                        c = 8 + 2 * e + t
                        ins = v.tensor_tensor_reduce(out=prob[:, e, a:b], in0=bank[2 + e][:, a:b], in1=bias2[e][:, a:b],
                                                     scale=-1.0, scalar=3e38, op0=ALU.add, op1=ALU.min,
                                                     accum_out=st[:, c:c + 1])
                ins.then_inc(att_biased, 1)

            def scale_prob(j):
                dve.wait_ge(exp_ready, 4 * j + 4)
                step(v.reciprocal(st[:, 16:20], st[:, 16:20]))
                for e in range(2):
                    for t, (a, b) in enumerate(KEYS):
                        c = 16 + 2 * e + t
                        ins = v.tensor_scalar(prob[:, e, a:b], prob[:, e, a:b], st[:, c:c + 1], None, ALU.mult)
                ins.then_inc(prob_ready, 1)

            def other_taps(i):
                m = CONV_ORDER[i]
                u = ("xbc", i)
                dve.wait_ge(first_tap_ready, i + 1)
                for d in range(1, TAPS):
                    ins = v.scalar_tensor_tensor(out=xcT[:, m, d:S], in0=acc(u)[:, 0:S - d], scalar=tap(3 - d, m),
                                                 in1=xcT[:, m, d:S], op0=ALU.mult, op1=ALU.add)
                    if d < TAPS - 1:
                        step(ins)
                took(ins, u)
                dve.wait_ge(unit_taken[unit_no[u] % 2], unit_no[u] // 2 + 1)
                dve.sem_inc(conv_ready, 1)

            def silu_of(i):
                m = CONV_ORDER[i]
                dve.wait_ge(tanh_ready, i + 1)
                v.scalar_tensor_tensor(out=xcT[:, m, :], in0=th[:, i % 2, 0:S], scalar=1.0, in1=xcT[:, m, :],
                                       op0=ALU.add, op1=ALU.mult).then_inc(xc_ready, 1)

            def bcast(a, n):
                return a.unsqueeze(2).to_broadcast([P, HPG, n])

            def make_seg_in(q):
                c, g = q // GROUPS, q % GROUPS
                for part, a in enumerate((dA_hi, dA_lo)):
                    ins = v.tensor_tensor(seg_in[part][:, :].rearrange("p (h l) -> p h l", h=HPG),
                                          tri[:, :].unsqueeze(1).to_broadcast([P, HPG, P]),
                                          bcast(a[:, c, g * HPG:(g + 1) * HPG].bitcast(F32), P), ALU.mult)
                ins.then_inc(seg_in_ready, 1)

            make_bias(0)
            for j in range(12):
                if j == PAIRS + 2:
                    dve.wait_ge(attT_ready, PAIRS)
                    make_seg_in(0)
                other_taps(2 * j)
                if j < PAIRS:
                    bias_logits(j)
                if j >= 1:
                    silu_of(2 * j - 1)
                if j + 1 < PAIRS:
                    make_bias(j + 1)
                if j < PAIRS:
                    scale_prob(j)
                other_taps(2 * j + 1)
                silu_of(2 * j)
            silu_of(23)

            for q in range(8):
                c, g = q // GROUPS, q % GROUPS
                hs = slice(g * HPG, (g + 1) * HPG)
                cols = slice(g * 512, (g + 1) * 512)
                src = bank[5][:, :].rearrange("p (h d) -> p h d", h=HPG)
                dve.wait_ge(xs_turned, q + 1)
                if q == 0:
                    dve.wait_ge(eacs_ready, 1)
                v.tensor_tensor(y[:, c, cols].rearrange("p (h d) -> p h d", h=HPG), src, bcast(hvec[:, 2, hs], HD), ALU.mult)
                v.tensor_tensor(xdt3[:, c, cols].rearrange("p (h d) -> p h d", h=HPG), src, bcast(dt[:, c, hs], HD), ALU.mult)\
                    .then_inc(xdt_ready, 1)
                dve.wait_ge(xdt_ready, q + 1)
                if c == 0:
                    if q >= 1:
                        dve.wait_ge(state_done, q)
                    v.tensor_tensor(xdec.rearrange("p (h d) -> p h d", h=HPG),
                                    xdt3[:, c, cols].rearrange("p (h d) -> p h d", h=HPG), bcast(dec[:, hs], HD), ALU.mult)
                dve.wait_ge(cb_done, q + 1)
                if c == 0:
                    v.tensor_copy(cbm[:, 1, :], bank[4][:, 256:384]).then_inc(b_tok_ready, 1)
                v.tensor_tensor(cbm[:, 0, :], bank[4][:, 0:P], tri[:, :], ALU.mult).then_inc(cb_ready, 1)
                dve.wait_ge(cb_ready, q + 1)
                dve.wait_ge(decay_ready, q + 1)
                v.tensor_tensor(decay.rearrange("p (h l) -> p h l", h=HPG), decay.rearrange("p (h l) -> p h l", h=HPG),
                                cbm[:, 0, :].unsqueeze(1).to_broadcast([P, HPG, P]), ALU.mult).then_inc(wts_ready, 1)
                if q < 7:
                    dve.wait_ge(seg_done, q + 1)
                    make_seg_in(q + 1)
                dve.wait_ge(y_diag_done, q + 1)
                ins = v.tensor_tensor(y[:, c, cols], y[:, c, cols], bank[6][:, :], ALU.add)
                if c == 1:
                    step(ins)
                    dve.wait_ge(y_off_done, g + 1)
                    step(v.tensor_tensor(y_off.rearrange("p (h d) -> p h d", h=HPG),
                                         bank[7][:, :].rearrange("p (h d) -> p h d", h=HPG),
                                         bcast(eacs[:, c, hs], HD), ALU.mult))
                    ins = v.tensor_tensor(y[:, c, cols], y[:, c, cols], y_off, ALU.add)
                ins.then_inc(y_ready, 1)
            dve.wait_ge(y_ready, 8)

            def norm_y(i, a, b):
                dve.wait_ge(y_rms_ready, i + 1)
                step(v.reciprocal(st[:, 32 + a:32 + b], st[:, 32 + a:32 + b]))
                for n in range(a, b):
                    g, t = n // 2, n % 2
                    v.tensor_scalar(y[:, t, g * 512:(g + 1) * 512], y[:, t, g * 512:(g + 1) * 512], st[:, 32 + n:33 + n],
                                    None, ALU.mult).then_inc(y_normed, 1)

            for n in range(8):
                g, t = n // 2, n % 2
                cols = slice(g * 512, (g + 1) * 512)
                u = ("z", n)
                dve.wait_ge(z_tanh_ready, n + 1)
                ins = v.scalar_tensor_tensor(out=th[:, n % 2, :], in0=th[:, n % 2, :], scalar=1.0, in1=acc(u)[:, :],
                                             op0=ALU.add, op1=ALU.mult)
                took(ins, u)
                dve.wait_ge(unit_taken[unit_no[u] % 2], unit_no[u] // 2 + 1)
                v.scalar_tensor_tensor(out=y[:, t, cols], in0=th[:, n % 2, :], scalar=0.5, in1=y[:, t, cols],
                                       op0=ALU.mult, op1=ALU.mult).then_inc(y_gated, 1)
                if n == 4:
                    dve.wait_ge(attT_hi_ready, 1)
                    v.tensor_tensor(attT_lo[:, :, :], attT[:, :, :], attT_hi[:, :, :].bitcast(F32), ALU.subtract)\
                        .then_inc(attT_lo_ready, 1)
                if n == 6:
                    norm_y(0, 0, 6)
            norm_y(1, 6, 8)

            dve.wait_ge(gate_ready, 16)
            def y_lo(j):
                dve.wait_ge(yT_hi_ready, 2 * j + 2)
                for m in (2 * j, 2 * j + 1):
                    c = (m % 2) * 256
                    v.scalar_tensor_tensor(out=yT_lo[:, m, :], in0=bank[2 + j % 2][:, c:c + S], scalar=g_ssm(m),
                                           in1=yT_hi[:, m, :].bitcast(F32), op0=ALU.mult, op1=ALU.subtract)\
                        .then_inc(yT_ready, 1)

            for m in range(8):
                u = ("att", m)
                wait_unit(dve, u)
                took(v.tensor_tensor(gT[:, 8 + m, :], acc(u)[:, 0:S], gT[:, 8 + m, :], ALU.mult), u)
                if m >= 1:
                    y_lo(m - 1)
            y_lo(7)

            def mix_lo(m):
                dve.wait_ge(mix_hi_ready, m + 1)
                v.tensor_tensor(hT_lo[:, m, :], gT[:, 8 + m, :], hT_hi[:, m, :].bitcast(F32), ALU.subtract).then_inc(mix_ready, 1)

            for m in range(8):
                u = ("ssm", m)
                wait_unit(dve, u)
                took(v.tensor_tensor(th[:, m % 2, 0:S], acc(u)[:, 0:S], gT[:, m, :], ALU.mult), u)
                dve.wait_ge(unit_taken[unit_no[u] % 2], unit_no[u] // 2 + 1)
                v.tensor_tensor(gT[:, 8 + m, :], th[:, m % 2, 0:S], gT[:, 8 + m, :], ALU.add).then_inc(mix_sum_ready, 1)
                if m >= 1:
                    mix_lo(m - 1)
            mix_lo(7)
            dve.wait_ge(x_again_landed, 32)
            def x2T_half(half):
                dve.wait_ge(x2_turned, 2 * half + 2)
                for k in (4 * half + 2, 4 * half + 3):
                    c = (k % 2) * 256
                    v.tensor_scalar(x2T[:, k, :], bank[3][:, c:c + S], g_ffn_k(k), None, ALU.mult).then_inc(x2T_ready_v, 1)

            for n in range(4):
                half, t = n // 2, n % 2
                u = ("out", n)
                wait_unit(dve, u)
                cols = slice(half * 512, (half + 1) * 512)
                v.tensor_tensor(x2[:, t, cols], acc(u)[:, :], x_again[:, t, cols], ALU.add).then_inc(x2_ready, 1)
                dve.wait_ge(x2_ready, n + 1)
                if half == 0:
                    dve.sem_inc(unit_taken[unit_no[u] % 2], 1)
                if n == 1:
                    x2T_half(0)
            rev = rt[:, 416:448]
            v.tensor_scalar(rev, iota[:, 0:32], -1.0, 32.0, ALU.mult, ALU.add)
            dve.wait_ge(x2_ss_ready, 4)
            v.tensor_tensor(st[:, 44:46], st[:, 40:42], st[:, 42:44], ALU.add).then_inc(x2_ss_ready, 1)
            x2T_half(1)
            dve.wait_ge(x2_rms_ready, 1)
            v.reciprocal(st[:, 46:48], st[:, 46:48]).then_inc(rs2_ready, 1)
            dve.wait_ge(rs2_ready, 1)

            NE = MG * ME
            T4 = lambda a, n=MG: rt[:, a:a + TT * n].rearrange("p (t n) -> p t n", t=TT)
            small2 = lambda a: rt[:, a:a + TT]
            per = lambda a, n: a.unsqueeze(2).to_broadcast([P, TT, n])
            max_g, max_1, max_2, w2, w1 = small2(448), small2(452), small2(456), small2(460), small2(462)
            lg, ge, pen, scr = T4(0, MG + NE), T4(72), T4(80), T4(96, NE)
            oh1, oh2, both, gate = T4(160, NE), T4(224, NE), T4(288, NE), T4(352, NE)
            gl, el = lg[:, :, 0:MG], lg[:, :, MG:]

            def first_largest(dst, vals, n, mx, best):
                step(v.tensor_reduce(mx, vals, AX.X, ALU.max))
                for t in range(TT):
                    ins = v.scalar_tensor_tensor(out=dst[:, t, :], in0=vals[:, t, :], scalar=mx[:, t:t + 1], in1=rev[:, 32 - n:],
                                                 op0=ALU.is_equal, op1=ALU.mult)
                step(ins)
                step(v.tensor_reduce(best, dst, AX.X, ALU.max))

            dve.wait_ge(route_done, 1)
            for t in range(TT):
                ins = v.scalar_tensor_tensor(out=lg[:, t, :], in0=bank[6 + t][:, 0:MG + NE], scalar=st[:, 46 + t:47 + t],
                                             in1=b_route[:, :], op0=ALU.mult, op1=ALU.add)
            step(ins)
            first_largest(scr[:, :, 0:MG], gl, MG, max_g, small2(450))
            v.tensor_tensor(ge, gl, per(max_g, MG), ALU.subtract)
            for t in range(TT):
                ins = v.tensor_scalar(pen[:, t, :], scr[:, t, 0:MG], rt[:, 450 + t:451 + t], LEAST, ALU.is_lt, ALU.mult)
            step(ins)
            for t in range(TT):
                ins = v.tensor_tensor(el[:, t, :].rearrange("p (g e) -> p g e", g=MG), el[:, t, :].rearrange("p (g e) -> p g e", g=MG),
                                      pen[:, t, :].unsqueeze(2).to_broadcast([P, MG, ME]), ALU.add)
            step(ins)
            first_largest(scr, el, NE, max_1, small2(454))
            step(v.tensor_tensor(oh1, scr, per(small2(454), NE), ALU.is_equal))
            step(v.scalar_tensor_tensor(out=el, in0=oh1, scalar=LEAST, in1=el, op0=ALU.mult, op1=ALU.add))
            first_largest(scr, el, NE, max_2, small2(458))
            step(v.tensor_tensor(oh2, scr, per(small2(458), NE), ALU.is_equal))
            v.tensor_tensor(both, oh1, oh2, ALU.add).then_inc(onehot_ready, 1)
            v.tensor_tensor(w2, max_2, max_1, ALU.subtract).then_inc(route_in, 1)
            v.tensor_scalar(iota1[:, :], iota[:, :], 1.0, None, ALU.add)
            step(v.tensor_scalar(iota1x.rearrange("p t e s -> p (t e) s"),
                                 iota[:, 0:PLACES].unsqueeze(1).to_broadcast([P, TT * EB, PLACES]), 1.0, None, ALU.add))
            dve.wait_ge(onehot_ready, 1)
            dve.wait_ge(rank_done, 1)
            step(v.scalar_tensor_tensor(out=rank1, in0=bank[6][:, 0:2 * NE].rearrange("p (t e) -> p t e", t=TT),
                                        scalar=1.0, in1=both, op0=ALU.add, op1=ALU.mult))

            def four(a):
                return a.rearrange("p t (e s) -> p t e s", e=EB)

            def grow(a, b):
                return a[:, :, bass.ds(b * EB, EB)].unsqueeze(3).to_broadcast([P, TT, EB, PLACES])

            def make_perm(b):
                v.tensor_tensor(four(perm), iota1x, grow(rank1, b), ALU.is_equal).then_inc(batch.perm_ready, 1)

            def make_pgate(b):
                dve.wait_ge(batch.perm_ready, b * 2 + 1)
                v.tensor_tensor(four(pgate), four(perm), grow(gate, b), ALU.mult).then_inc(batch.perm_ready, 1)

            def take_xgT(q, i):
                dve.wait_ge(q.gathered, i * 2 + 2)
                for k in range(4, KD):
                    ins = v.tensor_scalar(xgT[:, k, :], bank[2][:, (k - 4) * P:(k - 3) * P], g_ffn[:, k:k + 1], None, ALU.mult)
                ins.then_inc(q.xgT_ready_v, 1)

            def square_sum(t):
                dve.wait_ge(batch.added, 4 * BATCHES - 1 + t)
                if t:
                    dve.wait_ge(fin_ss_ready, t)
                v.tensor_tensor_reduce(out=xg_flat, in0=x2[:, t, :], in1=x2[:, t, :], scale=1.0, scalar=0.0,
                                       op0=ALU.mult, op1=ALU.add, accum_out=st[:, 48 + t:49 + t]).then_inc(fin_ss_ready, 1)

            def finish_pass(q, i, last=False):
                dve.wait_ge(q.silu_ready, i + 1)
                v.tensor_tensor(hid, bank[0][:, FF:2 * FF], sil, ALU.mult).then_inc(q.hid_ready, 1)
                for n in range(4):
                    half, t = n // 2, n % 2
                    cols = slice(half * 512, (half + 1) * 512)
                    dve.wait_ge(q.scattered, i * 4 + (n + 1))
                    v.tensor_tensor(x2[:, t, cols], x2[:, t, cols], bank[3 + t][:, :], ALU.add).then_inc(q.added, 1)
                    if last and n == 2:
                        square_sum(0)

            def make_next(b):
                dve.wait_ge(batch.places_done, b)
                make_perm(b)
                make_pgate(b)

            def pick(i):
                ex = dve.value_load(entry_i[0:1, bass.ds(i, 1)], min_val=0, max_val=NE - 1)
                own = over_now[:, 0:4].rearrange("p (a t) -> p a t", a=2)
                v.tensor_copy(own[:, 0, :].unsqueeze(2), rank1[:, :, bass.ds(ex, 1)])
                v.tensor_copy(own[:, 1, :].unsqueeze(2), gate[:, :, bass.ds(ex, 1)])
                v.tensor_copy(over_now[:, 4:5], entry[:, 0, bass.ds(i, 1)]).then_inc(over_picked, 1)
                dve.wait_ge(over_picked, i * 2 + 1)
                v.tensor_scalar(own[:, 0, :], own[:, 0, :], over_now[:, 4:5], None, ALU.subtract).then_inc(over_picked, 1)
                dve.wait_ge(over_picked, i * 2 + 2)
                for t in range(TT):
                    ins = v.tensor_scalar(perm[:, t, :], iota1[:, :], over_now[:, t:t + 1], None, ALU.is_equal)
                ins.then_inc(further.perm_ready, 1)
                dve.wait_ge(further.perm_ready, i * 2 + 1)
                for t in range(TT):
                    ins = v.tensor_scalar(pgate[:, t, :], perm[:, t, :], over_now[:, 2 + t:3 + t], None, ALU.mult)
                ins.then_inc(further.perm_ready, 1)

            make_perm(0)
            v.tensor_scalar(flags[:, 0:NE], bank[6][:, 2 * NE:3 * NE], float(PLACES), None, ALU.is_gt)
            step(v.tensor_scalar(flags[:, NE:2 * NE], bank[6][:, 2 * NE:3 * NE], float(PLACES + P), None, ALU.is_gt))
            n_over, first = over_now[:, 5:6], over_now[:, 6:7]
            v.tensor_reduce(n_over, flags, AX.X, ALU.add)
            step(v.tensor_tensor(over_at[:, 0:NE], flags[:, 0:NE], rev, ALU.mult))
            step(v.tensor_reduce(first, over_at[:, 0:NE], AX.X, ALU.max))
            v.tensor_scalar(first, first, -1.0, float(NE), ALU.mult, ALU.add)
            v.tensor_copy(n_over_i[:, 0:1], n_over)
            step(v.tensor_scalar(n_over_i[:, 1:2], n_over, 1.0, 0.0, ALU.subtract, ALU.max))
            v.tensor_copy(n_over_i[:, 2:3], first).then_inc(first_over_ready, 1)
            dve.wait_ge(route_exp, 1)
            step(v.tensor_reduce(w1, ge, AX.X, ALU.add))
            step(v.scalar_tensor_tensor(out=w1, in0=w2, scalar=1.0, in1=w1, op0=ALU.add, op1=ALU.mult))
            step(v.reciprocal(w1, w1))
            step(v.tensor_tensor(w2, w1, w2, ALU.mult))
            v.tensor_tensor(oh1, oh1, per(w1, NE), ALU.mult)
            step(v.tensor_tensor(oh2, oh2, per(w2, NE), ALU.mult))
            step(v.tensor_tensor(gate, oh1, oh2, ALU.add))
            make_pgate(0)
            take_xgT(batch, 0)
            step(v.tensor_copy(before[:, 0, :], flags))
            for n in range(6):
                a, b, d = n % 2, 1 - n % 2, 1 << n
                v.tensor_copy(before[:, b, 0:d], before[:, a, 0:d])
                step(v.tensor_tensor(before[:, b, d:64], before[:, a, d:64], before[:, a, 0:64 - d], ALU.add))
            step(v.tensor_tensor(over_at, before[:, 0, :], flags, ALU.mult))
            hit = th[:, :, :].rearrange("p a b -> p (a b)").rearrange("p (j i) -> p j i", j=MAX_OVER)
            step(v.tensor_tensor(hit, over_at.unsqueeze(1).to_broadcast([P, MAX_OVER, 64]),
                                 iota1[:, 0:MAX_OVER].unsqueeze(2).to_broadcast([P, MAX_OVER, 64]), ALU.is_equal))
            step(v.tensor_tensor(hit, hit, iota[:, 0:64].unsqueeze(1).to_broadcast([P, MAX_OVER, 64]), ALU.mult))
            step(v.tensor_reduce(entry[:, 1, 0:MAX_OVER], hit, AX.X, ALU.add))
            step(v.tensor_scalar(entry[:, 0, 0:MAX_OVER], entry[:, 1, 0:MAX_OVER], float(NE), float(P), ALU.is_ge, ALU.mult))
            step(v.scalar_tensor_tensor(out=entry[:, 1, 0:MAX_OVER], in0=entry[:, 0, 0:MAX_OVER], scalar=-float(NE) / P,
                                        in1=entry[:, 1, 0:MAX_OVER], op0=ALU.mult, op1=ALU.add))
            step(v.memset(entry[:, :, MAX_OVER:], 0.0))
            step(v.tensor_copy(entry_i[:, :], entry[:, 1, :]))
            v.tensor_scalar(entry[:, 0, 0:MAX_OVER], entry[:, 0, 0:MAX_OVER], float(PLACES), None, ALU.add).then_inc(route_ready, 1)
            dve.wait_ge(route_ready, 1)
            make_next(1)
            finish_pass(batch, 0)
            take_xgT(batch, 1)
            make_next(2)
            finish_pass(batch, 1)
            take_xgT(batch, 2)
            over = dve.value_load(n_over_i[0:1, 0:1], min_val=0, max_val=MAX_OVER)
            dve.wait_ge(batch.places_done, 3)
            with dve.If(over):
                pick(0)
            finish_pass(batch, 2)
            with dve.If(over):
                with dve.Fori(0, over) as i:
                    take_xgT(further, i)
                    dve.wait_ge(further.places_done, i + 1)
                    pick(i + 1)
                    dve.wait_ge(further.perm_ready, i * 2 + 4)
                    finish_pass(further, i)
                    dve.wait_ge(further.added, i * 4 + 4)
                    dve.sem_inc(over_turn, 1)
            make_next(3)
            with dve.Fori(0, BATCHES - 4) as r:
                take_xgT(batch, r + 3)
                make_next(r + 4)
                finish_pass(batch, r + 3)
            take_xgT(batch, BATCHES - 1)
            finish_pass(batch, BATCHES - 1, last=True)

            square_sum(1)
            dve.wait_ge(g_fin_landed, 16)
            dve.wait_ge(fin_rms_ready, 1)
            v.reciprocal(st[:, 50:52], st[:, 50:52]).then_inc(fin_rms_ready, 1)
            dve.wait_ge(fin_rms_ready, 2)
            v.scalar_tensor_tensor(out=h2[:, 1, :], in0=x2[:, 1, :], scalar=st[:, 51:52], in1=g_fin,
                                   op0=ALU.mult, op1=ALU.mult).then_inc(out_ready_v, 1)


_INS = ['x', 'norm_mix_g', 'w_in', 'conv_w', 'conv_b', 'dt_bias', 'a_log', 'd_skip', 'ssm_norm_g', 'kv_norm_g',
        'w_uk', 'w_uv', 'gate_b', 'w_branch_ssm', 'w_branch_att', 'w_out', 'norm_ffn_g', 'w_group', 'b_group',
        'w_router', 'b_router', 'w_e1', 'w_e3', 'w_e2', 'norm_final_g']


def kernel(**inputs):
    import numpy as _np
    import concourse.bacc as _bacc
    from concourse import mybir as _mybir
    from concourse.bass_utils import run_bass_kernel_spmd as _run

    nc = _bacc.Bacc("TRN2", target_bir_lowering=False, num_devices=1)
    arrays, args = {}, []
    for name in _INS:
        a = _np.ascontiguousarray(inputs[name])
        arrays[f"in_{name}_dram"] = a
        args.append(nc.dram_tensor(f"in_{name}_dram", a.shape, _mybir.dt.from_np(a.dtype), kind="ExternalInput").ap())
    args.append(nc.dram_tensor("out_dram", (1, S, D), F32, kind="ExternalOutput").ap())
    hybrid_block(nc, *args)
    r = _run(nc, [arrays], core_ids=[0])
    return r.results[0]["out_dram"]
```
